# Optimizing a Trainium2 kernel written in Bass

```python
import jax, jax.numpy as jnp
from jax import lax
import numpy as np

D_MODEL = 1024
BATCH = 1
SEQ = 128
DEPTH = 1
DEC_BATCH = 1
DEC_SEQ = 1024
PAST_LEN = 128

GRID_W = 64
ML_HEADS = 4
ML_DK = 128
ML_DV = 128
ML_WIDTH = ML_HEADS * ML_DV
HG_HEADS = 4
HG_DK = 128
HG_DV = 128
HG_WIDTH = HG_HEADS * HG_DV
AT_HEADS = 8
AT_KV_HEADS = 2
AT_GROUP = AT_HEADS // AT_KV_HEADS
AT_HD = 64
AT_WIDTH = AT_HEADS * AT_HD
N_BRANCH = 3
BRANCH_W = ML_WIDTH
FFN_HIDDEN = -(-8 * D_MODEL // (3 * 256)) * 256
CHUNK = 64
Q_BLOCK = 128
ROPE_THETA = 10000.0
EPS = 1e-6
IN_SIZES = (ML_HEADS * ML_DK, ML_HEADS * ML_DK, ML_WIDTH, ML_WIDTH, 2 * 2 * ML_HEADS,
            HG_HEADS * HG_DK, 2 * HG_HEADS * HG_DK, HG_WIDTH, HG_WIDTH,
            AT_HEADS * AT_HD, AT_KV_HEADS * AT_HD, AT_KV_HEADS * AT_HD, N_BRANCH * D_MODEL)
IN_COLS = 2 * ML_HEADS * ML_DK + 2 * ML_WIDTH + 4 * ML_HEADS + 3 * HG_HEADS * HG_DK + 2 * HG_WIDTH + (AT_HEADS + 2 * AT_KV_HEADS) * AT_HD + N_BRANCH * D_MODEL

kernel_name = 'hybrid_mlstm_hgrn2_gqa_diffusion_step'

def _rmsnorm(x, g):
    xf = x.astype(jnp.float32)
    xf = xf * lax.rsqrt(jnp.mean(xf * xf, axis=-1, keepdims=True) + EPS)
    return (xf * g.astype(jnp.float32)).astype(x.dtype)

def _headnorm(y, g):
    B, L = y.shape[:2]
    y = y * lax.rsqrt(jnp.mean(y * y, axis=-1, keepdims=True) + EPS)
    return y.reshape(B, L, -1) * g.astype(jnp.float32)

def _split(a, sizes):
    outs, off = [], 0
    for s in sizes:
        outs.append(a[..., off:off + s])
        off += s
    return outs

def _flip(a):
    return jnp.flip(a, axis=1)

def _to_chunks(a):
    B, L = a.shape[:2]
    a = a.reshape((B, L // CHUNK, CHUNK) + a.shape[2:])
    return jnp.swapaxes(jnp.moveaxis(a, 1, 0), 2, 3)

def _from_chunks(a):
    nc, B, H, C = a.shape[:4]
    a = jnp.moveaxis(jnp.swapaxes(a, 2, 3), 0, 1)
    return a.reshape((B, nc * C, H) + a.shape[4:])

def _mlstm_scan(q, k, v, ig, fg, C0, n0, m0):
    f32 = jnp.float32
    scale = ML_DK ** -0.5
    causal = jnp.tril(jnp.ones((CHUNK, CHUNK), dtype=bool))
    xs = tuple(_to_chunks(a.astype(f32)) for a in (q, k, v, ig, fg))

    def step(carry, inp):
        C, n, m = carry
        qc, kc, vc, ic, fc = inp
        qc = qc * scale
        b = jnp.cumsum(jax.nn.log_sigmoid(fc), axis=-1)
        d = jnp.where(causal, b[..., :, None] - b[..., None, :] + ic[..., None, :], -jnp.inf)
        m_state = b + m[..., None]
        m_t = jnp.maximum(m_state, jnp.max(d, axis=-1))
        w_intra = jnp.exp(d - m_t[..., None])
        w_state = jnp.exp(m_state - m_t)
        s = jnp.einsum('bhtd,bhsd->bhts', qc, kc) * w_intra
        num = jnp.einsum('bhts,bhsv->bhtv', s, vc) + w_state[..., None] * jnp.einsum('bhtd,bhdv->bhtv', qc, C)
        den = jnp.sum(s, axis=-1) + w_state * jnp.einsum('bhtd,bhd->bht', qc, n)
        h = num / jnp.maximum(jnp.abs(den), jnp.exp(-m_t))[..., None]
        b_end = b[..., -1]
        g = b_end[..., None] - b + ic
        m_new = jnp.maximum(b_end + m, jnp.max(g, axis=-1))
        w_k = jnp.exp(g - m_new[..., None])
        decay = jnp.exp(b_end + m - m_new)
        C_new = decay[..., None, None] * C + jnp.einsum('bhs,bhsd,bhsv->bhdv', w_k, kc, vc)
        n_new = decay[..., None] * n + jnp.einsum('bhs,bhsd->bhd', w_k, kc)
        return (C_new, n_new, m_new), h

    (C, n, m), h = lax.scan(step, (C0.astype(f32), n0.astype(f32), m0.astype(f32)), xs)
    return _from_chunks(h), (C, n, m)

def _hgrn_scan(q, k, logf, v, S0):
    f32 = jnp.float32
    causal = jnp.tril(jnp.ones((CHUNK, CHUNK), dtype=bool))[..., None]
    xs = tuple(_to_chunks(a.astype(f32)) for a in (q, k, logf, v))

    def step(S, inp):
        qc, kc, lf, vc = inp
        b = jnp.cumsum(lf, axis=2)
        d = jnp.where(causal, b[:, :, :, None, :] - b[:, :, None, :, :], -jnp.inf)
        a = jnp.einsum('bhtc,bhsc,bhtsc->bhts', qc, kc, jnp.exp(d))
        o = jnp.einsum('bhts,bhsv->bhtv', a, vc) + jnp.einsum('bhtc,bhcv->bhtv', qc * jnp.exp(b), S)
        b_end = b[:, :, -1:, :]
        S_new = jnp.exp(b_end[:, :, 0, :])[..., None] * S + jnp.einsum('bhsc,bhsv->bhcv', kc * jnp.exp(b_end - b), vc)
        return S_new, o

    S, o = lax.scan(step, S0.astype(f32), xs)
    return _from_chunks(o), S

def _axial_rope_tables(L):
    rows = L // GRID_W
    row = jnp.repeat(jnp.arange(rows, dtype=jnp.float32), GRID_W)
    col = jnp.tile(jnp.arange(GRID_W, dtype=jnp.float32), rows)
    n_freq = AT_HD // 4
    inv = ROPE_THETA ** (-jnp.arange(n_freq, dtype=jnp.float32) / n_freq)
    ang = jnp.concatenate([row[:, None] * inv, col[:, None] * inv], axis=-1)
    return jnp.cos(ang), jnp.sin(ang)

def _apply_rope(x, cos, sin):
    xf = x.astype(jnp.float32).reshape(x.shape[:-1] + (AT_HD // 2, 2))
    x1, x2 = xf[..., 0], xf[..., 1]
    c = cos[None, :, None, :]
    s = sin[None, :, None, :]
    out = jnp.stack([x1 * c - x2 * s, x1 * s + x2 * c], axis=-1).reshape(x.shape)
    return out.astype(x.dtype)

def _block_attention(q, k, v):
    B, Lq, H, D = q.shape
    nb = Lq // Q_BLOCK
    qb = jnp.moveaxis(q.reshape(B, nb, Q_BLOCK, AT_KV_HEADS, AT_GROUP, D), 1, 0)
    scale = D ** -0.5

    def one(qblk):
        s = jnp.einsum('bqkgd,bskd->bkgqs', qblk, k).astype(jnp.float32) * scale
        p = jax.nn.softmax(s, axis=-1).astype(v.dtype)
        return jnp.einsum('bkgqs,bskd->bqkgd', p, v)

    o = lax.map(one, qb)
    return jnp.moveaxis(o, 0, 1).reshape(B, Lq, H * D)

def _trunk_layer(x, ada, p, lb, rope, cache):
    f32 = jnp.float32
    B, L, _ = x.shape
    sh1, sc1, g1, sh2, sc2, g2 = jnp.split(ada, 6, axis=-1)
    h = _rmsnorm(x, p['norm1_g']) * (1 + sc1) + sh1
    proj = h @ p['w_in']
    (mq, mk, mv, mo, mg, hq, hf, hi, hg, aq, ak, av, bg) = _split(proj, IN_SIZES)

    mq = mq.reshape(B, L, ML_HEADS, ML_DK)
    mk = mk.reshape(B, L, ML_HEADS, ML_DK)
    mv = mv.reshape(B, L, ML_HEADS, ML_DV)
    gates = mg.reshape(B, L, 2, 2, ML_HEADS).astype(f32) + p['ml_gate_b'].astype(f32)
    if cache is None:
        z = (jnp.zeros((B, ML_HEADS, ML_DK, ML_DV), f32), jnp.zeros((B, ML_HEADS, ML_DK), f32), jnp.zeros((B, ML_HEADS), f32))
        init_f, init_b = z, z
    else:
        init_f = (cache['ml_C'][:, 0], cache['ml_n'][:, 0], cache['ml_m'][:, 0])
        init_b = (cache['ml_C'][:, 1], cache['ml_n'][:, 1], cache['ml_m'][:, 1])
    yf, (Cf, nf, mf) = _mlstm_scan(mq, mk, mv, gates[:, :, 0, 0], gates[:, :, 0, 1], *init_f)
    yb, (Cb, nb, mb) = _mlstm_scan(_flip(mq), _flip(mk), _flip(mv), _flip(gates[:, :, 1, 0]), _flip(gates[:, :, 1, 1]), *init_b)
    y_ml = (_headnorm(yf + _flip(yb), p['ml_norm_g']) * jax.nn.sigmoid(mo.astype(f32))).astype(x.dtype)

    hq = hq.reshape(B, L, HG_HEADS, HG_DK)
    hi = hi.reshape(B, L, HG_HEADS, HG_DV)
    hf = hf.reshape(B, L, 2, HG_HEADS, HG_DK).astype(f32)
    lbh = lb.reshape(2, HG_HEADS, HG_DK).astype(f32)
    logf = jnp.logaddexp(jnp.log(lbh), jnp.log1p(-lbh) + jax.nn.log_sigmoid(hf))
    kk = (1 - lbh) * jax.nn.sigmoid(-hf)
    if cache is None:
        zs = jnp.zeros((B, HG_HEADS, HG_DK, HG_DV), f32)
        s_f, s_b = zs, zs
    else:
        s_f, s_b = cache['hg_S'][:, 0], cache['hg_S'][:, 1]
    of, Sf = _hgrn_scan(hq, kk[:, :, 0], logf[:, :, 0], hi, s_f)
    ob, Sb = _hgrn_scan(_flip(hq), _flip(kk[:, :, 1]), _flip(logf[:, :, 1]), _flip(hi), s_b)
    y_hg = (_headnorm(of + _flip(ob), p['hg_norm_g']) * jax.nn.silu(hg.astype(f32))).astype(x.dtype)

    aq = _rmsnorm(aq.reshape(B, L, AT_HEADS, AT_HD), p['q_norm_g'])
    ak = _rmsnorm(ak.reshape(B, L, AT_KV_HEADS, AT_HD), p['k_norm_g'])
    av = av.reshape(B, L, AT_KV_HEADS, AT_HD)
    if cache is None:
        y_at = _block_attention(aq, ak, av)
    else:
        cos, sin = rope
        keys = jnp.concatenate([_apply_rope(ak, cos, sin), cache['k'].astype(ak.dtype)], axis=1)
        vals = jnp.concatenate([av, cache['v'].astype(av.dtype)], axis=1)
        y_at = _block_attention(_apply_rope(aq, cos, sin), keys, vals)

    branches = jnp.stack([y_ml, y_hg, y_at], axis=2)
    proj_b = jnp.einsum('blnw,nwd->blnd', branches, p['w_branch'])
    gates_b = jax.nn.sigmoid(bg.reshape(B, L, N_BRANCH, D_MODEL))
    merged = jnp.sum(gates_b * proj_b, axis=2)
    x = x + g1 * (merged @ p['w_out'])

    h2 = _rmsnorm(x, p['norm2_g']) * (1 + sc2) + sh2
    gu = h2 @ p['w_ffn_in']
    gt, up = gu[..., :FFN_HIDDEN], gu[..., FFN_HIDDEN:]
    x = x + g2 * ((jax.nn.silu(gt) * up) @ p['w_ffn_out'])

    ctx = None
    if cache is None:
        ctx = dict(k=ak, v=av, ml_C=jnp.stack([Cf, Cb], axis=1), ml_n=jnp.stack([nf, nb], axis=1),
                   ml_m=jnp.stack([mf, mb], axis=1), hg_S=jnp.stack([Sf, Sb], axis=1))
    return x, ctx

def setup_inputs(seed: int = 0) -> dict:
    key = jax.random.key(seed)
    ks = jax.random.split(key, 32)
    f32 = jnp.float32
    D = D_MODEL

    def nrm(k, shape, scale):
        return jax.random.normal(k, shape, f32) * scale

    ig_b = nrm(ks[14], (DEPTH, 2, ML_HEADS), 0.1)
    fg_b = jnp.linspace(3.0, 6.0, ML_HEADS, dtype=f32)[None, None, :] + nrm(ks[15], (DEPTH, 2, ML_HEADS), 0.1)
    return {
        'x_prompt': nrm(ks[0], (BATCH, SEQ, D), 1.0),
        'x_sample': nrm(ks[1], (DEC_BATCH, DEC_SEQ, D), 1.0),
        'c': nrm(ks[2], (DEC_BATCH, D), 1.0),
        'cache_k': nrm(ks[3], (DEC_BATCH, DEPTH, PAST_LEN, AT_KV_HEADS, AT_HD), 1.0),
        'cache_v': nrm(ks[4], (DEC_BATCH, DEPTH, PAST_LEN, AT_KV_HEADS, AT_HD), 0.5),
        'state_ml_C': nrm(ks[5], (DEC_BATCH, DEPTH, 2, ML_HEADS, ML_DK, ML_DV), 0.1),
        'state_ml_n': nrm(ks[6], (DEC_BATCH, DEPTH, 2, ML_HEADS, ML_DK), 1.0),
        'state_ml_m': nrm(ks[7], (DEC_BATCH, DEPTH, 2, ML_HEADS), 1.0),
        'state_hg_S': nrm(ks[8], (DEC_BATCH, DEPTH, 2, HG_HEADS, HG_DK, HG_DV), 0.5),
        'c_ctx': nrm(ks[9], (D,), 1.0),
        'w_ada': nrm(ks[10], (DEPTH, D, 6 * D), 0.5 * D ** -0.5),
        'b_ada': nrm(ks[11], (DEPTH, 6 * D), 0.02),
        'norm1_g': 1.0 + nrm(ks[12], (DEPTH, D), 0.05),
        'norm2_g': 1.0 + nrm(ks[13], (DEPTH, D), 0.05),
        'w_in': nrm(ks[16], (DEPTH, D, IN_COLS), D ** -0.5),
        'ml_gate_b': jnp.stack([ig_b, fg_b], axis=2),
        'ml_norm_g': 1.0 + nrm(ks[17], (DEPTH, ML_WIDTH), 0.05),
        'hg_lb_logits': nrm(ks[18], (DEPTH, 2, HG_HEADS * HG_DK), 0.5),
        'hg_norm_g': 1.0 + nrm(ks[19], (DEPTH, HG_WIDTH), 0.05),
        'q_norm_g': 1.0 + nrm(ks[20], (DEPTH, AT_HD), 0.05),
        'k_norm_g': 1.0 + nrm(ks[21], (DEPTH, AT_HD), 0.05),
        'w_branch': nrm(ks[22], (DEPTH, N_BRANCH, BRANCH_W, D), BRANCH_W ** -0.5),
        'w_out': nrm(ks[23], (DEPTH, D, D), D ** -0.5),
        'w_ffn_in': nrm(ks[24], (DEPTH, D, 2 * FFN_HIDDEN), D ** -0.5),
        'w_ffn_out': nrm(ks[25], (DEPTH, FFN_HIDDEN, D), FFN_HIDDEN ** -0.5),
        'final_g': 1.0 + nrm(ks[26], (D,), 0.05),
    }

def reference(x_prompt, x_sample, c, cache_k, cache_v, state_ml_C, state_ml_n, state_ml_m, state_hg_S,
              c_ctx, w_ada, b_ada, norm1_g, norm2_g, w_in, ml_gate_b, ml_norm_g, hg_lb_logits, hg_norm_g,
              q_norm_g, k_norm_g, w_branch, w_out, w_ffn_in, w_ffn_out, final_g):
    lb_all = jnp.cumsum(jax.nn.softmax(hg_lb_logits.astype(jnp.float32), axis=0), axis=0)
    lb_all = lb_all - lb_all[0]
    rope = _axial_rope_tables(x_sample.shape[1])
    xp, xs = x_prompt, x_sample
    nk, nv, nC, nn_, nm, nS = [], [], [], [], [], []
    for l in range(DEPTH):
        p = dict(norm1_g=norm1_g[l], norm2_g=norm2_g[l], w_in=w_in[l], ml_gate_b=ml_gate_b[l],
                 ml_norm_g=ml_norm_g[l], hg_norm_g=hg_norm_g[l], q_norm_g=q_norm_g[l], k_norm_g=k_norm_g[l],
                 w_branch=w_branch[l], w_out=w_out[l], w_ffn_in=w_ffn_in[l], w_ffn_out=w_ffn_out[l])
        ada_ctx = (jax.nn.silu(c_ctx) @ w_ada[l] + b_ada[l])[None, None, :]
        ada_lat = (jax.nn.silu(c) @ w_ada[l] + b_ada[l])[:, None, :]
        xp, ctx = _trunk_layer(xp, ada_ctx, p, lb_all[l], None, None)
        nk.append(ctx['k']); nv.append(ctx['v']); nC.append(ctx['ml_C'])
        nn_.append(ctx['ml_n']); nm.append(ctx['ml_m']); nS.append(ctx['hg_S'])
        cache = dict(k=cache_k[:, l], v=cache_v[:, l], ml_C=state_ml_C[:, l], ml_n=state_ml_n[:, l],
                     ml_m=state_ml_m[:, l], hg_S=state_hg_S[:, l])
        xs, _ = _trunk_layer(xs, ada_lat, p, lb_all[l], rope, cache)
    y_prompt = _rmsnorm(xp, final_g)
    y_sample = _rmsnorm(xs, final_g)
    new_k = jnp.stack(nk, axis=1)
    new_v = jnp.stack(nv, axis=1)
    new_ml_C = jnp.stack(nC, axis=1)
    new_ml_n = jnp.stack(nn_, axis=1)
    new_ml_m = jnp.stack(nm, axis=1)
    new_hg_S = jnp.stack(nS, axis=1)
    return (y_prompt, y_sample, new_k, new_v, new_ml_C, new_ml_n, new_ml_m, new_hg_S)


_drawn_inputs = setup_inputs


def setup_inputs(seed=0):
    import zlib

    import numpy as np

    out = dict(_drawn_inputs(seed))
    spreads = {}
    factors = {'cache_k': 8.0,
     'cache_v': 8.0,
     'state_ml_C': 8.0,
     'state_ml_n': 8.0,
     'state_ml_m': 8.0,
     'state_hg_S': 8.0,
     'norm2_g': 3.642,
     'ml_norm_g': 8.0,
     'hg_norm_g': 8.0,
     'q_norm_g': 8.0}
    for name, (base, spread) in spreads.items():
        noise = np.random.default_rng([zlib.crc32(name.encode()), seed]).standard_normal(out[name].shape)
        drawn = base * np.exp(spread * noise) if base else spread * noise
        out[name] = __import__('jax').numpy.asarray(drawn.astype(out[name].dtype))
    for name, factor in factors.items():
        out[name] = (out[name] * factor).astype(out[name].dtype)
    return out
```

```python
from contextlib import ExitStack

import concourse.bass as bass
import numpy as np
from concourse import mybir

F32 = mybir.dt.float32
F32R = mybir.dt.float32r
I32 = mybir.dt.int32
BF16 = mybir.dt.bfloat16
ALU = mybir.AluOpType
ACT = mybir.ActivationFunctionType
AX = mybir.AxisListType

P = 128
D = 1024
KD = D // P
CTX, LAT = 128, 1024
T = CTX + LAT
NT = T // P
TH = T // 3
HEADS = 4
DK = 128
AH, KV, HD = 8, 2, 64
PAST = 128
GRID_W = 64
ROPE_THETA = 10000.0
FFN = 2816
NH = FFN // P
EPS = 1e-6
HALF = 256
UNIT = KD * HALF
NTB = 5
TLAST = 2 * P + 16
TW = NTB * 512 + TLAST
NFQ, NBG = 10, 12
C_MV, C_MO, C_HI, C_HG, C_AQ, C_AK, C_AV, C_MG = 0, 512, 1024, 1536, 2048, 2560, 2688, 2816
R_MQ, R_MK, R_HQ, R_HF = 0, 4, 8, 12
HL = ((0, 0), (0, 1), (1, 0))


def three_passes(pe, out, lhs, rhs, first, last):
    for n, (a, b) in enumerate(HL):
        mm = pe.matmul(out, lhs[a], rhs[b], start=first and n == 0, stop=last and n == 2)
    return mm


class Core:
    pass


class Phase:

    def __init__(self, nc, tag):
        self.nc, self.tag, self.stack, self.sems = nc, tag, ExitStack(), []

    def __enter__(self):
        return self

    def __exit__(self, *a):
        self.stack.__exit__(*a)
        self.nc.clear_and_free_semaphores(self.sems)
        self.nc.all_engine_barrier()

    def sb(self, name, shape, dt=F32):
        return self.stack.enter_context(self.nc.sbuf_tensor(f"{self.tag}_{name}", shape, dt))

    def sem(self, name):
        handle = self.nc.alloc_semaphore(f"{self.tag}_{name}")
        self.sems.append(handle)
        return handle

    def block(self):
        return self.stack.enter_context(self.nc.Block())


class Chain:

    def __init__(self, eng, sem):
        self.eng, self.sem, self.n = eng, sem, 0
        self.i, self.per, self.base = None, 0, 0

    def __call__(self, ins):
        ins.then_inc(self.sem, 1)
        self.n += 1
        self.eng.wait_ge(self.sem, self.value())
        return self.n

    def value(self):
        return self.base + self.n if self.i is None else self.i * self.per + self.base + self.n

    def loop(self, i, per):
        self.base, self.n, self.i, self.per = self.base + self.n, 0, i, per

    def end(self, times):
        assert self.n == self.per, (self.n, self.per)
        self.base, self.n, self.i = self.base + self.per * times, 0, None


def modulate(nc, g):
    io, ps = g.io, g.ps
    with Phase(nc, "mod") as ph:
        rows = ph.sb("rows", [80, P])
        vcol = ph.sb("vcol", [P, 80])
        sig = ph.sb("sig", [P, 16])
        sc = ph.sb("sc", [P, KD, 2])
        ada = [ph.sb(f"ada{i}", [P, KD, 512]) for i in range(3)]
        mcol = ph.sb("mcol", [P, 32, 2])
        brow = ph.sb("brow", [2, 2048])
        grow = ph.sb("grow", [2, 2048])
        xt = ph.sb("xt", [P, NT, D])
        junk = ph.sb("junk", [P, D])
        ss = ph.sb("ss", [P, NT])
        ms = ph.sb("ms", [P, NT])
        rstd = ph.sb("rstd", [P, NT])
        half = ph.sb("half", [P, NT])
        hf = [ph.sb(f"hf{i}", [P, 512]) for i in range(3)]
        rows_in, brow_in = ph.sem("rows_in"), ph.sem("brow_in")
        x_in = [ph.sem(f"x_in{i}") for i in range(3)]
        ada_in = [ph.sem(f"ada_in{i}") for i in range(3)]
        ada_used, vcol_mm, sig_done = ph.sem("ada_used"), ph.sem("vcol_mm"), ph.sem("sig_done")
        dve, pool, squared, rstd_done = ph.sem("dve"), ph.sem("pool"), ph.sem("squared"), ph.sem("rstd_done")
        col_mm, row_mm, sc_done = ph.sem("col_mm"), ph.sem("row_mm"), ph.sem("sc_done")
        grow_done, grow_out = ph.sem("grow_done"), ph.sem("grow_out")
        vcol_done, mod_done, xs_done = ph.sem("vcol_done"), ph.sem("mod_done"), ph.sem("xs_done")
        turned, h_full, h_split = ph.sem("turned"), ph.sem("h_full"), ph.sem("h_split")
        ident_done = ph.sem("ident_done")
        groups = [(0, 1), (1, 4), (5, 4)]
        VCOL, COLS, ROWS = ps[:, 7, 0:80], ps[:, 7, 128:192], ps[0:2, 6, :]
        nblocks = 12
        block = ph.block()

        @block.sync
        def _(sp):
            at = 0
            for src in (io["b_ada"], io["norm1_g"], io["norm2_g"], io["c_ctx"], io["c"]):
                n = src.shape[0] // P
                sp.dma_start(rows[at:at + n, :], src.rearrange("(r c) -> r c", c=P)).then_inc(rows_in, 16)
                at += n
            for b in range(3):
                sp.dma_start(ada[b][:], io["w_ada"][b]).then_inc(ada_in[b], 16)
            sp.dma_start(xt[:, 0, :], io["x_prompt"]).then_inc(x_in[0], 16)
            for i in (1, 2):
                sp.dma_start(xt[:, 4 * i - 3:4 * i + 1, :],
                             io["x_sample"][512 * i - 512:512 * i, :].rearrange("(t p) d -> p t d", p=P)).then_inc(x_in[i], 16)
            for r in range(2):
                for n, lo in enumerate((2048, 5120)):
                    sp.dma_start(brow[r:r + 1, n * D:n * D + D],
                                 io["b_ada"][lo:lo + D].rearrange("(a n) -> a n", a=1)).then_inc(brow_in, 16)
            for b in range(3, nblocks):
                sp.wait_ge(ada_used, b - 2)
                sp.dma_start(ada[b % 3][:], io["w_ada"][b]).then_inc(ada_in[b % 3], 16)
            sp.wait_ge(grow_done, 4)
            sp.dma_start(g.gate_rows, grow[:]).then_inc(grow_out, 16)
            sp.wait_ge(grow_out, 16)

        @block.gpsimd
        def _(gp):
            gp.memset(g.ident[:], 0.0).then_inc(pool, 1)
            gp.memset(half[:], -0.5).then_inc(pool, 1)
            gp.wait_ge(pool, 1)
            gp.affine_select(out=g.ident[:], in_=g.ident[:], compare_op=ALU.not_equal, fill=1.0,
                             base=0, pattern=[[-1, P]], channel_multiplier=1).then_inc(ident_done, 1)
            for n, (t0, nt) in enumerate(groups):
                gp.wait_ge(squared, t0 + nt)
                gp.tensor_scalar(ms[:, t0:t0 + nt], ss[:, t0:t0 + nt], 1.0 / D, EPS, ALU.mult, ALU.add).then_inc(pool, 1)
                gp.wait_ge(pool, 3 + n)
                gp.tensor_tensor(rstd[:, t0:t0 + nt], ms[:, t0:t0 + nt], half[:, t0:t0 + nt], ALU.pow).then_inc(rstd_done, 1)

        @block.scalar
        def _(act):
            act.wait_ge(vcol_done, 1)
            act.activation(sig[:], vcol[:, 64:80], ACT.Sigmoid).then_inc(sig_done, 1)
            for i in range(NT):
                act.wait_ge(x_in[(i + 3) // 4], 16)
                if i:
                    act.wait_ge(squared, i)
                act.activation(junk[:], xt[:, i, :], ACT.Square, accum_out=ss[:, i:i + 1]).then_inc(squared, 1)
            act.wait_ge(mod_done, 1)
            n = 0
            for gi, (t0, nt) in enumerate(groups):
                who = min(gi, 1)
                for k in range(KD):
                    act.wait_ge(turned, n + 1)
                    if n >= 3:
                        act.wait_ge(h_split, n - 2)
                    act.activation(hf[n % 3][:, 0:nt * P], ps[:, n % 6, 0:nt * P], ACT.Identity,
                                   bias=g.mod[:, 1, k, who:who + 1], scale=g.mod[:, 0, k, who:who + 1]).then_inc(h_full, 1)
                    n += 1

        @block.vector
        def _(v):
            link = Chain(v, dve)
            v.wait_ge(vcol_mm, 1)
            v.tensor_copy(vcol[:], VCOL).then_inc(vcol_done, 1)
            v.wait_ge(vcol_done, 1)
            v.wait_ge(sig_done, 1)
            v.tensor_tensor(sc[:].rearrange("p k v -> p v k"), vcol[:, 64:80].rearrange("p (v k) -> p v k", v=2),
                            sig[:].rearrange("p (v k) -> p v k", v=2), ALU.mult).then_inc(sc_done, 1)

            def columns(n):
                at = 16 * n
                b0 = 24 * n
                bias = vcol[:, b0:b0 + 16].unsqueeze(2).broadcast_to([P, 16, 2])
                v.wait_ge(col_mm, n + 1)
                link(v.tensor_tensor(mcol[:, at:at + 16, :], COLS.rearrange("p (t v) -> p t v", v=2)[:, at:at + 16, :],
                                     bias, ALU.add))
                link(v.tensor_scalar(mcol[:, at + 8:at + 16, :], mcol[:, at + 8:at + 16, :], 1.0, None, ALU.add))
                link(v.tensor_tensor(g.mod[:, 2 * n, :, :], mcol[:, at + 8:at + 16, :],
                                     vcol[:, 48 + 8 * n:56 + 8 * n].unsqueeze(2).broadcast_to([P, 8, 2]), ALU.mult))
                v.tensor_copy(g.mod[:, 2 * n + 1, :, :], mcol[:, at:at + 8, :]).then_inc(mod_done, 1)

            columns(0)
            for gi, (t0, nt) in enumerate(groups):
                v.wait_ge(rstd_done, gi + 1)
                for i in range(t0, t0 + nt):
                    v.tensor_scalar(xt[:, i, :], xt[:, i, :], rstd[:, i:i + 1], None, ALU.mult).then_inc(xs_done, 1)
            n = 0
            for gi, (t0, nt) in enumerate(groups):
                for k in range(KD):
                    v.wait_ge(h_full, n + 1)
                    src, at = hf[n % 3][:, 0:nt * P], slice(t0 * P, (t0 + nt) * P)
                    link(v.tensor_copy(g.h[0][:, k, at], src))
                    v.tensor_tensor(g.h[1][:, k, at], src, g.h[0][:, k, at].bitcast(F32), ALU.subtract).then_inc(h_split, 1)
                    n += 1
            columns(1)
            v.wait_ge(brow_in, 64)
            for n in range(4):
                v.wait_ge(row_mm, n + 1)
                v.tensor_tensor(grow[:, 512 * n:512 * n + 512], ROWS, brow[:, 512 * n:512 * n + 512],
                                ALU.add).then_inc(grow_done, 1)

        @block.tensor
        def _(pe):
            pe.wait_ge(ident_done, 1)
            pe.wait_ge(rows_in, 80)
            pe.transpose(VCOL, rows[:], g.ident[0:80, 0:80]).then_inc(vcol_mm, 1)
            pe.wait_ge(sc_done, 1)

            def ada_columns(b):
                pe.wait_ge(ada_in[b % 3], 16 * (b // 3 + 1))
                for t in range(4):
                    for k in range(KD):
                        mm = pe.matmul(COLS[:, 8 * b + 2 * t:8 * b + 2 * t + 2], ada[b % 3][:, k, t * P:(t + 1) * P],
                                       sc[:, k, :], start=k == 0, stop=k == KD - 1)
                mm.then_inc(ada_used, 1)
                if b in (3, 7):
                    pe.wait_ge(ada_used, b + 1)
                    pe.nop().then_inc(col_mm, 1)

            for b in range(4):
                ada_columns(b)
            n = 0
            for gi, (t0, nt) in enumerate(groups):
                pe.wait_ge(xs_done, t0 + nt)
                for k in range(KD):
                    if n >= 6:
                        pe.wait_ge(h_full, n - 5)
                    for i in range(nt):
                        mm = pe.transpose(ps[:, n % 6, i * P:(i + 1) * P], xt[:, t0 + i, k * P:(k + 1) * P], g.ident[:])
                    mm.then_inc(turned, 1)
                    n += 1
            for b in range(4, 8):
                ada_columns(b)
            pe.wait_ge(h_full, n)
            for b in range(8, nblocks):
                pe.wait_ge(ada_in[b % 3], 16 * (b // 3 + 1))
                if b > 8:
                    pe.wait_ge(grow_done, b - 8)
                for k in range(KD):
                    mm = pe.matmul(ROWS, sc[:, k, :], ada[b % 3][:, k, :], start=k == 0, stop=k == KD - 1)
                mm.then_inc(ada_used, 1)
                pe.wait_ge(ada_used, b + 1)
                pe.nop().then_inc(row_mm, 1)


def project(nc, g):
    io, ps = g.io, g.ps
    with Phase(nc, "prj") as ph:
        raw = [ph.sb(f"raw{i}", [P, KD * TLAST]) for i in range(2)]
        w = [[ph.sb(f"w{n}{i}", [P, KD * 512], F32R) for i in range(2)] for n in ("hi", "lo")]
        tst = [ph.sb(f"tst{i}", [P, 512]) for i in range(6)]
        fst = [ph.sb(f"fst{i}", [P, T]) for i in range(2)]
        raw_in = [ph.sem(f"raw_in{i}") for i in range(2)]
        hi_done = ph.sem("hi_done")
        lo_done = ph.sem("lo_done")
        blk_done = ph.sem("blk_done")
        t_mm, t_ev = ph.sem("t_mm"), ph.sem("t_ev")
        f_mm, f_ev = ph.sem("f_mm"), ph.sem("f_ev")
        t_out = [ph.sem(f"t_out{i}") for i in range(6)]
        f_out = [ph.sem(f"f_out{i}") for i in range(2)]
        TU = 2 * NTB + 1
        TB = NTB + 1
        NF = NFQ + NBG
        block = ph.block()

        def f_slot(n):
            return n % 2

        @block.sync
        def _(sp):
            def load(slot, src, width, u):
                sp.wait_ge(lo_done, u + 1)
                sp.dma_start(raw[slot][:, 0:width], src).then_inc(raw_in[slot], 16)

            with sp.Fori(0, NTB) as b:
                for s in range(2):
                    load(s, io["w_tok"][bass.ds(2 * b + s, 1)].rearrange("a p n -> (a p) n"), UNIT, 2 * b + s)
            load(0, io["w_tok_last"], KD * TLAST, TU - 1)
            with sp.Fori(0, NF // 2) as i:
                for s in range(2):
                    load((TU + s) % 2, io["w_feat"][bass.ds(2 * i + s, 1)].rearrange("a p n -> (a p) n"), UNIT, 2 * i + s + TU)

        def raw_value(u, slot):
            return 8 * u + (16 if slot == 0 else 8)

        @block.vector
        def _(v):
            v.sem_inc(lo_done, 2)

            def lo(slot, u, wslot, at, width):
                v.wait_ge(hi_done, u + 1)
                v.tensor_tensor(w[1][wslot][:, at:at + width], raw[slot][:, 0:width],
                                w[0][wslot][:, at:at + width].bitcast(F32), ALU.subtract).then_inc(lo_done, 1)

            with v.Fori(0, 2) as i:
                for s in range(4):
                    lo(s % 2, 4 * i + s, s // 2, UNIT * (s % 2), UNIT)
            for s in range(2):
                lo(s, 8 + s, 0, UNIT * s, UNIT)
            lo(0, TU - 1, 1, 0, KD * TLAST)
            with v.Fori(0, NF // 2) as i:
                for s in range(2):
                    lo((TU + s) % 2, 2 * i + s + TU, s, 0, UNIT)

        @block.scalar
        def _(act):
            act.sem_inc(t_ev, 6)
            act.sem_inc(f_ev, 2)
            for s in (*t_out, *f_out):
                act.sem_inc(s, 16)

            def hi(slot, u, blk, wslot, at, width):
                act.wait_ge(raw_in[slot], raw_value(u, slot))
                act.wait_ge(blk_done, blk + 1)
                act.activation(w[0][wslot][:, at:at + width], raw[slot][:, 0:width], ACT.Copy).then_inc(hi_done, 1)

            def hi_block(b, slot):
                for s in range(2):
                    hi(s, 2 * b + s, b, slot, UNIT * s, UNIT)

            def hi_feat(f, s):
                hi((TU + s) % 2, f + TU, f + TB, s, 0, UNIT)

            def put_tok(b, width, fn):
                for i in range(NT):
                    n = NT * b + i
                    slot = n % 6
                    act.wait_ge(t_mm, n + 1)
                    act.wait_ge(t_out[slot], 16 * (n // 6) + 16)
                    act.activation(tst[slot][:, 0:width], ps[:, slot, 0:width], fn).then_inc(t_ev, 1)
                    act.wait_ge(t_ev, n + 7)
                    act.dma_start(g.tok_dram[i * P:(i + 1) * P, 512 * b:512 * b + width], tst[slot][:, 0:width]).then_inc(t_out[slot], 16)

            def put_feat(f, s, dst, fn):
                for c in range(2):
                    act.wait_ge(f_mm, 2 * f + c + 1)
                    act.wait_ge(f_out[c], 16 * f + 16)
                    act.activation(fst[c][:].rearrange("p (a n) -> p a n", a=3), ps[:, 3 * c:3 * c + 3, 0:TH], fn).then_inc(f_ev, 1)
                    act.wait_ge(f_ev, 2 * f + c + 3)
                    act.dma_start(dst(c), fst[c][:]).then_inc(f_out[c], 16)

            hi_block(0, 0)
            for b, fn in enumerate((ACT.Copy, ACT.Sigmoid, ACT.Copy, ACT.Silu)):
                hi_block(b + 1, (b + 1) % 2)
                put_tok(b, 512, fn)
            hi(0, TU - 1, TB - 1, 1, 0, KD * TLAST)
            put_tok(4, 512, ACT.Copy)
            hi_feat(0, 0)
            put_tok(5, TLAST, ACT.Copy)
            with act.Fori(0, NFQ // 2) as i:
                for s in range(2):
                    hi_feat(2 * i + s + 1, (s + 1) % 2)
                    put_feat(2 * i + s, s, lambda c: g.feat_dram[bass.ds((2 * i + s) * HALF + c * P, P), :], ACT.Copy)
            with act.Fori(0, NBG // 2 - 1) as i:
                for s in range(2):
                    hi_feat(2 * i + s + 1 + NFQ, (s + 1) % 2)
                    put_feat(2 * i + s + NFQ, s, lambda c: g.bg_dram[bass.ds((2 * i + s) * HALF + c * P, P), :], ACT.Sigmoid)
            hi_feat(NF - 1, 1)
            put_feat(NF - 2, 0, lambda c: g.bg_dram[(NBG - 2) * HALF + c * P:(NBG - 2) * HALF + c * P + P, :], ACT.Sigmoid)
            put_feat(NF - 1, 1, lambda c: g.bg_dram[(NBG - 1) * HALF + c * P:(NBG - 1) * HALF + c * P + P, :], ACT.Sigmoid)
            for s in range(6):
                act.wait_ge(t_out[s], 16 + 16 * 9)
            for s in range(2):
                act.wait_ge(f_out[s], 16 + 16 * NF)

        @block.tensor
        def _(pe):
            pe.sem_inc(blk_done, 2)

            def tok_block(b, s, width, units):
                ws = [w[p][s][:, 0:KD * width].rearrange("p (k n) -> p k n", k=KD) for p in range(2)]
                pe.wait_ge(lo_done, units + 2)
                for i in range(NT):
                    slot = (NT * s + i) % 6
                    pe.wait_ge(t_ev, NT * b + i + 1)
                    for k in range(KD):
                        mm = three_passes(pe, ps[:, slot, 0:width], [h[:, k, i * P:(i + 1) * P] for h in g.h],
                                          [x[:, k, :] for x in ws], k == 0, k == KD - 1)
                    mm.then_inc(t_mm, 1)
                pe.wait_ge(t_mm, NT * b + NT)
                pe.sem_inc(blk_done, 1)

            with pe.Fori(0, 2) as i:
                for s in range(2):
                    tok_block(2 * i + s, s, 512, 4 * i + 2 * s + 2)
            tok_block(4, 0, 512, 10)
            tok_block(5, 1, TLAST, TU)
            pe.wait_ge(t_ev, 6 + NT * TB)
            with pe.Fori(0, NF // 2) as i:
                for s in range(2):
                    f = 2 * i + s
                    ws = [w[p][s][:, 0:UNIT].rearrange("p (k n) -> p k n", k=KD) for p in range(2)]
                    pe.wait_ge(lo_done, f + TU + 3)
                    for c in range(2):
                        pe.wait_ge(f_ev, 2 * f + c + 1)
                        for t in range(3):
                            for k in range(KD):
                                mm = three_passes(pe, ps[:, 3 * c + t, 0:TH], [x[:, k, c * P:(c + 1) * P] for x in ws],
                                                  [h[:, k, t * TH:(t + 1) * TH] for h in g.h], k == 0, k == KD - 1)
                        mm.then_inc(f_mm, 1)
                    pe.wait_ge(f_mm, 2 * f + 2)
                    pe.sem_inc(blk_done, 1)


def gate_rows(nc, g):
    io, ps = g.io, g.ps
    with Phase(nc, "gat") as ph:
        mg = ph.sb("mg", [P, NT, 16])
        bias = ph.sb("bias", [HEADS, 4])
        m0 = ph.sb("m0", [HEADS, 2])
        gi = ph.sb("gi", [HEADS, 2, T])
        gf = ph.sb("gf", [HEADS, 2, T])
        ab = ph.sb("ab", [HEADS, 2, T])
        mn = ph.sb("mn", [HEADS, 2, T])
        cum = ph.sb("cum", [HEADS, 2, T])
        m = ph.sb("m", [HEADS, 2, T])
        keep = ph.sb("keep", [HEADS, 2, T])
        mp = ph.sb("mp", [HEADS, 2, NT])
        ue = ph.sb("ue", [HEADS, 2, NT])
        rows = ph.sb("rows", [HEADS, 10, T])
        dec = ph.sb("dec", [HEADS, 2, NT])
        mlast = ph.sb("mlast", [HEADS, 2])
        gin, turned, taken, dve, lns = ph.sem("gin"), ph.sem("turned"), ph.sem("taken"), ph.sem("dve"), ph.sem("lns")
        absd, rows_done, gout, kept = ph.sem("absd"), ph.sem("rows_done"), ph.sem("gout"), ph.sem("kept")
        block = ph.block()

        @block.sync
        def _(sp):
            with nc.allow_non_contiguous_dma(reason="a few small columns"):
                sp.dma_start(mg[:], g.tok_dram[:, C_MG:C_MG + 16].rearrange("(t p) c -> p t c", p=P)).then_inc(gin, 16)
                sp.dma_start(bias[:], io["ml_gate_b"]).then_inc(gin, 16)
                sp.dma_start(m0[:], io["ml_m0"]).then_inc(gin, 16)
                sp.wait_ge(rows_done, 1)
                sp.dma_start(g.gate_dram, rows[:]).then_inc(gout, 16)
                sp.dma_start(g.decay_dram, dec[:].rearrange("h d n -> h (d n)")).then_inc(gout, 16)
                sp.dma_start(g.outs["ml_m"], mlast[:]).then_inc(gout, 16)
            sp.wait_ge(gout, 48)

        @block.gpsimd
        def _(gp):
            gp.memset(keep[:], 1.0).then_inc(kept, 1)
            gp.wait_ge(kept, 1)
            gp.memset(keep[:, 0, 0:T:P], 0.0).then_inc(kept, 1)
            gp.memset(keep[:, 1, P - 1:T:P], 0.0).then_inc(kept, 1)

        @block.tensor
        def _(pe):
            pe.wait_ge(gin, 48)
            for q in range(4):
                if q >= 2:
                    pe.wait_ge(taken, q - 1)
                for t in range(NT):
                    mm = pe.transpose(ps[0:HEADS, 3 * (q % 2) + t // 3, t % 3 * P:t % 3 * P + P],
                                      mg[:, t, 4 * q:4 * q + 4], g.ident[:])
                mm.then_inc(turned, 1)

        @block.scalar
        def _(act):
            act.wait_ge(absd, 1)
            act.activation(ab[:], ab[:], ACT.Exp, scale=-1.0).then_inc(lns, 1)
            act.wait_ge(lns, 1)
            act.activation(ab[:], ab[:], ACT.Ln, bias=1.0).then_inc(lns, 1)

        @block.vector
        def _(v):
            link = Chain(v, dve)
            for q in range(4):
                v.wait_ge(turned, q + 1)
                dst = (gi, gf)[q % 2][:, q // 2, :].rearrange("h (a n) -> h a n", a=3)
                v.tensor_scalar(dst, ps[0:HEADS, 3 * (q % 2):3 * (q % 2) + 3, 0:TH], bias[:, q:q + 1], None,
                                ALU.add).then_inc(taken, 1)
            v.wait_ge(taken, 4)
            v.scalar_tensor_tensor(out=ab[:], in0=gf[:], scalar=-1.0, in1=gf[:], op0=ALU.mult, op1=ALU.max).then_inc(absd, 1)
            link(v.tensor_scalar(mn[:], gf[:], 0.0, None, ALU.min))
            v.wait_ge(lns, 2)
            link(v.tensor_tensor(gf[:], mn[:], ab[:], ALU.subtract))
            v.wait_ge(kept, 3)
            for d in range(2):
                def run(x, lo, hi):
                    y = x[:, d, lo:hi]
                    return y if d == 0 else y[:, ::-1]

                link(v.tensor_tensor_scan(run(cum, 0, T), run(keep, 0, T), run(gf, 0, T), 0.0, ALU.mult, ALU.add))
                link(v.tensor_tensor_scan(run(m, 0, CTX), run(gf, 0, CTX), run(gi, 0, CTX), 0.0, ALU.add, ALU.max))
                link(v.tensor_tensor_scan(run(m, CTX, T), run(gf, CTX, T), run(gi, CTX, T), m0[:, d:d + 1], ALU.add, ALU.max))
            link(v.memset(mp[:, :, 0:1], 0.0))
            link(v.tensor_copy(mp[:, 0, 1:2], m0[:, 0:1]))
            link(v.tensor_copy(mp[:, 1, NT - 1:NT], m0[:, 1:2]))
            link(v.tensor_copy(mp[:, 0, 2:NT], m[:, 0, 2 * P - 1:T - 1:P]))
            link(v.tensor_copy(mp[:, 1, 1:NT - 1], m[:, 1, 2 * P:T:P]))
            a, u, ws, wk, nm = (rows[:, 2 * n:2 * n + 2, :] for n in range(5))
            link(v.tensor_tensor(u, cum[:], m[:], ALU.subtract))
            link(v.tensor_tensor(a, gi[:], cum[:], ALU.subtract))
            link(v.tensor_copy(ue[:, 0, :], u[:, 0, P - 1:T:P]))
            link(v.tensor_copy(ue[:, 1, :], u[:, 1, 0:T:P]))
            for d in range(2):
                def tiles(x):
                    return x[:, d, :].rearrange("h (n p) -> h n p", p=P)

                def wide(x):
                    return x[:, d, :].unsqueeze(2).broadcast_to([HEADS, NT, P])

                link(v.tensor_tensor(tiles(ws), tiles(u), wide(mp), ALU.add))
                link(v.tensor_tensor(tiles(wk), tiles(a), wide(ue), ALU.add))
            link(v.tensor_scalar(nm, m[:], -1.0, None, ALU.mult))
            link(v.tensor_tensor(dec[:], mp[:], ue[:], ALU.add))
            link(v.tensor_copy(mlast[:, 0:1], m[:, 0, CTX - 1:CTX]))
            v.tensor_copy(mlast[:, 1:2], m[:, 1, 0:1]).then_inc(rows_done, 1)


def mlstm(nc, g):
    io, ps = g.io, g.ps
    V1 = DK + 1
    with Phase(nc, "mls") as ph:
        two = lambda name, shape: [ph.sb(f"{name}{s}", shape) for s in range(2)]
        q, k = two("q", [P, T]), two("k", [P, T])
        va = two("va", [P, NT, V1])
        mo = two("mo", [P, NT, P])
        a2, b2 = two("a2", [2, 2, T]), two("b2", [2, 2, T])
        r4 = two("r4", [4, T])
        wsr = two("wsr", [1, 2, T])
        dec = two("dec", [1, 2 * NT])
        s0 = two("s0", [P, 2, V1])
        gn = two("gn", [P, 1])
        qs = ph.sb("qs", [P, T])
        qw = ph.sb("qw", [P, 2, T])
        wb = ph.sb("wb", [P, 2, TH])
        wx = ph.sb("wx", [P, 2, TH])
        pw = ph.sb("pw", [P, 2, T])
        kw = ph.sb("kw", [P, 2, T])
        cols = ph.sb("cols", [P, NT, 4])
        decb = ph.sb("decb", [P, 2 * NT])
        st = ph.sb("st", [P, 2, NT, V1])
        den = ph.sb("den", [P, 2, NT])
        y = ph.sb("y", [P, NT, P])
        y2 = ph.sb("y2", [P, NT, P])
        junk = ph.sb("junk", [P, P])
        ss, ms, rstd, half = (ph.sb(n, [P, NT]) for n in ("ss", "ms", "rstd", "half"))
        yt = ph.sb("yt", [P, T])
        one = ph.sb("one", [1, P])
        neg = ph.sb("neg", [P, 2, TH], BF16)
        idb = ph.sb("idb", [P, P], BF16)
        NLOAD = 12
        loaded = [ph.sem(f"loaded{s}") for s in range(2)]
        free = ph.sem("free")
        sem = {n: ph.sem(n) for n in ("const", "qs", "misc", "cols", "wsb", "wsx", "qw", "dmm", "dx", "smm", "pw",
                                      "kt", "kw", "cmm", "st", "omm", "dve", "y", "ss", "act", "rstd", "yn", "ytm",
                                      "yte", "yout", "cout", "ms")}
        groups = range(3)
        block = ph.block()

        def head(i, s):
            return 2 * i + s

        @block.sync
        def _(sp):
            def load(i, s):
                h = head(i, s)
                sp.wait_ge(free, h + 1)
                feat = lambda r: g.feat_dram[bass.ds((h + r) * P, P), :]
                tok = lambda c: g.tok_dram[:, bass.ds(h * P + c, P)].rearrange("(t p) v -> p t v", p=P)
                gate = lambda lo, hi: g.gate_dram[bass.ds(h, 1), lo:hi, :]
                for dst, src in ((q[s][:], feat(R_MQ)), (k[s][:], feat(R_MK)), (va[s][:, :, 0:DK], tok(C_MV)),
                                 (mo[s][:], tok(C_MO)), (a2[s][0:1], gate(0, 2)), (b2[s][1:2], gate(2, 4)),
                                 (wsr[s][:], gate(4, 6)), (r4[s][:], gate(6, 10).rearrange("a r t -> (a r) t")),
                                 (dec[s][:], g.decay_dram[bass.ds(h, 1), :]),
                                 (s0[s][:, 0, :], io["ml_s0"][0, bass.ds(h * P, P), :]),
                                 (s0[s][:, 1, :], io["ml_s0"][1, bass.ds(h * P, P), :]),
                                 (gn[s][:], io["ml_g"][bass.ds(h * P, P), :])):
                    sp.dma_start(dst, src).then_inc(loaded[s], 16)

            sp.wait_ge(sem["const"], 10)
            with nc.allow_non_contiguous_dma(reason="one norm weight for a partition"):
                with sp.Fori(0, 2) as i:
                    for s in range(2):
                        load(i, s)

        @block.gpsimd
        def _(gp):
            c = sem["const"]
            for s in range(2):
                gp.memset(a2[s][:], 1.0).then_inc(c, 1)
                gp.memset(b2[s][:], 1.0).then_inc(c, 1)
                gp.memset(va[s][:, :, DK:V1], 1.0).then_inc(c, 1)
            gp.memset(half[:], -0.5).then_inc(c, 1)
            gp.memset(one[:], 1.0).then_inc(c, 1)
            gp.memset(neg[:], 0.0).then_inc(c, 1)
            gp.tensor_copy(idb[:], g.ident[:]).then_inc(c, 1)
            gp.wait_ge(c, 10)
            for d in range(2):
                sign = 1 if d == 0 else -1
                gp.affine_select(out=neg[:, d, :], in_=neg[:, d, :], compare_op=ALU.is_ge, fill=-1e30, base=0,
                                 pattern=[[0, 3], [sign, P]], channel_multiplier=-sign).then_inc(c, 1)

            with gp.Fori(0, 4) as i:
                gp.wait_ge(sem["st"], 6 * i + 6)
                for d in range(2):
                    gp.dma_start(g.outs["ml_s"][d, bass.ds(i * P, P), :], st[:, d, 0, :]).then_inc(sem["cout"], 16)
                gp.wait_ge(sem["ms"], i + 1)
                gp.tensor_tensor(rstd[:], ms[:], half[:], ALU.pow).then_inc(sem["rstd"], 1)

        @block.tensor
        def _(pe):
            pe.wait_ge(sem["const"], 12)

            def work(i, s):
                h = head(i, s)
                pe.wait_ge(loaded[s], 16 * NLOAD * i + 16 * NLOAD)
                pe.wait_ge(sem["yte"], h + 1)
                pe.matmul(ps[:, 7, 40:58], one[:], dec[s][:], start=True, stop=True)
                for j in range(NT):
                    mm = pe.transpose(ps[:, 7, 4 * j:4 * j + 4], r4[s][:, j * P:(j + 1) * P], g.ident[0:4, 0:4])
                mm.then_inc(sem["misc"], 1)
                for n in groups:
                    at = slice(n * TH, n * TH + TH)
                    if n:
                        pe.wait_ge(sem["dx"], 6 * h + 2 * n)
                    for d in range(2):
                        pe.matmul(ps[:, 1 + d, 0:TH], idb[:], neg[:, d, :], start=True, stop=False)
                        for j in range(3):
                            c = slice(n * TH + j * P, n * TH + j * P + P)
                            mm = pe.matmul(ps[:, 1 + d, j * P:(j + 1) * P], a2[s][:, d, c], b2[s][:, d, c],
                                           start=False, stop=j == 2)
                        mm.then_inc(sem["dmm"], 1)
                    if n:
                        pe.wait_ge(sem["pw"], 6 * h + 2 * n)
                    for j in range(3):
                        c = slice(n * TH + j * P, n * TH + j * P + P)
                        if n == 0 and j == 0:
                            pe.wait_ge(sem["qs"], h + 1)
                        mm = pe.matmul(ps[:, 0, j * P:(j + 1) * P], k[s][:, c], qs[:, c], start=True, stop=True)
                    mm.then_inc(sem["smm"], 1)
                    if n:
                        pe.wait_ge(sem["kw"], 6 * h + 2 * n)
                    for j in range(3):
                        c = slice(n * TH + j * P, n * TH + j * P + P)
                        mm = pe.transpose(ps[:, 3, j * P:(j + 1) * P], k[s][:, c], g.ident[:])
                    mm.then_inc(sem["kt"], 1)
                    if n:
                        pe.wait_ge(sem["wsx"], 6 * h + 2 * n)
                    for d in range(2):
                        mm = pe.matmul(ps[:, 5 + d, 0:TH], one[:], wsr[s][:, d, at], start=True, stop=True)
                        mm.then_inc(sem["wsb"], 1)
                for n in groups:
                    for d in range(2):
                        m = 2 * n + d
                        first = 3 * n if d == 0 else 6 - 3 * n
                        pe.wait_ge(sem["kw"], 6 * h + (2 * n + 1 + d if d == 0 else 6))
                        if m >= 2:
                            pe.wait_ge(sem["st"], 6 * h + m - 1)
                        bank = 4 if m % 2 == 0 else 3
                        for j in range(3):
                            c = slice((first + j) * P, (first + j) * P + P)
                            mm = pe.matmul(ps[:, bank, j * V1:j * V1 + V1], kw[:, d, c], va[s][:, first + j, :],
                                           start=True, stop=True)
                        mm.then_inc(sem["cmm"], 1)
                pe.wait_ge(sem["st"], 6 * h + 6)
                pe.wait_ge(sem["qw"], 6 * h + 6)
                pe.wait_ge(sem["pw"], 6 * h + 6)
                for n in groups:
                    for d in range(2):
                        if n:
                            pe.wait_ge(sem["y"], 3 * h + n)
                        for j in range(3):
                            t = 3 * n + j
                            c = slice(t * P, t * P + P)
                            out = ps[:, 5 + d, j * V1:j * V1 + V1]
                            mm = pe.matmul(out, pw[:, d, c], va[s][:, t, :], start=True, stop=t == 0)
                            if t:
                                mm = pe.matmul(out, qw[:, d, c], st[:, d, t, :], start=False, stop=True)
                        mm.then_inc(sem["omm"], 1)
                pe.wait_ge(sem["yn"], h + 1)
                for t in range(NT):
                    mm = pe.transpose(ps[:, t // 3, t % 3 * P:t % 3 * P + P], y2[:, t, :], g.ident[:])
                mm.then_inc(sem["ytm"], 1)

            with pe.Fori(0, 2) as i:
                for s in range(2):
                    work(i, s)

        @block.scalar
        def _(act):
            act.sem_inc(sem["yout"], 16)
            act.sem_inc(sem["yte"], 1)

            def work(i, s):
                h = head(i, s)
                act.wait_ge(loaded[s], 16 * NLOAD * i + 16 * NLOAD)
                act.activation(qs[:], q[s][:], ACT.Copy, scale=DK ** -0.5).then_inc(sem["qs"], 1)
                act.wait_ge(sem["misc"], h + 1)
                act.activation(cols[:].rearrange("p n c -> p (n c)"), ps[:, 7, 0:36], ACT.Exp).then_inc(sem["cols"], 1)
                act.activation(decb[:], ps[:, 7, 40:58], ACT.Exp).then_inc(sem["cols"], 1)
                for n in groups:
                    for d in range(2):
                        act.wait_ge(sem["dmm"], 6 * h + 2 * n + d + 1)
                        if n:
                            act.wait_ge(sem["pw"], 6 * h + 2 * n + d - 1)
                        act.activation(wx[:, d, :], ps[:, 1 + d, 0:TH], ACT.Exp).then_inc(sem["dx"], 1)
                    for d in range(2):
                        act.wait_ge(sem["wsb"], 6 * h + 2 * n + d + 1)
                        if n:
                            act.wait_ge(sem["qw"], 6 * h + 2 * n + d - 1)
                        act.activation(wb[:, d, :], ps[:, 5 + d, 0:TH], ACT.Exp).then_inc(sem["wsx"], 1)
                for t in range(NT):
                    if t % 3 == 0:
                        act.wait_ge(sem["y"], 3 * h + t // 3 + 1)
                    if t:
                        act.wait_ge(sem["ss"], 9 * h + t)
                    act.activation(junk[:], y[:, t, :], ACT.Square, accum_out=ss[:, t:t + 1]).then_inc(sem["ss"], 1)
                act.wait_ge(sem["ss"], 9 * h + NT)
                act.activation(ms[:], ss[:], ACT.Copy, bias=EPS, scale=1.0 / DK).then_inc(sem["ms"], 1)
                act.wait_ge(sem["ytm"], h + 1)
                act.wait_ge(sem["yout"], 16 * h + 16)
                act.activation(yt[:].rearrange("p (a n) -> p a n", a=3), ps[:, 0:3, 0:TH], ACT.Copy,
                               scale=gn[s][:, 0:1]).then_inc(sem["yte"], 1)
                act.wait_ge(sem["yte"], h + 2)
                act.dma_start(g.y_dram[bass.ds(h * P, P), :], yt[:]).then_inc(sem["yout"], 16)
                act.wait_ge(sem["cout"], 32 * h + 32)
                act.sem_inc(free, 1)

            act.sem_inc(free, 2)
            with act.Fori(0, 2) as i:
                for s in range(2):
                    work(i, s)
            act.wait_ge(sem["yout"], 80)

        @block.vector
        def _(v):
            link = Chain(v, sem["dve"])
            def work(i, s):
                h = head(i, s)
                v.wait_ge(loaded[s], 16 * NLOAD * i + 16 * NLOAD)
                for n in groups:
                    at = slice(n * TH, n * TH + TH)
                    for d in range(2):
                        v.wait_ge(sem["dx"], 6 * h + 2 * n + d + 1)
                        v.wait_ge(sem["smm"], 3 * h + n + 1)
                        v.tensor_tensor(pw[:, d, at], ps[:, 0, 0:TH], wx[:, d, :], ALU.mult).then_inc(sem["pw"], 1)
                    if n == 0:
                        v.wait_ge(sem["cols"], 2 * h + 2)
                    v.wait_ge(sem["kt"], 3 * h + n + 1)
                    for d in range(2):
                        w = cols[:, 3 * n:3 * n + 3, d].unsqueeze(2).broadcast_to([P, 3, P])
                        v.tensor_tensor(kw[:, d, at].rearrange("p (j c) -> p j c", j=3),
                                        ps[:, 3, 0:TH].rearrange("p (j c) -> p j c", j=3), w, ALU.mult).then_inc(sem["kw"], 1)
                    for d in range(2):
                        v.wait_ge(sem["wsx"], 6 * h + 2 * n + d + 1)
                        v.tensor_tensor(qw[:, d, at], qs[:, at], wb[:, d, :], ALU.mult).then_inc(sem["qw"], 1)
                v.wait_ge(free, h + 2)
                for n in groups:
                    for d in range(2):
                        m = 2 * n + d
                        first = 3 * n if d == 0 else 6 - 3 * n
                        v.wait_ge(sem["cmm"], 6 * h + m + 1)
                        bank = 4 if m % 2 == 0 else 3
                        order = range(3) if d == 0 else (2, 1, 0)
                        if n == 0:
                            v.tensor_copy(st[:, d, 1 if d == 0 else NT - 1, :], s0[s][:, d, :]).then_inc(sem["dve"], 1)
                            link.n += 1
                        for j in order:
                            t = first + j
                            add = ps[:, bank, j * V1:j * V1 + V1]
                            nxt = t + 1 if d == 0 else t - 1
                            if t == 0:
                                ins = v.tensor_copy(st[:, d, 0, :], add)
                            elif 1 <= nxt < NT:
                                v.wait_ge(sem["dve"], link.value())
                                ins = v.scalar_tensor_tensor(out=st[:, d, nxt, :], in0=st[:, d, t, :],
                                                             scalar=decb[:, NT * d + t:NT * d + t + 1], in1=add,
                                                             op0=ALU.mult, op1=ALU.add)
                            else:
                                continue
                            ins.then_inc(sem["dve"], 1)
                            link.n += 1
                        v.wait_ge(sem["dve"], link.value())
                        v.sem_inc(sem["st"], 1)
                for n in groups:
                    three = slice(3 * n, 3 * n + 3)
                    for d in range(2):
                        v.wait_ge(sem["omm"], 6 * h + 2 * n + d + 1)
                    o = [ps[:, 5 + d, 0:3 * V1].rearrange("p (j c) -> p j c", j=3) for d in range(2)]
                    for d in range(2):
                        link(v.scalar_tensor_tensor(out=den[:, d, three], in0=o[d][:, :, DK], scalar=-1.0,
                                                    in1=cols[:, three, 2 + d], op0=ALU.mult, op1=ALU.max))
                        link(v.tensor_tensor(den[:, d, three], den[:, d, three], o[d][:, :, DK], ALU.max))
                        link(v.reciprocal(den[:, d, three], den[:, d, three]))
                        r = den[:, d, three].unsqueeze(2).broadcast_to([P, 3, DK])
                        link(v.tensor_tensor((y, y2)[d][:, three, :], o[d][:, :, 0:DK], r, ALU.mult))
                    v.tensor_tensor(y[:, three, :], y[:, three, :], y2[:, three, :], ALU.add).then_inc(sem["y"], 1)
                v.wait_ge(sem["rstd"], h + 1)
                for t in range(NT):
                    ins = v.scalar_tensor_tensor(out=y2[:, t, :], in0=y[:, t, :], scalar=rstd[:, t:t + 1],
                                                 in1=mo[s][:, t, :], op0=ALU.mult, op1=ALU.mult)
                ins.then_inc(sem["yn"], 1)

            PER = 2 + 8 + 8 + 24
            with v.Fori(0, 2) as i:
                link.loop(i, 2 * PER)
                for s in range(2):
                    work(i, s)
            link.end(2)


def hgrn(nc, g):
    io, ps = g.io, g.ps
    LEVELS = 8
    with Phase(nc, "hgr") as ph:
        two = lambda name, shape: [ph.sb(f"{name}{s}", shape) for s in range(2)]
        q, hf = two("q", [P, T]), two("hf", [P, 2, T])
        va, hg = two("va", [P, NT, P]), two("hg", [P, NT, P])
        s0, gn = two("s0", [P, 2, P]), two("gn", [P, 1])
        tot = [ph.sb(f"tot{n}", [P, 2, T >> n]) for n in range(8)]
        qp, kp = ph.sb("qp", [P, 2, T]), ph.sb("kp", [P, 2, T])
        ad = ph.sb("ad", [P, 2, NT, 32])
        am = ph.sb("am", [P, 2, NT, P])
        kt = ph.sb("kt", [P, 2, T])
        st = ph.sb("st", [P, 2, NT, P])
        y2 = ph.sb("y2", [P, NT, P])
        junk = ph.sb("junk", [P, P])
        ss, ms, rstd, half = (ph.sb(n, [P, NT]) for n in ("ss", "ms", "rstd", "half"))
        yt = ph.sb("yt", [P, T])
        mask = ph.sb("mask", [P, 12, 32], I32)
        NLOAD = 8
        loaded = [ph.sem(f"loaded{s}") for s in range(2)]
        free = ph.sem("free")
        sem = {n: ph.sem(n) for n in ("const", "mask", "gates", "ini", "lmm", "pc", "upd", "far", "diag", "ktm", "kte",
                                      "smm", "dve", "omm", "ss", "ms", "rstd", "yn", "ytm", "yte", "yout", "cout", "st")}
        block = ph.block()

        def taken(l, d):
            return l + 2 * d + 1 if l < 2 else 2 * l + d + 1

        def far_order(d):
            return (0, 1) if d == 0 else (1, 0)

        @block.sync
        def _(sp):
            def load(i, s):
                h = 2 * i + s
                sp.wait_ge(free, h + 1)
                feat = lambda r: g.feat_dram[bass.ds((h + r) * P, P), :]
                tok = lambda c: g.tok_dram[:, bass.ds(h * P + c, P)].rearrange("(t p) v -> p t v", p=P)
                for dst, src in ((q[s][:], feat(R_HQ)), (hf[s][:, 0, :], feat(R_HF)), (hf[s][:, 1, :], feat(R_HF + 4)),
                                 (va[s][:], tok(C_HI)), (hg[s][:], tok(C_HG)),
                                 (s0[s][:, 0, :], io["hg_s0"][0, bass.ds(h * P, P), :]),
                                 (s0[s][:, 1, :], io["hg_s0"][1, bass.ds(h * P, P), :]),
                                 (gn[s][:], io["hg_g"][bass.ds(h * P, P), :])):
                    sp.dma_start(dst, src).then_inc(loaded[s], 16)

            sp.dma_start(mask[:], io["hg_mask"]).then_inc(sem["mask"], 16)
            with nc.allow_non_contiguous_dma(reason="one norm weight for a partition"):
                with sp.Fori(0, 2) as i:
                    for s in range(2):
                        load(i, s)

        @block.gpsimd
        def _(gp):
            gp.memset(half[:], -0.5).then_inc(sem["const"], 1)
            gp.memset(ad[:], 0.0).then_inc(sem["const"], 1)
            gp.memset(am[:], 0.0).then_inc(sem["const"], 1)
            with gp.Fori(0, 4) as i:
                gp.wait_ge(sem["st"], 6 * i + 6)
                for d in range(2):
                    gp.dma_start(g.outs["hg_s"][d, bass.ds(i * P, P), :], st[:, d, 0, :]).then_inc(sem["cout"], 16)
                gp.wait_ge(sem["ms"], i + 1)
                gp.tensor_tensor(rstd[:], ms[:], half[:], ALU.pow).then_inc(sem["rstd"], 1)

        @block.tensor
        def _(pe):
            def work(i, s):
                h = 2 * i + s
                pe.wait_ge(loaded[s], 16 * NLOAD * i + 16 * NLOAD)
                pe.wait_ge(sem["yte"], h + 1)
                pe.wait_ge(sem["gates"], 2 * h + 2)
                for l in range(6):
                    for d in range(2):
                        bank = 2 * (l % 2) + d
                        if l == 1:
                            pe.wait_ge(sem["ini"], 2 * h + d + 1)
                        if l >= 2:
                            pe.wait_ge(sem["upd"], 14 * h + 2 * (l - 2) + d + 1)
                            pe.wait_ge(sem["pc"], 12 * h + taken(l - 2, d))
                        for b in range(T // 32):
                            c = slice(32 * b, 32 * b + 32)
                            at = 32 * (b % 4)
                            mm = pe.matmul(ps[at:at + 32, bank, b // 4 * 32:b // 4 * 32 + 32], kp[:, d, c],
                                           q[s][:, c] if l == 0 else qp[:, d, c], start=True, stop=True)
                        mm.then_inc(sem["lmm"], 1)
                for d in range(2):
                    pe.wait_ge(sem["upd"], 14 * h + 8 + d + 1)
                    pe.wait_ge(sem["pc"], 12 * h + 8 + d + 1)
                    kb, qb = far_order(d)
                    for t in range(NT):
                        for half_ in range(2):
                            at = 64 * half_ + 32 * kb
                            mm = pe.matmul(ps[at:at + 32, d, 32 * t:32 * t + 32],
                                           kp[:, d, t * P + at:t * P + at + 32],
                                           qp[:, d, t * P + 64 * half_ + 32 * qb:t * P + 64 * half_ + 32 * qb + 32],
                                           start=True, stop=True)
                    mm.then_inc(sem["lmm"], 1)
                for d in range(2):
                    pe.wait_ge(sem["upd"], 14 * h + 10 + d + 1)
                    kb, qb = far_order(d)
                    for t in range(NT):
                        bank, col = 4 + 2 * d + t // 5, t % 5 * 64
                        mm = pe.matmul(ps[64 * kb:64 * kb + 64, bank, col:col + 64],
                                       kp[:, d, t * P + 64 * kb:t * P + 64 * kb + 64],
                                       qp[:, d, t * P + 64 * qb:t * P + 64 * qb + 64], start=True, stop=True)
                    mm.then_inc(sem["lmm"], 1)
                for n in range(3):
                    for d in range(2):
                        m = 2 * n + d
                        first = 3 * n if d == 0 else 6 - 3 * n
                        if m < 2:
                            pe.wait_ge(sem["upd"], 14 * h + 12 + d + 1)
                            pe.wait_ge(sem["far"], 4 * h + 2)
                        else:
                            pe.wait_ge(sem["kte"], 6 * h + m - 1)
                        for j in range(3):
                            c = slice((first + j) * P, (first + j) * P + P)
                            mm = pe.transpose(ps[:, m % 2, j * P:j * P + P], kp[:, d, c], g.ident[:])
                        mm.then_inc(sem["ktm"], 1)
                for n in range(3):
                    for d in range(2):
                        m = 2 * n + d
                        first = 3 * n if d == 0 else 6 - 3 * n
                        pe.wait_ge(sem["kte"], 6 * h + m + 1)
                        pe.wait_ge(sem["pc"], 12 * h + 12)
                        if m >= 2:
                            pe.wait_ge(sem["st"], 6 * h + m - 1)
                        for j in range(3):
                            c = slice((first + j) * P, (first + j) * P + P)
                            mm = pe.matmul(ps[:, 2 + m % 2, j * P:j * P + P], kt[:, d, c], va[s][:, first + j, :],
                                           start=True, stop=True)
                        mm.then_inc(sem["smm"], 1)
                pe.wait_ge(sem["far"], 4 * h + 4)
                pe.wait_ge(sem["diag"], h + 1)
                pe.wait_ge(sem["st"], 6 * h + 6)
                for t in range(NT):
                    out = ps[:, 4 + t // 3, t % 3 * P:t % 3 * P + P]
                    for d in range(2):
                        mm = pe.matmul(out, am[:, d, t, :], va[s][:, t, :], start=d == 0, stop=t == 0 and d == 1)
                    if t:
                        for d in range(2):
                            mm = pe.matmul(out, qp[:, d, t * P:t * P + P], st[:, d, t, :], start=False, stop=d == 1)
                    if t % 3 == 2:
                        mm.then_inc(sem["omm"], 1)
                pe.wait_ge(sem["yn"], h + 1)
                for t in range(NT):
                    mm = pe.transpose(ps[:, t // 3, t % 3 * P:t % 3 * P + P], y2[:, t, :], g.ident[:])
                mm.then_inc(sem["ytm"], 1)

            with pe.Fori(0, 2) as i:
                for s in range(2):
                    work(i, s)

        @block.scalar
        def _(act):
            act.sem_inc(sem["yout"], 16)
            act.sem_inc(sem["yte"], 1)
            act.sem_inc(free, 2)
            act.wait_ge(sem["const"], 3)

            def work(i, s):
                h = 2 * i + s
                act.wait_ge(loaded[s], 16 * NLOAD * i + 16 * NLOAD)
                act.activation(kp[:], hf[s][:], ACT.Sigmoid, scale=-1.0).then_inc(sem["gates"], 1)
                act.activation(tot[0][:], hf[s][:], ACT.Sigmoid).then_inc(sem["gates"], 1)
                for d in range(2):
                    act.wait_ge(sem["lmm"], 16 * h + 12 + d + 1)
                    kb, qb = far_order(d)
                    for half_ in range(2):
                        at, to = 64 * half_ + 32 * kb, 64 * half_ + 32 * qb
                        ins = act.activation(am[at:at + 32, d, :, to:to + 32],
                                             ps[at:at + 32, d, 0:32 * NT].rearrange("p (t c) -> p t c", c=32), ACT.Copy)
                    ins.then_inc(sem["far"], 1)
                for d in range(2):
                    act.wait_ge(sem["lmm"], 16 * h + 14 + d + 1)
                    kb, qb = far_order(d)
                    rows, to = slice(64 * kb, 64 * kb + 64), slice(64 * qb, 64 * qb + 64)
                    act.activation(am[rows, d, 0:5, to], ps[rows, 4 + 2 * d, 0:320].rearrange("p (t c) -> p t c", c=64), ACT.Copy)
                    act.activation(am[rows, d, 5:NT, to], ps[rows, 5 + 2 * d, 0:256].rearrange("p (t c) -> p t c", c=64),
                                   ACT.Copy).then_inc(sem["far"], 1)
                for n in range(3):
                    for d in range(2):
                        m = 2 * n + d
                        first = 3 * n if d == 0 else 6 - 3 * n
                        act.wait_ge(sem["ktm"], 6 * h + m + 1)
                        act.activation(kt[:, d, first * P:first * P + TH], ps[:, m % 2, 0:TH], ACT.Copy).then_inc(sem["kte"], 1)
                act.wait_ge(sem["pc"], 12 * h + 12)
                for d in range(2):
                    for b in range(4):
                        r = slice(32 * b, 32 * b + 32)
                        ins = act.activation(am[r, d, :, r], ad[r, d, :, :], ACT.Copy)
                ins.then_inc(sem["diag"], 1)
                for t in range(NT):
                    if t % 3 == 0:
                        act.wait_ge(sem["omm"], 3 * h + t // 3 + 1)
                    if t:
                        act.wait_ge(sem["ss"], 9 * h + t)
                    act.activation(junk[:], ps[:, 4 + t // 3, t % 3 * P:t % 3 * P + P], ACT.Square,
                                   accum_out=ss[:, t:t + 1]).then_inc(sem["ss"], 1)
                act.wait_ge(sem["ss"], 9 * h + NT)
                act.activation(ms[:], ss[:], ACT.Copy, bias=EPS, scale=1.0 / DK).then_inc(sem["ms"], 1)
                act.wait_ge(sem["ytm"], h + 1)
                act.wait_ge(sem["yout"], 16 * h + 16)
                act.activation(yt[:].rearrange("p (a n) -> p a n", a=3), ps[:, 0:3, 0:TH], ACT.Copy,
                               scale=gn[s][:, 0:1]).then_inc(sem["yte"], 1)
                act.wait_ge(sem["yte"], h + 2)
                act.dma_start(g.y_dram[bass.ds((HEADS + h) * P, P), :], yt[:]).then_inc(sem["yout"], 16)
                act.wait_ge(sem["cout"], 32 * h + 32)
                act.sem_inc(free, 1)

            with act.Fori(0, 2) as i:
                for s in range(2):
                    work(i, s)
            act.wait_ge(sem["yout"], 80)

        @block.vector
        def _(v):
            link = Chain(v, sem["dve"])
            v.wait_ge(sem["mask"], 16)
            v.wait_ge(sem["const"], 3)

            def work(i, s):
                h = 2 * i + s
                v.wait_ge(loaded[s], 16 * NLOAD * i + 16 * NLOAD)
                v.wait_ge(sem["gates"], 2 * h + 2)
                v.wait_ge(free, h + 2)
                for d in range(2):
                    v.tensor_tensor(qp[:, d, :], q[s][:], tot[0][:, d, :], ALU.mult).then_inc(sem["ini"], 1)

                def take(l, d):
                    m = mask[:, 2 * l + d, :].unsqueeze(1).broadcast_to([P, NT, 32])
                    v.copy_predicated(ad[:, d, :, :], m, ps[:, 2 * (l % 2) + d, 0:32 * NT].rearrange("p (t c) -> p t c", c=32)
                                      ).then_inc(sem["pc"], 1)

                def widen(l, d):
                    size = 1 << (l - 1)
                    kb, qb = far_order(d)
                    v.wait_ge(sem["lmm"], 16 * h + 2 * l + d + 1)
                    if l > 1 or d:
                        v.wait_ge(sem["pc"], 12 * h + (2 if l == 1 else min(2 * l + d, 12)))
                    pair = lambda x: x[:, d, :].rearrange("p (n a e) -> p n a e", a=2, e=size)
                    t2 = tot[l - 1][:, d, :].rearrange("p (n a) -> p n a", a=2)
                    wide = lambda b: t2[:, :, b:b + 1].broadcast_to([P, T // (2 * size), size])
                    v.tensor_tensor(pair(qp)[:, :, qb, :], pair(qp)[:, :, qb, :], wide(kb), ALU.mult)
                    if l == 1:
                        take(0, d)
                        v.wait_ge(sem["pc"], 12 * h + 2 * d + 1)
                    elif l < 6:
                        take(l, d)
                    v.tensor_tensor(pair(kp)[:, :, kb, :], pair(kp)[:, :, kb, :], wide(qb), ALU.mult).then_inc(sem["upd"], 1)
                    if l == 1:
                        take(1, d)
                    link(v.tensor_tensor(tot[l][:, d, :], t2[:, :, 0], t2[:, :, 1], ALU.mult))

                for l in range(1, LEVELS):
                    for d in range(2):
                        widen(l, d)
                for n in range(3):
                    for d in range(2):
                        m = 2 * n + d
                        first = 3 * n if d == 0 else 6 - 3 * n
                        v.wait_ge(sem["smm"], 6 * h + m + 1)
                        if n == 0:
                            v.tensor_copy(st[:, d, 1 if d == 0 else NT - 1, :], s0[s][:, d, :]).then_inc(sem["dve"], 1)
                            link.n += 1
                        for j in range(3) if d == 0 else (2, 1, 0):
                            t = first + j
                            add = ps[:, 2 + m % 2, j * P:j * P + P]
                            nxt = t + 1 if d == 0 else t - 1
                            if t == 0:
                                ins = v.tensor_copy(st[:, d, 0, :], add)
                            elif 1 <= nxt < NT:
                                v.wait_ge(sem["dve"], link.value())
                                ins = v.scalar_tensor_tensor(out=st[:, d, nxt, :], in0=st[:, d, t, :],
                                                             scalar=tot[7][:, d, t:t + 1], in1=add,
                                                             op0=ALU.mult, op1=ALU.add)
                            else:
                                continue
                            ins.then_inc(sem["dve"], 1)
                            link.n += 1
                        v.wait_ge(sem["dve"], link.value())
                        v.sem_inc(sem["st"], 1)
                v.wait_ge(sem["rstd"], h + 1)
                for t in range(NT):
                    ins = v.scalar_tensor_tensor(out=y2[:, t, :], in0=ps[:, 4 + t // 3, t % 3 * P:t % 3 * P + P],
                                                 scalar=rstd[:, t:t + 1], in1=hg[s][:, t, :], op0=ALU.mult, op1=ALU.mult)
                ins.then_inc(sem["yn"], 1)

            PER = 14 + 2 + 8 + 8
            with v.Fori(0, 2) as i:
                link.loop(i, 2 * PER)
                for s in range(2):
                    work(i, s)
            link.end(2)


def attention(nc, g):
    io, ps = g.io, g.ps
    NK = NT + 1
    KW = (NT - 1) * P + PAST
    H1 = HD + 1
    QS = HD ** -0.5
    with Phase(nc, "att") as ph:
        kn = ph.sb("kn", [P, NT, KV, HD])
        k2 = ph.sb("k2", [P, NT, KV, HD])
        kr = ph.sb("kr", [P, NK, KV, HD])
        kpart = [ph.sb(f"kpart{n}", [P, NK, KV, 2, HD], F32R) for n in ("hi", "lo")]
        kt = [ph.sb(f"kt{n}", [P, KV, NK * P], F32R) for n in ("hi", "lo")]
        va = ph.sb("va", [P, NK, KV, H1])
        kss, kms, krs, khalf = (ph.sb(n, [P, NT * KV]) for n in ("kss", "kms", "krs", "khalf"))
        grow = ph.sb("grow", [P, 2, HD])
        tab = ph.sb("tab", [P, NT - 1, 2, HD // 2])
        qtab = ph.sb("qtab", [P, NT - 1, 4, HD // 2])
        r1, r2 = ph.sb("r1", [P, NT - 1, KV, HD // 2]), ph.sb("r2", [P, NT - 1, KV, HD // 2])
        q = ph.sb("q", [P, AH, HD])
        qtb = ph.sb("qtb", [P, 4, HD // 2])
        q2, qn, qr = (ph.sb(n, [P, AH, HD]) for n in ("q2", "qn", "qr"))
        u1, u2 = ph.sb("u1", [P, AH, HD // 2]), ph.sb("u2", [P, AH, HD // 2])
        qss, qms, qrs = (ph.sb(n, [P, AH]) for n in ("qss", "qms", "qrs"))
        qpart = ph.sb("qpart", [P, AH, 2, HD], F32R)
        qt = ph.sb("qt", [P, AH, P], F32R)
        pr = [ph.sb(f"pr{i}", [P, KW]) for i in range(2)]
        pt = [ph.sb(f"pt{i}", [P, KW]) for i in range(2)]
        mx, nm = ph.sb("mx", [P, 2]), ph.sb("nm", [P, 2])
        rs = ph.sb("rs", [P, 2])
        mxc, rsc = ph.sb("mxc", [P, AH]), ph.sb("rsc", [P, AH])
        y = ph.sb("y", [P, AH, HD])
        yt = [ph.sb(f"yt{i}", [P, 4, P]) for i in range(2)]
        names = ("load qload const knd kpow kout ktm kte qd qpow rope qpart qtm qte smm mx ex ptm pte omm on ytm yte "
                 "yout0 yout1 kv tabd csmm cmx cex cptm cpte comm cdone dve cpart")
        sem = {n: ph.sem(n) for n in names.split()}
        block = ph.block()
        SB = [slice(0, 3), slice(3, 6)]

        PT, OB = 6, 7

        def use(h, n):
            return 3 * h + n + (2 if h > 5 else 0)

        USES = 24 + 2 + 1

        @block.sync
        def _(sp):
            tok = lambda c, w: g.tok_dram[:, c:c + w].rearrange("(t p) v -> p t v", p=P)
            with nc.allow_non_contiguous_dma(reason="rows of 64 values"):
                sp.dma_start(kn[:].rearrange("p t h d -> p t (h d)"), tok(C_AK, KV * HD)).then_inc(sem["load"], 16)
                sp.dma_start(kr[:, 8].rearrange("p h d -> p (h d)"), io["cache_k"]).then_inc(sem["load"], 16)
                sp.dma_start(grow[:].rearrange("p a d -> p (a d)"), io["qk_g"].partition_broadcast(P)).then_inc(sem["load"], 16)
                sp.dma_start(tab[:], io["rope"]).then_inc(sem["load"], 16)
                for kv in range(KV):
                    src = g.tok_dram[:, C_AV + kv * HD:C_AV + kv * HD + HD]
                    sp.dma_start(va[:, 0:8, kv, 0:HD], src[CTX:T, :].rearrange("(t p) v -> p t v", p=P)).then_inc(sem["kv"], 16)
                    sp.dma_start(va[:, 9, kv, 0:HD], src[0:CTX, :]).then_inc(sem["kv"], 16)
                    sp.dma_start(va[:, 8, kv, 0:HD], io["cache_v"][:, kv * HD:kv * HD + HD]).then_inc(sem["kv"], 16)
            sp.dma_start(q[:].rearrange("p h d -> p (h d)"), g.tok_dram[0:P, C_AQ:C_AQ + AH * HD]).then_inc(sem["qload"], 16)
            sp.wait_ge(sem["kpow"], 3)
            sp.dma_start(g.outs["k"], kn[:, 0].rearrange("p h d -> p (h d)")).then_inc(sem["kout"], 16)
            sp.dma_start(g.outs["v"], g.tok_dram[0:CTX, C_AV:C_AV + KV * HD]).then_inc(sem["kout"], 16)
            sp.wait_ge(sem["cpart"], 1)
            sp.dma_start(q[:].rearrange("p h d -> p (h d)"), g.tok_dram[P:2 * P, C_AQ:C_AQ + AH * HD]).then_inc(sem["qload"], 16)
            with sp.Fori(0, 7) as i:
                sp.wait_ge(sem["qpart"], i + 1)
                sp.dma_start(q[:].rearrange("p h d -> p (h d)"),
                             g.tok_dram[bass.ds(i * P + 2 * P, P), C_AQ:C_AQ + AH * HD]).then_inc(sem["qload"], 16)
            sp.wait_ge(sem["kout"], 32)

        @block.gpsimd
        def _(gp):
            gp.memset(khalf[:], -0.5).then_inc(sem["const"], 1)
            gp.memset(va[:, :, :, HD:H1], 1.0).then_inc(sem["const"], 1)
            gp.wait_ge(sem["const"], 1)
            gp.wait_ge(sem["knd"], 3)
            gp.tensor_tensor(krs[:], kms[:], khalf[:], ALU.pow).then_inc(sem["kpow"], 1)
            gp.wait_ge(sem["qd"], 3)
            gp.tensor_tensor(qrs[:], qms[:], khalf[:, 0:AH], ALU.pow).then_inc(sem["qpow"], 1)

            def rope(n):
                gp.wait_ge(sem["qd"], 4 * n + 4 + 3)
                gp.tensor_tensor(qrs[:], qms[:], khalf[:, 0:AH], ALU.pow).then_inc(sem["qpow"], 1)
                gp.wait_ge(sem["qd"], 4 * n + 4 + 4)
                x = qn[:].rearrange("p h (d e) -> p h d e", e=2)
                o = qr[:].rearrange("p h (d e) -> p h d e", e=2)
                w = lambda c: qtb[:, c, :].unsqueeze(1).broadcast_to([P, AH, HD // 2])
                for e in range(2):
                    a, b = (0, 1) if e == 0 else (2, 3)
                    gp.tensor_tensor(u1[:], x[:, :, :, 0], w(a), ALU.mult).then_inc(sem["rope"], 1)
                    gp.tensor_tensor(u2[:], x[:, :, :, 1], w(b), ALU.mult).then_inc(sem["rope"], 1)
                    gp.wait_ge(sem["rope"], 6 * n + 3 * e + 2)
                    gp.tensor_tensor(o[:, :, :, e], u1[:], u2[:], ALU.subtract if e == 0 else ALU.add).then_inc(sem["rope"], 1)
                    gp.wait_ge(sem["rope"], 6 * n + 3 * e + 3)

            rope(0)
            with gp.Fori(0, 7) as i:
                rope(i + 1)

        def scores(pe, buf, h):
            kv = h % 2
            for n in range(3):
                for part in range(2):
                    mm = pe.matmul(ps[:, 3 * buf + n, 0:TH], qt[:, h, :], kt[part][:, kv, n * TH:n * TH + TH],
                                   start=part == 0, stop=part == 1)
            mm.then_inc(sem["smm"], 1)

        @block.tensor
        def _(pe):
            pe.wait_ge(sem["knd"], 5)
            n = 0
            for part in range(2):
                for kv in range(KV):
                    for t0, nt in ((0, 4), (4, 4), (8, 2)):
                        if n >= 6:
                            pe.wait_ge(sem["kte"], n - 5)
                        for t in range(nt):
                            mm = pe.transpose(ps[:, n % 6, t * P:t * P + P],
                                              kpart[part][:, t0 + t, kv].rearrange("p a d -> p (a d)").bitcast(F32), g.ident[:])
                        mm.then_inc(sem["ktm"], 1)
                        n += 1
            pe.wait_ge(sem["kte"], 12)
            pe.wait_ge(sem["cpart"], 1)
            for h in range(AH):
                mm = pe.transpose(ps[:, h // 4, h % 4 * P:h % 4 * P + P],
                                  qpart[:, h].rearrange("p a d -> p (a d)").bitcast(F32), g.ident[:])
            mm.then_inc(sem["qtm"], 1)
            pe.wait_ge(sem["qte"], 1)
            for h in range(AH):
                for part in range(2):
                    mm = pe.matmul(ps[:, 2 + h // 4, h % 4 * P:h % 4 * P + P], qt[:, h, :], kt[part][:, h % 2, 9 * P:10 * P],
                                   start=part == 0, stop=part == 1)
            mm.then_inc(sem["csmm"], 1)
            pe.wait_ge(sem["cex"], 8)
            for h in range(AH):
                mm = pe.transpose(ps[:, 4 + h // 4, h % 4 * P:h % 4 * P + P], pr[0][:, h * P:h * P + P], g.ident[:])
            mm.then_inc(sem["cptm"], 1)
            pe.wait_ge(sem["cpte"], 1)
            pe.wait_ge(sem["kv"], 96)
            pe.wait_ge(sem["const"], 2)
            for h in range(AH):
                mm = pe.matmul(ps[:, 6 + h // 4, h % 4 * H1:h % 4 * H1 + H1], pt[0][:, h * P:h * P + P], va[:, 9, h % 2, :],
                               start=True, stop=True)
            mm.then_inc(sem["comm"], 1)
            pe.wait_ge(sem["qpart"], 1)
            for h in range(AH):
                mm = pe.transpose(ps[:, h // 4, h % 4 * P:h % 4 * P + P],
                                  qpart[:, h].rearrange("p a d -> p (a d)").bitcast(F32), g.ident[:])
            mm.then_inc(sem["qtm"], 1)
            pe.wait_ge(sem["cdone"], 1)
            for t in range(4):
                mm = pe.transpose(ps[:, 2, t * P:t * P + P], y[:, 2 * t:2 * t + 2, :].rearrange("p h d -> p (h d)"), g.ident[:])
            mm.then_inc(sem["ytm"], 1)
            pe.wait_ge(sem["yte"], 1)
            pe.wait_ge(sem["qte"], 2)
            scores(pe, 0, 0)
            scores(pe, 1, 1)

            def tile(i, more):
                for h in range(AH):
                    nh = 8 * i + h
                    pe.wait_ge(sem["ex"], nh + 1)
                    for n in range(3):
                        if n == 2 and (h < 6 or more):
                            if h == 6 and more:
                                pe.wait_ge(sem["pte"], USES * i + 20 + 1)
                            scores(pe, h % 2, (h + 2) % AH)
                        k = use(h, n)
                        pe.wait_ge(sem["pte"], USES * i + k + 1)
                        for j in range(3):
                            c = (3 * n + j) * P
                            mm = pe.transpose(ps[:, PT, j * P:j * P + P], pr[h % 2][:, c:c + P], g.ident[:])
                        mm.then_inc(sem["ptm"], 1)
                    if h:
                        values(i, h - 1)
                    if h == 5:
                        if more:
                            pe.wait_ge(sem["qpart"], i + 2)
                        for n in range(2):
                            k = 18 + n
                            pe.wait_ge(sem["pte"], USES * i + k + 1)
                            for j in range(4):
                                mm = pe.transpose(ps[:, PT, j * P:j * P + P],
                                                  qpart[:, 4 * n + j].rearrange("p a d -> p (a d)").bitcast(F32), g.ident[:])
                            mm.then_inc(sem["ptm"], 1)
                values(i, AH - 1)
                pe.wait_ge(sem["on"], 8 * i + 9)
                pe.wait_ge(sem["pte"], USES * i + USES)
                for t in range(4):
                    mm = pe.transpose(ps[:, PT, t * P:t * P + P],
                                      y[:, 2 * t:2 * t + 2, :].rearrange("p h d -> p (h d)"), g.ident[:])
                mm.then_inc(sem["ptm"], 1)

            def values(i, h):
                pe.wait_ge(sem["pte"], USES * i + use(h, 2) + 2)
                pe.wait_ge(sem["on"], 8 * i + h + 1)
                for t in range(NT):
                    mm = pe.matmul(ps[:, OB, 0:H1], pt[h % 2][:, t * P:t * P + P], va[:, t, h % 2, :],
                                   start=t == 0, stop=t == NT - 1)
                mm.then_inc(sem["omm"], 1)

            with pe.Fori(0, 7) as i:
                tile(i, True)
            tile(7, False)

        @block.scalar
        def _(act):
            for n in range(12):
                act.wait_ge(sem["ktm"], n + 1)
                part, kv, (t0, nt) = n // 6, n // 3 % 2, ((0, 4), (4, 4), (8, 2))[n % 3]
                act.activation(kt[part][:, kv, t0 * P:(t0 + nt) * P], ps[:, n % 6, 0:nt * P], ACT.Copy).then_inc(sem["kte"], 1)
            act.wait_ge(sem["qtm"], 1)
            act.activation(qt[:], ps[:, 0:2, :].rearrange("p a (h n) -> p (a h) n", h=4), ACT.Copy).then_inc(sem["qte"], 1)
            act.wait_ge(sem["cmx"], 1)
            for h in range(AH):
                act.activation(pr[0][:, h * P:h * P + P], ps[:, 2 + h // 4, h % 4 * P:h % 4 * P + P], ACT.Exp,
                               bias=mxc[:, h:h + 1], scale=QS).then_inc(sem["cex"], 1)
            act.wait_ge(sem["cptm"], 1)
            act.activation(pt[0][:, 0:AH * P].rearrange("p (a n) -> p a n", a=2), ps[:, 4:6, :], ACT.Copy).then_inc(sem["cpte"], 1)
            act.wait_ge(sem["qtm"], 2)
            act.wait_ge(sem["csmm"], 1)
            act.activation(qt[:], ps[:, 0:2, :].rearrange("p a (h n) -> p (a h) n", h=4), ACT.Copy).then_inc(sem["qte"], 1)
            act.wait_ge(sem["ytm"], 1)
            act.activation(yt[0][:].rearrange("p t n -> p (t n)"), ps[:, 2, :], ACT.Copy).then_inc(sem["yte"], 1)
            act.wait_ge(sem["yte"], 1)
            act.dma_start(g.y_dram[2 * 4 * P:, 0:P].rearrange("(t p) n -> p t n", p=P), yt[0][:]).then_inc(sem["yout0"], 16)
            act.wait_ge(sem["yout0"], 16)

            def exps(i, h):
                nh = 8 * i + h
                act.wait_ge(sem["mx"], nh + 1)
                if h >= 2:
                    act.wait_ge(sem["ptm"], USES * i + use(h - 2, 2) + 1)
                elif h == 0 and not (isinstance(i, int) and i == 0):
                    act.wait_ge(sem["ptm"], USES * i + use(6, 2) + 1 - USES)
                act.activation(pr[h % 2][:], ps[:, SB[h % 2], 0:TH], ACT.Exp, bias=nm[:, h % 2:h % 2 + 1],
                               scale=QS).then_inc(sem["ex"], 1)

            def tile(i, more):
                for h in range(AH):
                    k = use(h, 1)
                    act.wait_ge(sem["ptm"], USES * i + k + 1)
                    act.activation(pt[h % 2][:, TH:2 * TH], ps[:, PT, 0:TH], ACT.Copy).then_inc(sem["pte"], 1)
                    if h < 7:
                        exps(i, h + 1)
                    elif more:
                        exps(i + 1, 0)
                    if h == 5:
                        for n in range(2):
                            k = 18 + n
                            act.wait_ge(sem["ptm"], USES * i + k + 1)
                            act.activation(qt[:, 4 * n:4 * n + 4, :], ps[:, PT, :].rearrange("p (h n) -> p h n", h=4),
                                           ACT.Copy).then_inc(sem["pte"], 1)
                act.wait_ge(sem["ptm"], USES * i + USES)
                act.wait_ge(sem["yout0"], 16 * i + 16)
                act.activation(yt[0][:].rearrange("p t n -> p (t n)"), ps[:, PT, :], ACT.Copy).then_inc(sem["pte"], 1)
                act.wait_ge(sem["pte"], USES * i + USES + 1)
                act.dma_start(g.y_dram[2 * 4 * P:, bass.ds(i * P + P, P)].rearrange("(t p) n -> p t n", p=P),
                              yt[0][:]).then_inc(sem["yout0"], 16)

            act.sem_inc(sem["pte"], 1)
            exps(0, 0)
            with act.Fori(0, 7) as i:
                tile(i, True)
            tile(7, False)
            act.wait_ge(sem["yout0"], 16 * 9)

        @block.vector
        def _(v):
            link = Chain(v, sem["dve"])
            wide = lambda x, n: x.unsqueeze(2).broadcast_to([P, n, HD])
            flat = lambda x: x.rearrange("p t h d -> p (t h) d")
            v.wait_ge(sem["load"], 64)
            v.tensor_tensor(k2[:], kn[:], kn[:], ALU.mult).then_inc(sem["knd"], 1)
            v.wait_ge(sem["knd"], 1)
            v.tensor_reduce(kss[:], flat(k2[:]), AX.X, ALU.add).then_inc(sem["knd"], 1)
            v.wait_ge(sem["knd"], 2)
            v.tensor_scalar(kms[:], kss[:], 1.0 / HD, EPS, ALU.mult, ALU.add).then_inc(sem["knd"], 1)
            gq = grow[:, 0, :].rearrange("p (d e) -> p d e", e=2)
            for c, (e, t) in enumerate(((0, 0), (1, 1), (0, 1), (1, 0))):
                link(v.tensor_tensor(qtab[:, :, c, :], tab[:, :, t, :],
                                     gq[:, :, e].unsqueeze(1).broadcast_to([P, NT - 1, HD // 2]), ALU.mult))
            v.wait_ge(sem["kpow"], 1)
            link(v.tensor_tensor(flat(kn[:]), flat(kn[:]), wide(krs[:], NT * KV), ALU.mult))
            link(v.tensor_tensor(flat(kn[:]), flat(kn[:]), grow[:, 1, :].unsqueeze(1).broadcast_to([P, NT * KV, HD]), ALU.mult))
            v.sem_inc(sem["kpow"], 2)
            x = kn[:, 1:].rearrange("p t h (d e) -> p t h d e", e=2)
            o = kr[:, 0:8].rearrange("p t h (d e) -> p t h d e", e=2)
            w = lambda c: tab[:, :, c, :].unsqueeze(2).broadcast_to([P, NT - 1, KV, HD // 2])
            for e in range(2):
                link(v.tensor_tensor(r1[:], x[:, :, :, :, 0], w(e), ALU.mult))
                link(v.tensor_tensor(r2[:], x[:, :, :, :, 1], w(1 - e), ALU.mult))
                link(v.tensor_tensor(o[:, :, :, :, e], r1[:], r2[:], ALU.subtract if e == 0 else ALU.add))
            link(v.tensor_copy(kr[:, 9], kn[:, 0]))
            for a in range(2):
                link(v.tensor_copy(flat(kpart[0][:, :, :, a, :]), flat(kr[:])))
            v.tensor_tensor(flat(kpart[1][:, :, :, 0, :]), flat(kr[:]), flat(kpart[0][:, :, :, 0, :].bitcast(F32)),
                            ALU.subtract).then_inc(sem["knd"], 1)
            v.tensor_tensor(flat(kpart[1][:, :, :, 1, :]), flat(kr[:]), flat(kpart[0][:, :, :, 1, :].bitcast(F32)),
                            ALU.subtract).then_inc(sem["knd"], 1)

            def norm_a(n):
                v.wait_ge(sem["qload"], 16 * n + 16)
                v.tensor_tensor(q2[:], q[:], q[:], ALU.mult).then_inc(sem["qd"], 1)
                v.wait_ge(sem["qd"], 4 * n + 1)
                v.tensor_reduce(qss[:], q2[:], AX.X, ALU.add).then_inc(sem["qd"], 1)
                v.wait_ge(sem["qd"], 4 * n + 2)
                v.tensor_scalar(qms[:], qss[:], 1.0 / HD, EPS, ALU.mult, ALU.add).then_inc(sem["qd"], 1)

            def norm_b(n, table):
                v.wait_ge(sem["qpow"], n + 1)
                if table is not None:
                    v.tensor_copy(qtb[:], table)
                v.tensor_tensor(qn[:], q[:], wide(qrs[:], AH), ALU.mult).then_inc(sem["qd"], 1)

            def split(x, done, n):
                v.tensor_copy(qpart[:, :, 0, :], x).then_inc(sem["dve"], 1)
                link.n += 1
                v.wait_ge(sem["dve"], link.value())
                v.tensor_tensor(qpart[:, :, 1, :], x, qpart[:, :, 0, :].bitcast(F32), ALU.subtract).then_inc(done, 1)

            norm_a(0)
            norm_b(0, None)
            v.wait_ge(sem["qd"], 4)
            link(v.tensor_tensor(qr[:], qn[:], grow[:, 0, :].unsqueeze(1).broadcast_to([P, AH, HD]), ALU.mult))
            split(qr[:], sem["cpart"], 0)
            v.wait_ge(sem["csmm"], 1)
            c4 = lambda b: ps[:, b:b + 2, :].rearrange("p a (h n) -> p (a h) n", h=4)
            link(v.tensor_reduce(mxc[:], c4(2), AX.X, ALU.max))
            v.tensor_scalar(mxc[:], mxc[:], -QS, None, ALU.mult).then_inc(sem["cmx"], 1)
            norm_a(1)
            norm_b(1, qtab[:, 0])
            v.wait_ge(sem["comm"], 1)
            oc = ps[:, 6:8, 0:4 * H1].rearrange("p a (h n) -> p a h n", h=4)
            r4 = rsc[:].rearrange("p (a h) -> p a h", a=2)
            link(v.reciprocal(r4, oc[:, :, :, HD]))
            for a in range(2):
                ins = v.tensor_tensor(y[:, 4 * a:4 * a + 4, :], oc[:, a, :, 0:HD], r4[:, a].unsqueeze(2).broadcast_to([P, 4, HD]),
                                      ALU.mult)
            ins.then_inc(sem["cdone"], 1)
            v.wait_ge(sem["rope"], 6)
            v.wait_ge(sem["qtm"], 1)
            split(qr[:], sem["qpart"], 1)
            v.sem_inc(sem["on"], 1)

            def peak(nh, h):
                v.wait_ge(sem["smm"], nh + 1)
                link(v.tensor_reduce(mx[:, h % 2:h % 2 + 1], ps[:, SB[h % 2], 0:TH], AX.XY, ALU.max))
                v.tensor_scalar(nm[:, h % 2:h % 2 + 1], mx[:, h % 2:h % 2 + 1], -QS, None, ALU.mult).then_inc(sem["mx"], 1)

            def normed(i, h):
                v.wait_ge(sem["omm"], 8 * i + h + 1)
                o = ps[:, OB, 0:H1]
                link(v.reciprocal(rs[:, h % 2:h % 2 + 1], o[:, HD:H1]))
                v.tensor_scalar(y[:, h, :], o[:, 0:HD], rs[:, h % 2:h % 2 + 1], None, ALU.mult).then_inc(sem["on"], 1)

            def tile(i, more):
                for h in range(AH):
                    for n in (0, 2):
                        k = use(h, n)
                        v.wait_ge(sem["ptm"], USES * i + k + 1)
                        v.tensor_copy(pt[h % 2][:, n * TH:n * TH + TH], ps[:, PT, 0:TH]).then_inc(sem["pte"], 1)
                        if n == 0:
                            if h < 6 or more:
                                peak(8 * i + h + 2, h)
                    if h:
                        normed(i, h - 1)
                    if more:
                        if h == 0:
                            norm_a(i + 2)
                        if h == 2:
                            norm_b(i + 2, qtab[:, bass.ds(i + 1, 1)].rearrange("p a c d -> p (a c) d"))
                        if h == 4:
                            v.wait_ge(sem["rope"], 6 * i + 12)
                            v.wait_ge(sem["ptm"], USES * i + use(4, 0) + 1)
                            split(qr[:], sem["qpart"], 1)
                normed(i, AH - 1)

            peak(0, 0)
            peak(1, 1)
            with v.Fori(0, 7) as i:
                link.loop(i, 8 + 8 + 1)
                tile(i, True)
            link.end(7)
            tile(7, False)


def merge(nc, g):
    io, ps = g.io, g.ps
    KB = 4
    with Phase(nc, "mrg") as ph:
        y = ph.sb("y", [P, KB, T])
        ys = [ph.sb(f"ys{n}", [P, KB, T], F32R) for n in ("hi", "lo")]
        raw = [ph.sb(f"raw{i}", [P, KB * 512]) for i in range(2)]
        w = [[ph.sb(f"w{n}{i}", [P, KB * 512], F32R) for i in range(2)] for n in ("hi", "lo")]
        bg = [ph.sb(f"bg{i}", [P, T]) for i in range(4)]
        part = [ph.sb(f"part{i}", [P, T]) for i in range(2)]
        y_in = ph.sem("y_in")
        w_in = [ph.sem(f"w_in{i}") for i in range(2)]
        bg_in = [ph.sem(f"bg_in{i}") for i in range(4)]
        y_hi, y_lo = ph.sem("y_hi"), ph.sem("y_lo")
        w_hi, w_lo = ph.sem("w_hi"), ph.sem("w_lo")
        mm_done = ph.sem("mm_done")
        taken = ph.sem("taken")
        bg_used = ph.sem("bg_used")
        dve = ph.sem("dve")
        NB = 3
        block = ph.block()

        @block.sync
        def _(sp):
            for n in range(NB):
                if n:
                    sp.wait_ge(y_lo, KB * n)
                sp.dma_start(y[:], g.y_dram[n * 512:n * 512 + 512, :].rearrange("(k p) t -> p k t", p=P)).then_inc(y_in, 16)
                for s in range(2):
                    if n:
                        sp.wait_ge(w_lo, 2 * n + s - 1)
                    sp.dma_start(raw[s][:], io["w_branch"][2 * n + s]).then_inc(w_in[s], 16)

        @block.gpsimd
        def _(gp):
            for n in range(8 * NB):
                if n >= 4:
                    gp.wait_ge(bg_used, n - 3)
                gp.dma_start(bg[n % 4][:], g.bg_dram[n * P:n * P + P, :]).then_inc(bg_in[n % 4], 16)

        @block.scalar
        def _(act):
            def weights(n, s):
                act.wait_ge(w_in[s], 16 * n + 16)
                if n:
                    act.wait_ge(mm_done, 8 * n + 4 * s - 4)
                act.activation(w[0][s][:], raw[s][:], ACT.Copy).then_inc(w_hi, 1)

            def ys_hi(n):
                act.wait_ge(y_in, 16 * n + 16)
                if n:
                    act.wait_ge(mm_done, 8 * n)
                for k in range(KB):
                    act.activation(ys[0][:, k, :], y[:, k, :], ACT.Copy).then_inc(y_hi, 1)

            ys_hi(0)
            for n in range(NB):
                for s in range(2):
                    if n + s == 0:
                        weights(0, 0)
                        weights(0, 1)
                    elif (n, s) != (NB - 1, 1):
                        m = 2 * n + s + 1
                        weights(m // 2, m % 2) if m > 1 else None
                if n < NB - 1:
                    ys_hi(n + 1)

        @block.vector
        def _(v):
            link = Chain(v, dve)
            v.sem_inc(taken, 2)

            def weights(m):
                v.wait_ge(w_hi, m + 1)
                v.tensor_tensor(w[1][m % 2][:], raw[m % 2][:], w[0][m % 2][:].bitcast(F32), ALU.subtract).then_inc(w_lo, 1)

            def ys_lo(n):
                for k in range(KB):
                    v.wait_ge(y_hi, KB * n + k + 1)
                    v.tensor_tensor(ys[1][:, k, :], y[:, k, :], ys[0][:, k, :].bitcast(F32), ALU.subtract).then_inc(y_lo, 1)

            ys_lo(0)
            weights(0)
            weights(1)
            for n in range(NB):
                for t in range(8):
                    if t == 4 and n:
                        weights(2 * n + 1)
                    m = 8 * n + t
                    v.wait_ge(mm_done, m + 1)
                    v.wait_ge(bg_in[m % 4], 16 * (m // 4) + 16)
                    into = g.merged[:, t, :]
                    dst = part[t % 2][:] if n else into
                    v.tensor_tensor(dst.rearrange("p (a n) -> p a n", a=3), ps[:, 3 * (t % 2):3 * (t % 2) + 3, 0:TH],
                                    bg[m % 4][:].rearrange("p (a n) -> p a n", a=3), ALU.mult).then_inc(taken, 1)
                    v.wait_ge(taken, m + 3)
                    v.sem_inc(bg_used, 1)
                    if n:
                        link(v.tensor_tensor(into, into, part[t % 2][:], ALU.add))
                if n < NB - 1:
                    ys_lo(n + 1)
                    weights(2 * n + 2)

        @block.tensor
        def _(pe):
            with pe.Fori(0, NB) as n:
                for t in range(8):
                    s = t // 4
                    if t == 0:
                        pe.wait_ge(y_lo, KB * n + KB)
                    if t % 4 == 0:
                        pe.wait_ge(w_lo, 2 * n + s + 1)
                    pe.wait_ge(taken, 8 * n + t + 1)
                    ws = [x[s][:].rearrange("p (k n) -> p k n", k=KB) for x in w]
                    for c in range(3):
                        for k in range(KB):
                            mm = three_passes(pe, ps[:, 3 * (t % 2) + c, 0:TH], [x[:, k, t % 4 * P:t % 4 * P + P] for x in ws],
                                              [x[:, k, c * TH:(c + 1) * TH] for x in ys], k == 0, k == KB - 1)
                    mm.then_inc(mm_done, 1)


def out_norm(nc, g):
    io, ps = g.io, g.ps
    with Phase(nc, "out") as ph:
        raw = [ph.sb(f"raw{i}", [P, D]) for i in range(4)]
        w = [ph.sb(f"w{n}", [P, KD, D], F32R) for n in ("hi", "lo")]
        g1 = ph.sb("g1", [P, 2, D])
        free = g.merged[:].rearrange("p k t -> p (k t)")
        xin, x1, xs, hm = ([free[:, (2 * n + i) * D:(2 * n + i + 1) * D] for i in range(2)] for n in range(4))
        hm = [x.rearrange("p (k n) -> p k n", k=KD) for x in hm]
        junk = free[:, 8 * D:9 * D]
        m_hi, m_lo = ph.sem("m_hi"), ph.sem("m_lo")
        ss, ms, rstd = (ph.sb(n, [P, NT]) for n in ("ss", "ms", "rstd"))
        half = ph.sb("half", [P, 1])
        w_in = [ph.sem(f"w_in{i}") for i in range(4)]
        x_in = [ph.sem(f"x_in{i}") for i in range(2)]
        x_out = [ph.sem(f"x_out{i}") for i in range(2)]
        g_in = ph.sem("g_in")
        w_hi, w_lo = ph.sem("w_hi"), ph.sem("w_lo")
        mm_done, gated, x1_done, squared = ph.sem("mm_done"), ph.sem("gated"), ph.sem("x1_done"), ph.sem("squared")
        pool, rstd_done, xs_done = ph.sem("pool"), ph.sem("rstd_done"), ph.sem("xs_done")
        turned, scaled, h_full, h_hi, h_lo = (ph.sem(n) for n in ("turned", "scaled", "h_full", "h_hi", "h_lo"))
        block = ph.block()

        @block.sync
        def _(sp):
            for who in range(2):
                sp.dma_start(g1[:, who, :], g.gate_rows[who, 0:D].partition_broadcast(P)).then_inc(g_in, 16)
            for k in range(KD):
                if k >= 4:
                    sp.wait_ge(w_lo, k - 3)
                sp.dma_start(raw[k % 4][:], io["w_out"][k * P:k * P + P, :]).then_inc(w_in[k % 4], 16)
            sp.wait_ge(m_lo, KD)
            sp.dma_start(xin[0][:], io["x_prompt"]).then_inc(x_in[0], 16)
            for i in range(1, NT):
                if i >= 2:
                    sp.wait_ge(x1_done, i - 1)
                sp.dma_start(xin[i % 2][:], io["x_sample"][i * P - P:i * P, :]).then_inc(x_in[i % 2], 16)

        @block.gpsimd
        def _(gp):
            gp.memset(half[:], -0.5).then_inc(pool, 1)
            for i in range(NT):
                gp.wait_ge(squared, i + 1)
                gp.tensor_scalar(ms[:, i:i + 1], ss[:, i:i + 1], 1.0 / D, EPS, ALU.mult, ALU.add).then_inc(pool, 1)
                gp.wait_ge(pool, i + 2)
                gp.tensor_tensor(rstd[:, i:i + 1], ms[:, i:i + 1], half[:], ALU.pow).then_inc(rstd_done, 1)

        @block.scalar
        def _(act):
            def square(i):
                act.wait_ge(x1_done, i + 1)
                act.dma_start(g.x1_dram[i * P:i * P + P, :], x1[i % 2][:]).then_inc(x_out[i % 2], 16)
                if i:
                    act.wait_ge(squared, i)
                act.activation(junk[:], x1[i % 2][:], ACT.Square, accum_out=ss[:, i:i + 1]).then_inc(squared, 1)
                act.wait_ge(rstd_done, i + 1)
                if i >= 2:
                    act.wait_ge(turned, i - 1)
                act.activation(xs[i % 2][:], x1[i % 2][:], ACT.Copy, scale=rstd[:, i:i + 1]).then_inc(xs_done, 1)

            def split(i):
                act.wait_ge(h_full, i + 1)
                act.activation(g.h[0][:, :, i * P:i * P + P], hm[i % 2][:], ACT.Copy).then_inc(h_hi, 1)

            for k in range(KD):
                act.activation(g.h[0][:, k, :], g.merged[:, k, :], ACT.Copy).then_inc(m_hi, 1)
                act.wait_ge(w_in[k % 4], 16 * (k // 4) + 16)
                act.activation(w[0][:, k, :], raw[k % 4][:], ACT.Copy).then_inc(w_hi, 1)
            for i in range(NT):
                square(i)
                if i:
                    split(i - 1)
            split(NT - 1)
            act.wait_ge(x_out[0], 16 * 5)
            act.wait_ge(x_out[1], 16 * 4)

        @block.vector
        def _(v):
            for k in range(KD):
                v.wait_ge(m_hi, k + 1)
                v.tensor_tensor(g.h[1][:, k, :], g.merged[:, k, :], g.h[0][:, k, :].bitcast(F32), ALU.subtract).then_inc(m_lo, 1)
                v.wait_ge(w_hi, k + 1)
                v.tensor_tensor(w[1][:, k, :], raw[k % 4][:], w[0][:, k, :].bitcast(F32), ALU.subtract).then_inc(w_lo, 1)
            v.wait_ge(g_in, 32)
            v.wait_ge(m_lo, KD)

            def residual(i):
                who = min(i, 1)
                v.wait_ge(mm_done, i + 1)
                if i >= 2:
                    v.wait_ge(x_out[i % 2], 16 * (i // 2))
                    v.wait_ge(xs_done, i - 1)
                v.tensor_tensor(x1[i % 2][:].rearrange("p (a n) -> p a n", a=2), ps[:, 2 * (i % 2):2 * (i % 2) + 2, :],
                                g1[:, who, :].rearrange("p (a n) -> p a n", a=2), ALU.mult).then_inc(gated, 1)
                v.wait_ge(gated, i + 1)
                v.wait_ge(x_in[i % 2], 16 * (i // 2) + 16)
                v.tensor_tensor(x1[i % 2][:], x1[i % 2][:], xin[i % 2][:], ALU.add).then_inc(x1_done, 1)

            def modulated(i):
                who = min(i, 1)
                col = lambda c: g.mod[:, c, :, who:who + 1].broadcast_to([P, KD, P])
                if i >= 2:
                    v.wait_ge(h_lo, i - 1)
                v.wait_ge(turned, i + 1)
                v.tensor_tensor(hm[i % 2][:], ps[:, 4 + 2 * (i % 2):6 + 2 * (i % 2), :].rearrange("p a (k n) -> p (a k) n", n=P),
                                col(2), ALU.mult).then_inc(scaled, 1)
                v.wait_ge(scaled, i + 1)
                v.tensor_tensor(hm[i % 2][:], hm[i % 2][:], col(3), ALU.add).then_inc(h_full, 1)

            def split(i):
                v.wait_ge(h_hi, i + 1)
                v.tensor_tensor(g.h[1][:, :, i * P:i * P + P], hm[i % 2][:], g.h[0][:, :, i * P:i * P + P].bitcast(F32),
                                ALU.subtract).then_inc(h_lo, 1)

            for i in range(NT):
                residual(i)
                if i >= 1:
                    modulated(i - 1)
                if i >= 2:
                    split(i - 2)
            split(NT - 2)
            modulated(NT - 1)
            split(NT - 1)

        @block.tensor
        def _(pe):
            def turn(i):
                pe.wait_ge(xs_done, i + 1)
                if i >= 2:
                    pe.wait_ge(scaled, i - 1)
                for k in range(KD):
                    mm = pe.transpose(ps[:, 4 + 2 * (i % 2) + k // 4, k % 4 * P:k % 4 * P + P], xs[i % 2][:, k * P:k * P + P],
                                      g.ident[:])
                mm.then_inc(turned, 1)

            for i in range(NT):
                if i >= 2:
                    pe.wait_ge(gated, i - 1)
                for k in range(KD):
                    if i == 0:
                        pe.wait_ge(m_lo, k + 1)
                        pe.wait_ge(w_lo, k + 1)
                    for n in range(2):
                        mm = three_passes(pe, ps[:, 2 * (i % 2) + n, :], [x[:, k, i * P:i * P + P] for x in g.h],
                                          [x[:, k, 512 * n:512 * n + 512] for x in w], k == 0, k == KD - 1)
                mm.then_inc(mm_done, 1)
                if i:
                    turn(i - 1)
            turn(NT - 1)


def ffn(nc, g):
    io, ps = g.io, g.ps
    with Phase(nc, "ffn") as ph:
        raw = [ph.sb(f"raw{i}", [P, UNIT]) for i in range(2)]
        w = [[ph.sb(f"w{n}{i}", [P, KD, HALF], F32R) for i in range(2)] for n in ("hi", "lo")]
        oraw = [ph.sb(f"oraw{i}", [P, D]) for i in range(2)]
        ow = [[ph.sb(f"ow{n}{i}", [P, D], F32R) for i in range(2)] for n in ("hi", "lo")]
        gate = ph.sb("gate", [P, T])
        a = [[ph.sb(f"a{n}{i}", [P, T], F32R) for i in range(2)] for n in ("hi", "lo")]
        w_in = [ph.sem(f"w_in{i}") for i in range(2)]
        o_in = [ph.sem(f"o_in{i}") for i in range(2)]
        w_hi, w_lo, o_hi, o_lo = (ph.sem(n) for n in ("w_hi", "w_lo", "o_hi", "o_lo"))
        gu_mm = ph.sem("gu_mm")
        silu = ph.sem("silu")
        prod = ph.sem("prod")
        a_hi, a_lo = ph.sem("a_hi"), ph.sem("a_lo")
        out_mm = ph.sem("out_mm")
        added = ph.sem("added")
        cleared = ph.sem("cleared")
        GATE, UP, OUT = 0, 3, 6
        block = ph.block()

        @block.sync
        def _(sp):
            def load(j, s, wait=True):
                if wait:
                    sp.wait_ge(w_lo, j - 1)
                sp.dma_start(raw[s][:], io["w_ffn_in"][bass.ds(j, 1)].rearrange("a p n -> (a p) n")).then_inc(w_in[s], 16)
                if wait:
                    sp.wait_ge(o_lo, j - 1)
                sp.dma_start(oraw[s][:], io["w_ffn_out"][bass.ds(j * P, P), :]).then_inc(o_in[s], 16)

            load(0, 0, False)
            load(1, 1, False)
            with sp.Fori(0, NH // 2 - 1) as i:
                for s in range(2):
                    load(2 * i + s + 2, s)

        @block.gpsimd
        def _(gp):
            gp.memset(g.acc, 0.0).then_inc(cleared, 1)

        def times(j, s):
            return 8 * j + 16 - 8 * s

        @block.scalar
        def _(act):
            act.sem_inc(silu, 3)

            def w_split(j, s, wait=True):
                act.wait_ge(w_in[s], times(j, s))
                if wait:
                    act.wait_ge(gu_mm, 6 * j - 6)
                act.activation(w[0][s][:].rearrange("p k n -> p (k n)"), raw[s][:], ACT.Copy).then_inc(w_hi, 1)

            def step(j, s, first=False, last=False):
                if not last:
                    w_split(j + 1, 1 - s, not first)
                for t in range(3):
                    act.wait_ge(gu_mm, 6 * j + t + 1)
                    if not first:
                        act.wait_ge(a_lo, 3 * j + t - 2)
                    act.activation(gate[:, t * TH:t * TH + TH], ps[:, GATE + t, 0:TH], ACT.Silu).then_inc(silu, 1)
                    if t == 0:
                        act.wait_ge(o_in[s], times(j, s))
                        if not first:
                            act.wait_ge(added, 18 * j - 16)
                        act.activation(ow[0][s][:], oraw[s][:], ACT.Copy).then_inc(o_hi, 1)
                for t in range(3):
                    act.wait_ge(prod, 3 * j + t + 4)
                    act.activation(a[0][s][:, t * TH:t * TH + TH], gate[:, t * TH:t * TH + TH], ACT.Copy).then_inc(a_hi, 1)

            w_split(0, 0, False)
            step(0, 0, first=True)
            with act.Fori(0, NH // 2 - 1) as i:
                for s in range(2):
                    step(2 * i + 1 + s, 1 - s)
            step(NH - 1, 1, last=True)

        @block.vector
        def _(v):
            v.sem_inc(prod, 3)
            v.sem_inc(added, 2)

            def w_split(j, s):
                v.wait_ge(w_hi, j + 1)
                v.tensor_tensor(w[1][s][:].rearrange("p k n -> p (k n)"), raw[s][:],
                                w[0][s][:].rearrange("p k n -> p (k n)").bitcast(F32), ALU.subtract).then_inc(w_lo, 1)

            def add(j, us):
                for u in us:
                    dst = g.acc[:, u // 2, u % 2 * 512:u % 2 * 512 + 512]
                    v.wait_ge(out_mm, 18 * j + u + 1)
                    v.tensor_tensor(dst, dst, ps[:, OUT + u % 2, :], ALU.add).then_inc(added, 1)

            def times_up(j, t):
                r = slice(t * TH, t * TH + TH)
                v.wait_ge(gu_mm, 6 * j + t + 4)
                v.wait_ge(silu, 3 * j + t + 4)
                v.tensor_tensor(gate[:, r], gate[:, r], ps[:, UP + t, 0:TH], ALU.mult).then_inc(prod, 1)

            def a_split(j, s, t):
                r = slice(t * TH, t * TH + TH)
                v.wait_ge(a_hi, 3 * j + t + 1)
                v.tensor_tensor(a[1][s][:, r], gate[:, r], a[0][s][:, r].bitcast(F32), ALU.subtract).then_inc(a_lo, 1)

            def step(j, s, first=False, last=False):
                if not first:
                    add(j - 1, range(0, 3))
                if not last:
                    w_split(j + 1, 1 - s)
                if not first:
                    add(j - 1, range(3, 6))
                v.wait_ge(o_hi, j + 1)
                v.tensor_tensor(ow[1][s][:], oraw[s][:], ow[0][s][:].bitcast(F32), ALU.subtract).then_inc(o_lo, 1)
                if not first:
                    add(j - 1, range(6, 9))
                for t in range(3):
                    times_up(j, t)
                    if not first:
                        add(j - 1, range(9 + 3 * t, 12 + 3 * t))
                    a_split(j, s, t)

            w_split(0, 0)
            v.wait_ge(cleared, 1)
            step(0, 0, first=True)
            with v.Fori(0, NH // 2 - 1) as i:
                for s in range(2):
                    step(2 * i + 1 + s, 1 - s)
            step(NH - 1, 1, last=True)
            add(NH - 1, range(18))

        @block.tensor
        def _(pe):
            def out(j, s, us):
                for u in us:
                    tile = u // 2
                    if u == 0:
                        pe.wait_ge(o_lo, j + 1)
                    if u % 6 == 0:
                        pe.wait_ge(a_lo, 3 * j + u // 6 + 1)
                    pe.wait_ge(added, 18 * j + u + 1)
                    three_passes(pe, ps[:, OUT + u % 2, :], [x[s][:, tile * P:tile * P + P] for x in a],
                                 [x[s][:, u % 2 * 512:u % 2 * 512 + 512] for x in ow], True, True).then_inc(out_mm, 1)

            def step(j, s, first=False):
                pe.wait_ge(w_lo, j + 1)
                for n in range(6):
                    t = n % 3
                    pe.wait_ge(silu if n < 3 else prod, 3 * j + t + 1)
                    for k in range(KD):
                        mm = three_passes(pe, ps[:, (GATE if n < 3 else UP) + t, 0:TH],
                                          [x[s][:, k, n // 3 * P:n // 3 * P + P] for x in w],
                                          [x[:, k, t * TH:t * TH + TH] for x in g.h], k == 0, k == KD - 1)
                    mm.then_inc(gu_mm, 1)
                    if not first:
                        out(j - 1, 1 - s, range(3 * n, 3 * n + 3))

            step(0, 0, first=True)
            with pe.Fori(0, NH // 2 - 1) as i:
                for s in range(2):
                    step(2 * i + 1 + s, 1 - s)
            step(NH - 1, 1)
            out(NH - 1, 1, range(18))


def finish(nc, g):
    io = g.io
    with Phase(nc, "fin") as ph:
        g2 = ph.sb("g2", [P, 2, D])
        fg = ph.sb("fg", [P, D])
        x1 = ph.sb("x1", [P, NT, D])
        out = [ph.sb(f"out{i}", [P, D]) for i in range(3)]
        junk = ph.sb("junk", [P, D])
        ss, ms, rstd = (ph.sb(n, [P, NT]) for n in ("ss", "ms", "rstd"))
        half = ph.sb("half", [P, 1])
        g_in, x_in, y_out = ph.sem("g_in"), [ph.sem(f"x_in{i}") for i in range(3)], ph.sem("y_out")
        gated, summed, squared, pool, rstd_done, y_done = (ph.sem(n) for n in ("gated", "summed", "squared", "pool",
                                                                             "rstd_done", "y_done"))
        y_outs = [ph.sem(f"y_out{i}") for i in range(3)]
        block = ph.block()

        @block.sync
        def _(sp):
            for who in range(2):
                sp.dma_start(g2[:, who, :], g.gate_rows[who, D:2 * D].partition_broadcast(P)).then_inc(g_in, 16)
            for n in range(3):
                sp.dma_start(x1[:, 3 * n:3 * n + 3, :],
                             g.x1_dram[3 * n * P:3 * (n + 1) * P, :].rearrange("(t p) d -> p t d", p=P)).then_inc(x_in[n], 16)
            sp.dma_start(fg[:], io["final_g"].partition_broadcast(P)).then_inc(g_in, 16)
            for i in range(NT):
                sp.wait_ge(y_done, i + 1)
                dst = g.outs["y_sample"][i * P - P:i * P, :] if i else g.outs["y_prompt"]
                sp.dma_start(dst, out[i % 3][:]).then_inc(y_outs[i % 3], 16)
            for s in y_outs:
                sp.wait_ge(s, 48)

        @block.gpsimd
        def _(gp):
            gp.memset(half[:], -0.5).then_inc(pool, 1)
            for i in range(NT):
                gp.wait_ge(squared, i + 1)
                gp.tensor_scalar(ms[:, i:i + 1], ss[:, i:i + 1], 1.0 / D, EPS, ALU.mult, ALU.add).then_inc(pool, 1)
                gp.wait_ge(pool, i + 2)
                gp.tensor_tensor(rstd[:, i:i + 1], ms[:, i:i + 1], half[:], ALU.pow).then_inc(rstd_done, 1)

        @block.scalar
        def _(act):
            for i in range(NT):
                act.wait_ge(summed, i + 1)
                if i:
                    act.wait_ge(squared, i)
                act.activation(junk[:], x1[:, i, :], ACT.Square, accum_out=ss[:, i:i + 1]).then_inc(squared, 1)

        @block.vector
        def _(v):
            def total(i):
                v.tensor_tensor(g.acc[:, i, :], g.acc[:, i, :], g2[:, min(i, 1), :], ALU.mult).then_inc(gated, 1)
                v.wait_ge(x_in[i // 3], 16)
                v.wait_ge(gated, i + 1)
                v.tensor_tensor(x1[:, i, :], x1[:, i, :], g.acc[:, i, :], ALU.add).then_inc(summed, 1)

            v.wait_ge(g_in, 48)
            total(0)
            total(1)
            for i in range(NT):
                if i + 2 < NT:
                    total(i + 2)
                v.wait_ge(rstd_done, i + 1)
                if i >= 3:
                    v.wait_ge(y_outs[i % 3], 16 * (i // 3))
                v.scalar_tensor_tensor(out=out[i % 3][:], in0=x1[:, i, :], scalar=rstd[:, i:i + 1], in1=fg[:],
                                       op0=ALU.mult, op1=ALU.mult).then_inc(y_done, 1)


OUTS = [("y_prompt", [CTX, D]), ("y_sample", [LAT, D]), ("k", [CTX, KV * HD]), ("v", [CTX, KV * HD]),
        ("ml_s", [2, HEADS * P, DK + 1]), ("ml_m", [HEADS, 2]), ("hg_s", [2, HEADS * P, DK])]


def build(nc, io, outs):
    with ExitStack() as stack:
        g = Core()
        g.io, g.outs = io, outs
        dram = lambda name, shape: nc.dram_tensor(name, shape, F32).ap()
        g.gate_rows = dram("gate_rows", [2, 2 * D])
        g.tok_dram = dram("tok_dram", [T, TW])
        g.feat_dram = dram("feat_dram", [NFQ * HALF, T])
        g.bg_dram = dram("bg_dram", [NBG * HALF, T])
        g.gate_dram = dram("gate_dram", [HEADS, 10, T])
        g.decay_dram = dram("decay_dram", [HEADS, 2 * NT])
        g.y_dram = dram("y_dram", [3 * 4 * P, T])
        g.x1_dram = dram("x1_dram", [T, D])
        sb = lambda n, s, d=F32: stack.enter_context(nc.sbuf_tensor(n, s, d))
        g.ps = stack.enter_context(nc.psum_tensor("ps", [P, 8, 512], F32))
        g.ident = sb("ident", [P, P])
        g.mod = sb("mod", [P, 4, KD, 2])

        def operand(hs, name):
            return [hs.enter_context(nc.sbuf_tensor(f"{name}_{n}", [P, KD, T], F32R)) for n in ("hi", "lo")]

        with ExitStack() as hs:
            g.h = operand(hs, "h")
            modulate(nc, g)
            project(nc, g)
        gate_rows(nc, g)
        mlstm(nc, g)
        hgrn(nc, g)
        attention(nc, g)
        g.merged = sb("merged", [P, KD, T])
        merge(nc, g)
        g.h = operand(stack, "h2")
        out_norm(nc, g)
        g.acc = g.merged[:].rearrange("p k t -> p (k t)").rearrange("p (t d) -> p t d", d=D)
        ffn(nc, g)
        finish(nc, g)


def units(a, width):
    k, n = a.shape
    return np.ascontiguousarray(a.reshape(k // P, P, n // width, width).transpose(2, 1, 0, 3)
                                .reshape(n // width, P, k // P * width))


def lay_out(i):
    w_in = np.asarray(i["w_in"])[0]
    o = {}
    at = {}
    pos = 0
    for name, n in (("mq", 512), ("mk", 512), ("mv", 512), ("mo", 512), ("mg", 16), ("hq", 512), ("hf", 1024),
                    ("hi", 512), ("hg", 512), ("aq", 512), ("ak", 128), ("av", 128), ("bg", 3072)):
        at[name] = w_in[:, pos:pos + n]
        pos += n
    aq = at["aq"].reshape(D, KV, AH // KV, HD).transpose(0, 2, 1, 3).reshape(D, AH * HD)
    tok = np.concatenate([at["mv"], at["mo"], at["hi"], at["hg"], aq], axis=1)
    wt = tok.reshape(2, 4, P, NTB, 512).transpose(3, 0, 2, 1, 4).reshape(2 * NTB, P, UNIT)
    last = np.concatenate([at["ak"], at["av"], at["mg"]], axis=1)
    feat = np.concatenate([at["mq"], at["mk"], at["hq"], at["hf"], at["bg"]], axis=1)
    o["w_tok"] = np.ascontiguousarray(wt)
    o["w_tok_last"] = units(last, TLAST)[0]
    o["w_feat"] = units(feat, HALF)
    wa = np.asarray(i["w_ada"])[0].reshape(D, 6, D)
    wa = np.concatenate([wa[:, 0:2], wa[:, 3:5], wa[:, 2:3], wa[:, 5:6]], axis=1).reshape(D, 6 * D)
    o["w_ada"] = units(wa, 512).reshape(12, P, KD, 512)
    o["b_ada"] = np.asarray(i["b_ada"])[0]
    o["norm1_g"] = np.asarray(i["norm1_g"])[0]
    o["norm2_g"] = np.asarray(i["norm2_g"])[0]
    o["c"] = np.asarray(i["c"])[0]
    o["c_ctx"] = np.asarray(i["c_ctx"])
    o["x_prompt"] = np.asarray(i["x_prompt"])[0]
    o["x_sample"] = np.asarray(i["x_sample"])[0]
    o["ml_gate_b"] = np.asarray(i["ml_gate_b"])[0].transpose(2, 0, 1).reshape(HEADS, 4)
    o["ml_m0"] = np.asarray(i["state_ml_m"])[0, 0].T
    o["ml_s0"] = np.concatenate([np.asarray(i["state_ml_C"])[0, 0], np.asarray(i["state_ml_n"])[0, 0][..., None]],
                                axis=-1).reshape(2, HEADS * P, DK + 1)
    o["cache_k"] = np.asarray(i["cache_k"])[0, 0].reshape(PAST, KV * HD)
    o["cache_v"] = np.asarray(i["cache_v"])[0, 0].reshape(PAST, KV * HD)
    o["qk_g"] = np.concatenate([np.asarray(i["q_norm_g"])[0], np.asarray(i["k_norm_g"])[0]])
    pos = np.arange(LAT)
    inv = (np.float32(ROPE_THETA) ** (-np.arange(HD // 4, dtype=np.float32) / np.float32(HD // 4))).astype(np.float32)
    ang = np.concatenate([(pos // GRID_W).astype(np.float32)[:, None] * inv,
                          (pos % GRID_W).astype(np.float32)[:, None] * inv], axis=-1)
    o["rope"] = np.stack([np.cos(ang), np.sin(ang)], axis=1).astype(np.float32).reshape(LAT // P, P, 2, HD // 2) \
        .transpose(1, 0, 2, 3)
    o["hg_s0"] = np.asarray(i["state_hg_S"])[0, 0].reshape(2, HEADS * P, DK)
    o["hg_g"] = np.asarray(i["hg_norm_g"])[0][:, None]
    key, query = np.arange(P)[:, None] % 32, np.arange(32)[None, :]
    masks = [key == query] * 2
    for l in range(1, 6):
        same = (key >> l) == (query >> l)
        kh, qh = (key >> (l - 1)) & 1, (query >> (l - 1)) & 1
        masks += [same & (kh == 0) & (qh == 1), same & (kh == 1) & (qh == 0)]
    o["hg_mask"] = np.stack(masks, axis=1).astype(np.int32)
    wb = np.asarray(i["w_branch"])[0]
    wb = np.stack([wb[0], wb[1], wb[2].reshape(KV, AH // KV, HD, D).transpose(1, 0, 2, 3).reshape(AH * HD, D)])
    o["w_branch"] = np.concatenate([units(x, 512) for x in wb])
    o["w_out"] = np.asarray(i["w_out"])[0]
    wf = np.asarray(i["w_ffn_in"])[0].reshape(D, 2, NH, P).transpose(0, 2, 1, 3).reshape(D, 2 * FFN)
    o["w_ffn_in"] = units(wf, HALF)
    o["w_ffn_out"] = np.asarray(i["w_ffn_out"])[0]
    o["final_g"] = np.asarray(i["final_g"])
    o["ml_g"] = np.asarray(i["ml_norm_g"])[0][:, None]
    return {k: np.ascontiguousarray(v) for k, v in o.items()}


def kernel(**inputs):
    import concourse.bacc as bacc
    from concourse.bass_utils import run_bass_kernel_spmd

    nc = bacc.Bacc("TRN2", target_bir_lowering=False, num_devices=1)
    arrays = {f"in_{name}": a for name, a in lay_out(inputs).items()}
    io = {name[3:]: nc.dram_tensor(name, a.shape, mybir.dt.from_np(a.dtype), kind="ExternalInput").ap()
          for name, a in arrays.items()}
    outs = {name: nc.dram_tensor(f"out_{name}", shape, F32, kind="ExternalOutput").ap() for name, shape in OUTS}
    build(nc, io, outs)
    r = run_bass_kernel_spmd(nc, [arrays], core_ids=[0]).results[0]
    y_prompt, y_sample, k, v, ml_s, ml_m, hg_s = (np.asarray(r[f"out_{name}"]) for name, _ in OUTS)
    kv = (1, 1, CTX, KV, HD)
    ml_s = ml_s.reshape(1, 1, 2, HEADS, DK, DK + 1)
    return (y_prompt[None], y_sample[None], k.reshape(kv), v.reshape(kv), np.ascontiguousarray(ml_s[..., :DK]),
            np.ascontiguousarray(ml_s[..., DK]), np.ascontiguousarray(ml_m.T)[None, None],
            hg_s.reshape(1, 1, 2, HEADS, DK, DK))
```

```python
from contextlib import ExitStack

import concourse.bass as bass
import numpy as np
from concourse import mybir

F32 = mybir.dt.float32
F32R = mybir.dt.float32r
I32 = mybir.dt.int32
BF16 = mybir.dt.bfloat16
ALU = mybir.AluOpType
ACT = mybir.ActivationFunctionType
AX = mybir.AxisListType

P = 128
D = 1024
KD = D // P
CTX, LAT = 128, 1024
T = CTX + LAT
NT = T // P
TH = T // 3
HEADS = 4
DK = 128
AH, KV, HD = 8, 2, 64
PAST = 128
GRID_W = 64
ROPE_THETA = 10000.0
FFN = 2816
NH = FFN // P
EPS = 1e-6
HALF = 256
UNIT = KD * HALF
NTB = 5
TLAST = 2 * P + 16
TW = NTB * 512 + TLAST
NFQ, NBG = 10, 12
C_MV, C_MO, C_HI, C_HG, C_AQ, C_AK, C_AV, C_MG = 0, 512, 1024, 1536, 2048, 2560, 2688, 2816
R_MQ, R_MK, R_HQ, R_HF = 0, 4, 8, 12
HL = ((0, 0), (0, 1), (1, 0))


def three_passes(pe, out, lhs, rhs, first, last):
    for n, (a, b) in enumerate(HL):
        mm = pe.matmul(out, lhs[a], rhs[b], start=first and n == 0, stop=last and n == 2)
    return mm


class Core:
    pass


class Phase:

    def __init__(self, nc, tag):
        self.nc, self.tag, self.stack, self.sems = nc, tag, ExitStack(), []

    def __enter__(self):
        return self

    def __exit__(self, *a):
        self.stack.__exit__(*a)
        self.nc.clear_and_free_semaphores(self.sems)
        self.nc.all_engine_barrier()

    def sb(self, name, shape, dt=F32):
        return self.stack.enter_context(self.nc.sbuf_tensor(f"{self.tag}_{name}", shape, dt))

    def sem(self, name):
        handle = self.nc.alloc_semaphore(f"{self.tag}_{name}")
        self.sems.append(handle)
        return handle

    def block(self):
        return self.stack.enter_context(self.nc.Block())


class Chain:

    def __init__(self, eng, sem):
        self.eng, self.sem, self.n = eng, sem, 0
        self.i, self.per, self.base = None, 0, 0

    def __call__(self, ins):
        ins.then_inc(self.sem, 1)
        self.n += 1
        self.eng.wait_ge(self.sem, self.value())
        return self.n

    def value(self):
        return self.base + self.n if self.i is None else self.i * self.per + self.base + self.n

    def loop(self, i, per):
        self.base, self.n, self.i, self.per = self.base + self.n, 0, i, per

    def end(self, times):
        assert self.n == self.per, (self.n, self.per)
        self.base, self.n, self.i = self.base + self.per * times, 0, None


def ada_rows(pe, g, out, w):
    for k in range(KD):
        mm = pe.matmul(out, g.sc[:, k, :], w[:, k, :], start=k == 0, stop=k == KD - 1)
    return mm


def ada_turn(pe, g, cols, b, row):
    for t in range(4):
        mm = pe.transpose(cols[:, 8 * b + 2 * t:8 * b + 2 * t + 2], row[:, t * P:t * P + P], g.ident[0:2, 0:2])
    return mm


def columns(v, link, g, cols, n, done):
    b0 = 24 * n
    bias = g.vcol[:, b0:b0 + 16].unsqueeze(2).broadcast_to([P, 16, 2])
    link(v.tensor_tensor(g.mcol[:], cols.rearrange("p (t v) -> p t v", v=2), bias, ALU.add))
    link(v.tensor_scalar(g.mcol[:, 8:16, :], g.mcol[:, 8:16, :], 1.0, None, ALU.add))
    link(v.tensor_tensor(g.mod[:, 2 * n, :, :], g.mcol[:, 8:16, :],
                         g.vcol[:, 48 + 8 * n:56 + 8 * n].unsqueeze(2).broadcast_to([P, 8, 2]), ALU.mult))
    v.tensor_copy(g.mod[:, 2 * n + 1, :, :], g.mcol[:, 0:8, :]).then_inc(done, 1)


def modulate(nc, g):
    io, ps = g.io, g.ps
    with Phase(nc, "mod") as ph:
        rows = ph.sb("rows", [80, P])
        sig = ph.sb("sig", [P, 16])
        ada = [ph.sb(f"ada{i}", [P, KD, 512]) for i in range(4)]
        xt = ph.sb("xt", [P, NT, D])
        junk = ph.sb("junk", [P, D])
        ss = ph.sb("ss", [P, NT])
        ms = ph.sb("ms", [P, NT])
        rstd = ph.sb("rstd", [P, NT])
        half = ph.sb("half", [P, NT])
        hf = [ph.sb(f"hf{i}", [P, 512]) for i in range(3)]
        arow = [ph.sb(f"arow{i}", [2, 512]) for i in range(2)]
        row_mm, row_done = ph.sem("row_mm"), ph.sem("row_done")
        rows_in = ph.sem("rows_in")
        x_in = [ph.sem(f"x_in{i}") for i in range(3)]
        ada_in = [ph.sem(f"ada_in{i}") for i in range(4)]
        vcol_mm, sig_done = ph.sem("vcol_mm"), ph.sem("sig_done")
        dve, pool, squared, rstd_done = ph.sem("dve"), ph.sem("pool"), ph.sem("squared"), ph.sem("rstd_done")
        col_mm, sc_done = ph.sem("col_mm"), ph.sem("sc_done")
        vcol_done, mod_done, xs_done = ph.sem("vcol_done"), ph.sem("mod_done"), ph.sem("xs_done")
        turned, h_full, h_split = ph.sem("turned"), ph.sem("h_full"), ph.sem("h_split")
        ident_done = ph.sem("ident_done")
        groups = [(0, 1), (1, 4), (5, 4)]
        VCOL, COLS, ROWS = ps[:, 7, 0:80], ps[:, 6, 0:32], [ps[0:2, 4, :], ps[0:2, 5, :]]
        vcol, sc = g.vcol, g.sc
        block = ph.block()

        @block.sync
        def _(sp):
            at = 0
            for src in (io["b_ada"], io["norm1_g"], io["norm2_g"], io["c_ctx"], io["c"]):
                n = src.shape[0] // P
                sp.dma_start(rows[at:at + n, :], src.rearrange("(r c) -> r c", c=P)).then_inc(rows_in, 16)
                at += n
            for b in range(4):
                sp.dma_start(ada[b][:], io["w_ada"][b]).then_inc(ada_in[b], 16)
            sp.dma_start(xt[:, 0, :], io["x_prompt"]).then_inc(x_in[0], 16)
            for i in (1, 2):
                sp.dma_start(xt[:, 4 * i - 3:4 * i + 1, :],
                             io["x_sample"][512 * i - 512:512 * i, :].rearrange("(t p) d -> p t d", p=P)).then_inc(x_in[i], 16)

        @block.gpsimd
        def _(gp):
            gp.memset(g.ident[:], 0.0).then_inc(pool, 1)
            gp.memset(half[:], -0.5).then_inc(pool, 1)
            gp.wait_ge(pool, 1)
            gp.affine_select(out=g.ident[:], in_=g.ident[:], compare_op=ALU.not_equal, fill=1.0,
                             base=0, pattern=[[-1, P]], channel_multiplier=1).then_inc(ident_done, 1)
            for n, (t0, nt) in enumerate(groups):
                gp.wait_ge(squared, t0 + nt)
                gp.tensor_scalar(ms[:, t0:t0 + nt], ss[:, t0:t0 + nt], 1.0 / D, EPS, ALU.mult, ALU.add).then_inc(pool, 1)
                gp.wait_ge(pool, 3 + n)
                gp.tensor_tensor(rstd[:, t0:t0 + nt], ms[:, t0:t0 + nt], half[:, t0:t0 + nt], ALU.pow).then_inc(rstd_done, 1)

        @block.scalar
        def _(act):
            act.wait_ge(vcol_done, 1)
            act.activation(sig[:], vcol[:, 64:80], ACT.Sigmoid).then_inc(sig_done, 1)
            for i in range(NT):
                act.wait_ge(x_in[(i + 3) // 4], 16)
                if i:
                    act.wait_ge(squared, i)
                act.activation(junk[:], xt[:, i, :], ACT.Square, accum_out=ss[:, i:i + 1]).then_inc(squared, 1)
            act.wait_ge(mod_done, 1)
            n = 0
            for gi, (t0, nt) in enumerate(groups):
                who = min(gi, 1)
                for k in range(KD):
                    act.wait_ge(turned, n + 1)
                    if n >= 3:
                        act.wait_ge(h_split, n - 2)
                    act.activation(hf[n % 3][:, 0:nt * P], ps[:, n % 6, 0:nt * P], ACT.Identity,
                                   bias=g.mod[:, 1, k, who:who + 1], scale=g.mod[:, 0, k, who:who + 1]).then_inc(h_full, 1)
                    n += 1

        @block.vector
        def _(v):
            link = Chain(v, dve)
            v.wait_ge(vcol_mm, 1)
            v.tensor_copy(vcol[:], VCOL).then_inc(vcol_done, 1)
            v.wait_ge(vcol_done, 1)
            v.wait_ge(sig_done, 1)
            v.tensor_tensor(sc[:].rearrange("p k v -> p v k"), vcol[:, 64:80].rearrange("p (v k) -> p v k", v=2),
                            sig[:].rearrange("p (v k) -> p v k", v=2), ALU.mult).then_inc(sc_done, 1)

            for b in range(4):
                if b >= 2:
                    v.wait_ge(col_mm, b - 1)
                v.wait_ge(row_mm, b + 1)
                v.tensor_copy(arow[b % 2][:], ROWS[b % 2]).then_inc(row_done, 1)
            for gi, (t0, nt) in enumerate(groups):
                v.wait_ge(rstd_done, gi + 1)
                for i in range(t0, t0 + nt):
                    v.tensor_scalar(xt[:, i, :], xt[:, i, :], rstd[:, i:i + 1], None, ALU.mult).then_inc(xs_done, 1)
            v.wait_ge(col_mm, 4)
            columns(v, link, g, COLS, 0, mod_done)
            n = 0
            for gi, (t0, nt) in enumerate(groups):
                for k in range(KD):
                    v.wait_ge(h_full, n + 1)
                    src, at = hf[n % 3][:, 0:nt * P], slice(t0 * P, (t0 + nt) * P)
                    link(v.tensor_copy(g.h[0][:, k, at], src))
                    v.tensor_tensor(g.h[1][:, k, at], src, g.h[0][:, k, at].bitcast(F32), ALU.subtract).then_inc(h_split, 1)
                    n += 1

        @block.tensor
        def _(pe):
            pe.wait_ge(ident_done, 1)
            pe.wait_ge(rows_in, 80)
            pe.transpose(VCOL, rows[:], g.ident[0:80, 0:80]).then_inc(vcol_mm, 1)
            pe.wait_ge(sc_done, 1)

            for b in range(5):
                if b < 4:
                    pe.wait_ge(ada_in[b], 16)
                    if b >= 2:
                        pe.wait_ge(row_done, b - 1)
                    ada_rows(pe, g, ROWS[b % 2], ada[b]).then_inc(row_mm, 1)
                if b:
                    pe.wait_ge(row_done, b)
                    ada_turn(pe, g, COLS, b - 1, arow[(b - 1) % 2]).then_inc(col_mm, 1)
            n = 0
            for gi, (t0, nt) in enumerate(groups):
                pe.wait_ge(xs_done, t0 + nt)
                for k in range(KD):
                    if n >= 6:
                        pe.wait_ge(h_full, n - 5)
                    for i in range(nt):
                        mm = pe.transpose(ps[:, n % 6, i * P:(i + 1) * P], xt[:, t0 + i, k * P:(k + 1) * P], g.ident[:])
                    mm.then_inc(turned, 1)
                    n += 1


def project(nc, g):
    io, ps = g.io, g.ps
    with Phase(nc, "prj") as ph:
        raw = [ph.sb(f"raw{i}", [P, KD * TLAST]) for i in range(2)]
        w = [[ph.sb(f"w{n}{i}", [P, KD * 512], F32R) for i in range(2)] for n in ("hi", "lo")]
        tst = [ph.sb(f"tst{i}", [P, 512]) for i in range(6)]
        fst = [ph.sb(f"fst{i}", [P, T]) for i in range(2)]
        raw_in = [ph.sem(f"raw_in{i}") for i in range(2)]
        hi_done = ph.sem("hi_done")
        lo_done = ph.sem("lo_done")
        blk_done = ph.sem("blk_done")
        t_mm, t_ev = ph.sem("t_mm"), ph.sem("t_ev")
        f_mm, f_ev = ph.sem("f_mm"), ph.sem("f_ev")
        t_out = [ph.sem(f"t_out{i}") for i in range(6)]
        f_out = [ph.sem(f"f_out{i}") for i in range(2)]
        TU = 2 * NTB + 1
        TB = NTB + 1
        NF = NFQ + NBG
        block = ph.block()

        def f_slot(n):
            return n % 2

        @block.sync
        def _(sp):
            def load(slot, src, width, u):
                sp.wait_ge(lo_done, u + 1)
                sp.dma_start(raw[slot][:, 0:width], src).then_inc(raw_in[slot], 16)

            with sp.Fori(0, NTB) as b:
                for s in range(2):
                    load(s, io["w_tok"][bass.ds(2 * b + s, 1)].rearrange("a p n -> (a p) n"), UNIT, 2 * b + s)
            load(0, io["w_tok_last"], KD * TLAST, TU - 1)
            with sp.Fori(0, NF // 2) as i:
                for s in range(2):
                    load((TU + s) % 2, io["w_feat"][bass.ds(2 * i + s, 1)].rearrange("a p n -> (a p) n"), UNIT, 2 * i + s + TU)

        def raw_value(u, slot):
            return 8 * u + (16 if slot == 0 else 8)

        @block.vector
        def _(v):
            v.sem_inc(lo_done, 2)

            def lo(slot, u, wslot, at, width):
                v.wait_ge(hi_done, u + 1)
                v.tensor_tensor(w[1][wslot][:, at:at + width], raw[slot][:, 0:width],
                                w[0][wslot][:, at:at + width].bitcast(F32), ALU.subtract).then_inc(lo_done, 1)

            with v.Fori(0, 2) as i:
                for s in range(4):
                    lo(s % 2, 4 * i + s, s // 2, UNIT * (s % 2), UNIT)
            for s in range(2):
                lo(s, 8 + s, 0, UNIT * s, UNIT)
            lo(0, TU - 1, 1, 0, KD * TLAST)
            with v.Fori(0, NF // 2) as i:
                for s in range(2):
                    lo((TU + s) % 2, 2 * i + s + TU, s, 0, UNIT)

        @block.scalar
        def _(act):
            act.sem_inc(t_ev, 6)
            act.sem_inc(f_ev, 2)
            for s in (*t_out, *f_out):
                act.sem_inc(s, 16)

            def hi(slot, u, blk, wslot, at, width):
                act.wait_ge(raw_in[slot], raw_value(u, slot))
                act.wait_ge(blk_done, blk + 1)
                act.activation(w[0][wslot][:, at:at + width], raw[slot][:, 0:width], ACT.Copy).then_inc(hi_done, 1)

            def hi_block(b, slot):
                for s in range(2):
                    hi(s, 2 * b + s, b, slot, UNIT * s, UNIT)

            def hi_feat(f, s):
                hi((TU + s) % 2, f + TU, f + TB, s, 0, UNIT)

            def put_tok(b, width, fn):
                for i in range(NT):
                    n = NT * b + i
                    slot = n % 6
                    act.wait_ge(t_mm, n + 1)
                    act.wait_ge(t_out[slot], 16 * (n // 6) + 16)
                    act.activation(tst[slot][:, 0:width], ps[:, slot, 0:width], fn).then_inc(t_ev, 1)
                    act.wait_ge(t_ev, n + 7)
                    act.dma_start(g.tok_dram[i * P:(i + 1) * P, 512 * b:512 * b + width], tst[slot][:, 0:width]).then_inc(t_out[slot], 16)

            def put_feat(f, s, dst, fn):
                for c in range(2):
                    act.wait_ge(f_mm, 2 * f + c + 1)
                    act.wait_ge(f_out[c], 16 * f + 16)
                    act.activation(fst[c][:].rearrange("p (a n) -> p a n", a=3), ps[:, 3 * c:3 * c + 3, 0:TH], fn).then_inc(f_ev, 1)
                    act.wait_ge(f_ev, 2 * f + c + 3)
                    act.dma_start(dst(c), fst[c][:]).then_inc(f_out[c], 16)

            hi_block(0, 0)
            for b, fn in enumerate((ACT.Copy, ACT.Sigmoid, ACT.Copy, ACT.Silu)):
                hi_block(b + 1, (b + 1) % 2)
                put_tok(b, 512, fn)
            hi(0, TU - 1, TB - 1, 1, 0, KD * TLAST)
            put_tok(4, 512, ACT.Copy)
            hi_feat(0, 0)
            put_tok(5, TLAST, ACT.Copy)
            with act.Fori(0, NFQ // 2) as i:
                for s in range(2):
                    hi_feat(2 * i + s + 1, (s + 1) % 2)
                    put_feat(2 * i + s, s, lambda c: g.feat_dram[bass.ds((2 * i + s) * HALF + c * P, P), :], ACT.Copy)
            with act.Fori(0, NBG // 2 - 1) as i:
                for s in range(2):
                    hi_feat(2 * i + s + 1 + NFQ, (s + 1) % 2)
                    put_feat(2 * i + s + NFQ, s, lambda c: g.bg_dram[bass.ds((2 * i + s) * HALF + c * P, P), :], ACT.Sigmoid)
            hi_feat(NF - 1, 1)
            put_feat(NF - 2, 0, lambda c: g.bg_dram[(NBG - 2) * HALF + c * P:(NBG - 2) * HALF + c * P + P, :], ACT.Sigmoid)
            put_feat(NF - 1, 1, lambda c: g.bg_dram[(NBG - 1) * HALF + c * P:(NBG - 1) * HALF + c * P + P, :], ACT.Sigmoid)
            for s in range(6):
                act.wait_ge(t_out[s], 16 + 16 * 9)
            for s in range(2):
                act.wait_ge(f_out[s], 16 + 16 * NF)

        @block.tensor
        def _(pe):
            pe.sem_inc(blk_done, 2)

            def tok_block(b, s, width, units):
                ws = [w[p][s][:, 0:KD * width].rearrange("p (k n) -> p k n", k=KD) for p in range(2)]
                pe.wait_ge(lo_done, units + 2)
                for i in range(NT):
                    slot = (NT * s + i) % 6
                    pe.wait_ge(t_ev, NT * b + i + 1)
                    for k in range(KD):
                        mm = three_passes(pe, ps[:, slot, 0:width], [h[:, k, i * P:(i + 1) * P] for h in g.h],
                                          [x[:, k, :] for x in ws], k == 0, k == KD - 1)
                    mm.then_inc(t_mm, 1)
                pe.wait_ge(t_mm, NT * b + NT)
                pe.sem_inc(blk_done, 1)

            with pe.Fori(0, 2) as i:
                for s in range(2):
                    tok_block(2 * i + s, s, 512, 4 * i + 2 * s + 2)
            tok_block(4, 0, 512, 10)
            tok_block(5, 1, TLAST, TU)
            pe.wait_ge(t_ev, 6 + NT * TB)
            with pe.Fori(0, NF // 2) as i:
                for s in range(2):
                    f = 2 * i + s
                    ws = [w[p][s][:, 0:UNIT].rearrange("p (k n) -> p k n", k=KD) for p in range(2)]
                    pe.wait_ge(lo_done, f + TU + 3)
                    for c in range(2):
                        pe.wait_ge(f_ev, 2 * f + c + 1)
                        for t in range(3):
                            for k in range(KD):
                                mm = three_passes(pe, ps[:, 3 * c + t, 0:TH], [x[:, k, c * P:(c + 1) * P] for x in ws],
                                                  [h[:, k, t * TH:(t + 1) * TH] for h in g.h], k == 0, k == KD - 1)
                        mm.then_inc(f_mm, 1)
                    pe.wait_ge(f_mm, 2 * f + 2)
                    pe.sem_inc(blk_done, 1)


def gate_rows(nc, g):
    io, ps = g.io, g.ps
    with Phase(nc, "gat") as ph:
        mg = ph.sb("mg", [P, NT, 16])
        bias = ph.sb("bias", [HEADS, 4])
        m0 = ph.sb("m0", [HEADS, 2])
        gi = ph.sb("gi", [HEADS, 2, T])
        gf = ph.sb("gf", [HEADS, 2, T])
        ab = ph.sb("ab", [HEADS, 2, T])
        mn = ph.sb("mn", [HEADS, 2, T])
        cum = ph.sb("cum", [HEADS, 2, T])
        m = ph.sb("m", [HEADS, 2, T])
        keep = ph.sb("keep", [HEADS, 2, T])
        mp = ph.sb("mp", [HEADS, 2, NT])
        ue = ph.sb("ue", [HEADS, 2, NT])
        rows = ph.sb("rows", [HEADS, 10, T])
        dec = ph.sb("dec", [HEADS, 2, NT])
        mlast = ph.sb("mlast", [HEADS, 2])
        gin, turned, taken, dve, lns = ph.sem("gin"), ph.sem("turned"), ph.sem("taken"), ph.sem("dve"), ph.sem("lns")
        absd, rows_done, gout, kept = ph.sem("absd"), ph.sem("rows_done"), ph.sem("gout"), ph.sem("kept")
        ada = [ph.sb(f"ada{i}", [P, KD, 512]) for i in range(4)]
        arow = [ph.sb(f"arow{i}", [2, 512]) for i in range(2)]
        brow = ph.sb("brow", [2, 2048])
        grow = ph.sb("grow", [2, 2048])
        ada_in = [ph.sem(f"ada_in{i}") for i in range(4)]
        row_done, col_mm = ph.sem("row_done"), ph.sem("col_mm")
        ada_used, brow_in = ph.sem("ada_used"), ph.sem("brow_in")
        col_done, grow_out = ph.sem("col_done"), ph.sem("grow_out")
        COLS, ROWS = ps[:, 6, 0:32], [ps[0:2, 7, :], ps[0:2, 2, :]]
        block = ph.block()

        @block.sync
        def _(sp):
            with nc.allow_non_contiguous_dma(reason="a few small columns"):
                sp.dma_start(mg[:], g.tok_dram[:, C_MG:C_MG + 16].rearrange("(t p) c -> p t c", p=P)).then_inc(gin, 16)
                sp.dma_start(bias[:], io["ml_gate_b"]).then_inc(gin, 16)
                sp.dma_start(m0[:], io["ml_m0"]).then_inc(gin, 16)
                for b in range(8):
                    if b >= 4:
                        sp.wait_ge(ada_used, b - 3)
                    sp.dma_start(ada[b % 4][:], io["w_ada"][4 + b]).then_inc(ada_in[b % 4], 16)
                for r in range(2):
                    for n, lo in enumerate((2048, 5120)):
                        sp.dma_start(brow[r:r + 1, n * D:n * D + D],
                                     io["b_ada"][lo:lo + D].rearrange("(a n) -> a n", a=1)).then_inc(brow_in, 16)
                sp.wait_ge(rows_done, 1)
                sp.dma_start(g.gate_dram, rows[:]).then_inc(gout, 16)
                sp.dma_start(g.decay_dram, dec[:].rearrange("h d n -> h (d n)")).then_inc(gout, 16)
                sp.dma_start(g.outs["ml_m"], mlast[:]).then_inc(gout, 16)
            sp.wait_ge(row_done, 8)
            sp.dma_start(g.gate_rows, grow[:]).then_inc(grow_out, 16)
            sp.wait_ge(gout, 48)
            sp.wait_ge(grow_out, 16)

        @block.gpsimd
        def _(gp):
            gp.memset(keep[:], 1.0).then_inc(kept, 1)
            gp.wait_ge(kept, 1)
            gp.memset(keep[:, 0, 0:T:P], 0.0).then_inc(kept, 1)
            gp.memset(keep[:, 1, P - 1:T:P], 0.0).then_inc(kept, 1)

        @block.tensor
        def _(pe):
            pe.wait_ge(gin, 48)
            for q in range(4):
                if q >= 2:
                    pe.wait_ge(taken, q - 1)
                for t in range(NT):
                    mm = pe.transpose(ps[0:HEADS, 3 * (q % 2) + t // 3, t % 3 * P:t % 3 * P + P],
                                      mg[:, t, 4 * q:4 * q + 4], g.ident[:])
                mm.then_inc(turned, 1)
            for b in range(8):
                pe.wait_ge(ada_in[b % 4], 16 * (b // 4 + 1))
                if b == 1:
                    pe.wait_ge(taken, 4)
                if b >= 2:
                    pe.wait_ge(row_done, b - 1)
                ada_rows(pe, g, ROWS[b % 2], ada[b % 4]).then_inc(ada_used, 1)
                if 1 <= b <= 4:
                    pe.wait_ge(row_done, b)
                    ada_turn(pe, g, COLS, b - 1, arow[(b - 1) % 2]).then_inc(col_mm, 1)

        @block.scalar
        def _(act):
            act.wait_ge(absd, 1)
            act.activation(ab[:], ab[:], ACT.Exp, scale=-1.0).then_inc(lns, 1)
            act.wait_ge(lns, 1)
            act.activation(ab[:], ab[:], ACT.Ln, bias=1.0).then_inc(lns, 1)

        @block.vector
        def _(v):
            link = Chain(v, dve)
            for q in range(4):
                v.wait_ge(turned, q + 1)
                dst = (gi, gf)[q % 2][:, q // 2, :].rearrange("h (a n) -> h a n", a=3)
                v.tensor_scalar(dst, ps[0:HEADS, 3 * (q % 2):3 * (q % 2) + 3, 0:TH], bias[:, q:q + 1], None,
                                ALU.add).then_inc(taken, 1)
            v.wait_ge(taken, 4)
            v.scalar_tensor_tensor(out=ab[:], in0=gf[:], scalar=-1.0, in1=gf[:], op0=ALU.mult, op1=ALU.max).then_inc(absd, 1)
            link(v.tensor_scalar(mn[:], gf[:], 0.0, None, ALU.min))
            v.wait_ge(lns, 2)
            link(v.tensor_tensor(gf[:], mn[:], ab[:], ALU.subtract))
            v.wait_ge(kept, 3)
            for d in range(2):
                def run(x, lo, hi):
                    y = x[:, d, lo:hi]
                    return y if d == 0 else y[:, ::-1]

                link(v.tensor_tensor_scan(run(cum, 0, T), run(keep, 0, T), run(gf, 0, T), 0.0, ALU.mult, ALU.add))
                link(v.tensor_tensor_scan(run(m, 0, CTX), run(gf, 0, CTX), run(gi, 0, CTX), 0.0, ALU.add, ALU.max))
                link(v.tensor_tensor_scan(run(m, CTX, T), run(gf, CTX, T), run(gi, CTX, T), m0[:, d:d + 1], ALU.add, ALU.max))
            link(v.memset(mp[:, :, 0:1], 0.0))
            link(v.tensor_copy(mp[:, 0, 1:2], m0[:, 0:1]))
            link(v.tensor_copy(mp[:, 1, NT - 1:NT], m0[:, 1:2]))
            link(v.tensor_copy(mp[:, 0, 2:NT], m[:, 0, 2 * P - 1:T - 1:P]))
            link(v.tensor_copy(mp[:, 1, 1:NT - 1], m[:, 1, 2 * P:T:P]))
            a, u, ws, wk, nm = (rows[:, 2 * n:2 * n + 2, :] for n in range(5))
            link(v.tensor_tensor(u, cum[:], m[:], ALU.subtract))
            link(v.tensor_tensor(a, gi[:], cum[:], ALU.subtract))
            link(v.tensor_copy(ue[:, 0, :], u[:, 0, P - 1:T:P]))
            link(v.tensor_copy(ue[:, 1, :], u[:, 1, 0:T:P]))
            for d in range(2):
                def tiles(x):
                    return x[:, d, :].rearrange("h (n p) -> h n p", p=P)

                def wide(x):
                    return x[:, d, :].unsqueeze(2).broadcast_to([HEADS, NT, P])

                link(v.tensor_tensor(tiles(ws), tiles(u), wide(mp), ALU.add))
                link(v.tensor_tensor(tiles(wk), tiles(a), wide(ue), ALU.add))
            link(v.tensor_scalar(nm, m[:], -1.0, None, ALU.mult))
            link(v.tensor_tensor(dec[:], mp[:], ue[:], ALU.add))
            link(v.tensor_copy(mlast[:, 0:1], m[:, 0, CTX - 1:CTX]))
            v.tensor_copy(mlast[:, 1:2], m[:, 1, 0:1]).then_inc(rows_done, 1)
            for b in range(4):
                if b >= 2:
                    v.wait_ge(col_mm, b - 1)
                v.wait_ge(ada_used, b + 1)
                v.tensor_copy(arow[b % 2][:], ROWS[b % 2]).then_inc(row_done, 1)
            v.wait_ge(brow_in, 64)
            for n in range(4):
                v.wait_ge(ada_used, n + 5)
                v.tensor_tensor(grow[:, 512 * n:512 * n + 512], ROWS[n % 2], brow[:, 512 * n:512 * n + 512],
                                ALU.add).then_inc(row_done, 1)
                if n == 0:
                    v.wait_ge(col_mm, 4)
                    columns(v, link, g, COLS, 1, col_done)


def mlstm(nc, g):
    io, ps = g.io, g.ps
    V1 = DK + 1
    with Phase(nc, "mls") as ph:
        two = lambda name, shape: [ph.sb(f"{name}{s}", shape) for s in range(2)]
        q, k = two("q", [P, T]), two("k", [P, T])
        va = two("va", [P, NT, V1])
        mo = two("mo", [P, NT, P])
        a2, b2 = two("a2", [2, 2, T]), two("b2", [2, 2, T])
        r4 = two("r4", [4, T])
        wsr = two("wsr", [1, 2, T])
        dec = two("dec", [1, 2 * NT])
        s0 = two("s0", [P, 2, V1])
        gn = two("gn", [P, 1])
        qs = ph.sb("qs", [P, T])
        qw = ph.sb("qw", [P, 2, T])
        wb = ph.sb("wb", [P, 2, TH])
        wx = ph.sb("wx", [P, 2, TH])
        pw = ph.sb("pw", [P, 2, T])
        kw = ph.sb("kw", [P, 2, T])
        cols = ph.sb("cols", [P, NT, 4])
        decb = ph.sb("decb", [P, 2 * NT])
        st = ph.sb("st", [P, 2, NT, V1])
        den = ph.sb("den", [P, 2, NT])
        y = ph.sb("y", [P, NT, P])
        y2 = ph.sb("y2", [P, NT, P])
        junk = ph.sb("junk", [P, P])
        ss, ms, rstd, half = (ph.sb(n, [P, NT]) for n in ("ss", "ms", "rstd", "half"))
        yt = ph.sb("yt", [P, T])
        one = ph.sb("one", [1, P])
        neg = ph.sb("neg", [P, 2, TH], BF16)
        idb = ph.sb("idb", [P, P], BF16)
        NLOAD = 12
        loaded = [ph.sem(f"loaded{s}") for s in range(2)]
        free = ph.sem("free")
        sem = {n: ph.sem(n) for n in ("const", "qs", "misc", "cols", "wsb", "wsx", "qw", "dmm", "dx", "smm", "pw",
                                      "kt", "kw", "cmm", "st", "omm", "dve", "y", "ss", "act", "rstd", "yn", "ytm",
                                      "yte", "yout", "cout", "ms")}
        groups = range(3)
        block = ph.block()

        def head(i, s):
            return 2 * i + s

        @block.sync
        def _(sp):
            def load(i, s):
                h = head(i, s)
                sp.wait_ge(free, h + 1)
                feat = lambda r: g.feat_dram[bass.ds((h + r) * P, P), :]
                tok = lambda c: g.tok_dram[:, bass.ds(h * P + c, P)].rearrange("(t p) v -> p t v", p=P)
                gate = lambda lo, hi: g.gate_dram[bass.ds(h, 1), lo:hi, :]
                for dst, src in ((q[s][:], feat(R_MQ)), (k[s][:], feat(R_MK)), (va[s][:, :, 0:DK], tok(C_MV)),
                                 (mo[s][:], tok(C_MO)), (a2[s][0:1], gate(0, 2)), (b2[s][1:2], gate(2, 4)),
                                 (wsr[s][:], gate(4, 6)), (r4[s][:], gate(6, 10).rearrange("a r t -> (a r) t")),
                                 (dec[s][:], g.decay_dram[bass.ds(h, 1), :]),
                                 (s0[s][:, 0, :], io["ml_s0"][0, bass.ds(h * P, P), :]),
                                 (s0[s][:, 1, :], io["ml_s0"][1, bass.ds(h * P, P), :]),
                                 (gn[s][:], io["ml_g"][bass.ds(h * P, P), :])):
                    sp.dma_start(dst, src).then_inc(loaded[s], 16)

            sp.wait_ge(sem["const"], 10)
            with nc.allow_non_contiguous_dma(reason="one norm weight for a partition"):
                with sp.Fori(0, 2) as i:
                    for s in range(2):
                        load(i, s)

        @block.gpsimd
        def _(gp):
            c = sem["const"]
            for s in range(2):
                gp.memset(a2[s][:], 1.0).then_inc(c, 1)
                gp.memset(b2[s][:], 1.0).then_inc(c, 1)
                gp.memset(va[s][:, :, DK:V1], 1.0).then_inc(c, 1)
            gp.memset(half[:], -0.5).then_inc(c, 1)
            gp.memset(one[:], 1.0).then_inc(c, 1)
            gp.memset(neg[:], 0.0).then_inc(c, 1)
            gp.tensor_copy(idb[:], g.ident[:]).then_inc(c, 1)
            gp.wait_ge(c, 10)
            for d in range(2):
                sign = 1 if d == 0 else -1
                gp.affine_select(out=neg[:, d, :], in_=neg[:, d, :], compare_op=ALU.is_ge, fill=-1e30, base=0,
                                 pattern=[[0, 3], [sign, P]], channel_multiplier=-sign).then_inc(c, 1)

            with gp.Fori(0, 4) as i:
                gp.wait_ge(sem["st"], 6 * i + 6)
                for d in range(2):
                    gp.dma_start(g.outs["ml_s"][d, bass.ds(i * P, P), :], st[:, d, 0, :]).then_inc(sem["cout"], 16)
                gp.wait_ge(sem["ms"], i + 1)
                gp.tensor_tensor(rstd[:], ms[:], half[:], ALU.pow).then_inc(sem["rstd"], 1)

        @block.tensor
        def _(pe):
            pe.wait_ge(sem["const"], 12)

            def work(i, s):
                h = head(i, s)
                pe.wait_ge(loaded[s], 16 * NLOAD * i + 16 * NLOAD)
                pe.wait_ge(sem["yte"], h + 1)
                pe.matmul(ps[:, 7, 40:58], one[:], dec[s][:], start=True, stop=True)
                for j in range(NT):
                    mm = pe.transpose(ps[:, 7, 4 * j:4 * j + 4], r4[s][:, j * P:(j + 1) * P], g.ident[0:4, 0:4])
                mm.then_inc(sem["misc"], 1)
                for n in groups:
                    at = slice(n * TH, n * TH + TH)
                    if n:
                        pe.wait_ge(sem["dx"], 6 * h + 2 * n)
                    for d in range(2):
                        pe.matmul(ps[:, 1 + d, 0:TH], idb[:], neg[:, d, :], start=True, stop=False)
                        for j in range(3):
                            c = slice(n * TH + j * P, n * TH + j * P + P)
                            mm = pe.matmul(ps[:, 1 + d, j * P:(j + 1) * P], a2[s][:, d, c], b2[s][:, d, c],
                                           start=False, stop=j == 2)
                        mm.then_inc(sem["dmm"], 1)
                    if n:
                        pe.wait_ge(sem["pw"], 6 * h + 2 * n)
                    for j in range(3):
                        c = slice(n * TH + j * P, n * TH + j * P + P)
                        if n == 0 and j == 0:
                            pe.wait_ge(sem["qs"], h + 1)
                        mm = pe.matmul(ps[:, 0, j * P:(j + 1) * P], k[s][:, c], qs[:, c], start=True, stop=True)
                    mm.then_inc(sem["smm"], 1)
                    if n:
                        pe.wait_ge(sem["kw"], 6 * h + 2 * n)
                    for j in range(3):
                        c = slice(n * TH + j * P, n * TH + j * P + P)
                        mm = pe.transpose(ps[:, 3, j * P:(j + 1) * P], k[s][:, c], g.ident[:])
                    mm.then_inc(sem["kt"], 1)
                    if n:
                        pe.wait_ge(sem["wsx"], 6 * h + 2 * n)
                    for d in range(2):
                        mm = pe.matmul(ps[:, 5 + d, 0:TH], one[:], wsr[s][:, d, at], start=True, stop=True)
                        mm.then_inc(sem["wsb"], 1)
                for n in groups:
                    for d in range(2):
                        m = 2 * n + d
                        first = 3 * n if d == 0 else 6 - 3 * n
                        pe.wait_ge(sem["kw"], 6 * h + (2 * n + 1 + d if d == 0 else 6))
                        if m >= 2:
                            pe.wait_ge(sem["st"], 6 * h + m - 1)
                        bank = 4 if m % 2 == 0 else 3
                        for j in range(3):
                            c = slice((first + j) * P, (first + j) * P + P)
                            mm = pe.matmul(ps[:, bank, j * V1:j * V1 + V1], kw[:, d, c], va[s][:, first + j, :],
                                           start=True, stop=True)
                        mm.then_inc(sem["cmm"], 1)
                pe.wait_ge(sem["st"], 6 * h + 6)
                pe.wait_ge(sem["qw"], 6 * h + 6)
                pe.wait_ge(sem["pw"], 6 * h + 6)
                for n in groups:
                    for d in range(2):
                        if n:
                            pe.wait_ge(sem["y"], 3 * h + n)
                        for j in range(3):
                            t = 3 * n + j
                            c = slice(t * P, t * P + P)
                            out = ps[:, 5 + d, j * V1:j * V1 + V1]
                            mm = pe.matmul(out, pw[:, d, c], va[s][:, t, :], start=True, stop=t == 0)
                            if t:
                                mm = pe.matmul(out, qw[:, d, c], st[:, d, t, :], start=False, stop=True)
                        mm.then_inc(sem["omm"], 1)
                pe.wait_ge(sem["yn"], h + 1)
                for t in range(NT):
                    mm = pe.transpose(ps[:, t // 3, t % 3 * P:t % 3 * P + P], y2[:, t, :], g.ident[:])
                mm.then_inc(sem["ytm"], 1)

            with pe.Fori(0, 2) as i:
                for s in range(2):
                    work(i, s)

        @block.scalar
        def _(act):
            act.sem_inc(sem["yout"], 16)
            act.sem_inc(sem["yte"], 1)

            def work(i, s):
                h = head(i, s)
                act.wait_ge(loaded[s], 16 * NLOAD * i + 16 * NLOAD)
                act.activation(qs[:], q[s][:], ACT.Copy, scale=DK ** -0.5).then_inc(sem["qs"], 1)
                act.wait_ge(sem["misc"], h + 1)
                act.activation(cols[:].rearrange("p n c -> p (n c)"), ps[:, 7, 0:36], ACT.Exp).then_inc(sem["cols"], 1)
                act.activation(decb[:], ps[:, 7, 40:58], ACT.Exp).then_inc(sem["cols"], 1)
                for n in groups:
                    for d in range(2):
                        act.wait_ge(sem["dmm"], 6 * h + 2 * n + d + 1)
                        if n:
                            act.wait_ge(sem["pw"], 6 * h + 2 * n + d - 1)
                        act.activation(wx[:, d, :], ps[:, 1 + d, 0:TH], ACT.Exp).then_inc(sem["dx"], 1)
                    for d in range(2):
                        act.wait_ge(sem["wsb"], 6 * h + 2 * n + d + 1)
                        if n:
                            act.wait_ge(sem["qw"], 6 * h + 2 * n + d - 1)
                        act.activation(wb[:, d, :], ps[:, 5 + d, 0:TH], ACT.Exp).then_inc(sem["wsx"], 1)
                for t in range(NT):
                    if t % 3 == 0:
                        act.wait_ge(sem["y"], 3 * h + t // 3 + 1)
                    if t:
                        act.wait_ge(sem["ss"], 9 * h + t)
                    act.activation(junk[:], y[:, t, :], ACT.Square, accum_out=ss[:, t:t + 1]).then_inc(sem["ss"], 1)
                act.wait_ge(sem["ss"], 9 * h + NT)
                act.activation(ms[:], ss[:], ACT.Copy, bias=EPS, scale=1.0 / DK).then_inc(sem["ms"], 1)
                act.wait_ge(sem["ytm"], h + 1)
                act.wait_ge(sem["yout"], 16 * h + 16)
                act.activation(yt[:].rearrange("p (a n) -> p a n", a=3), ps[:, 0:3, 0:TH], ACT.Copy,
                               scale=gn[s][:, 0:1]).then_inc(sem["yte"], 1)
                act.wait_ge(sem["yte"], h + 2)
                act.dma_start(g.y_dram[bass.ds(h * P, P), :], yt[:]).then_inc(sem["yout"], 16)
                act.wait_ge(sem["cout"], 32 * h + 32)
                act.sem_inc(free, 1)

            act.sem_inc(free, 2)
            with act.Fori(0, 2) as i:
                for s in range(2):
                    work(i, s)
            act.wait_ge(sem["yout"], 80)

        @block.vector
        def _(v):
            link = Chain(v, sem["dve"])
            def work(i, s):
                h = head(i, s)
                v.wait_ge(loaded[s], 16 * NLOAD * i + 16 * NLOAD)
                for n in groups:
                    at = slice(n * TH, n * TH + TH)
                    for d in range(2):
                        v.wait_ge(sem["dx"], 6 * h + 2 * n + d + 1)
                        v.wait_ge(sem["smm"], 3 * h + n + 1)
                        v.tensor_tensor(pw[:, d, at], ps[:, 0, 0:TH], wx[:, d, :], ALU.mult).then_inc(sem["pw"], 1)
                    if n == 0:
                        v.wait_ge(sem["cols"], 2 * h + 2)
                    v.wait_ge(sem["kt"], 3 * h + n + 1)
                    for d in range(2):
                        w = cols[:, 3 * n:3 * n + 3, d].unsqueeze(2).broadcast_to([P, 3, P])
                        v.tensor_tensor(kw[:, d, at].rearrange("p (j c) -> p j c", j=3),
                                        ps[:, 3, 0:TH].rearrange("p (j c) -> p j c", j=3), w, ALU.mult).then_inc(sem["kw"], 1)
                    for d in range(2):
                        v.wait_ge(sem["wsx"], 6 * h + 2 * n + d + 1)
                        v.tensor_tensor(qw[:, d, at], qs[:, at], wb[:, d, :], ALU.mult).then_inc(sem["qw"], 1)
                v.wait_ge(free, h + 2)
                for n in groups:
                    for d in range(2):
                        m = 2 * n + d
                        first = 3 * n if d == 0 else 6 - 3 * n
                        v.wait_ge(sem["cmm"], 6 * h + m + 1)
                        bank = 4 if m % 2 == 0 else 3
                        order = range(3) if d == 0 else (2, 1, 0)
                        if n == 0:
                            v.tensor_copy(st[:, d, 1 if d == 0 else NT - 1, :], s0[s][:, d, :]).then_inc(sem["dve"], 1)
                            link.n += 1
                        for j in order:
                            t = first + j
                            add = ps[:, bank, j * V1:j * V1 + V1]
                            nxt = t + 1 if d == 0 else t - 1
                            if t == 0:
                                ins = v.tensor_copy(st[:, d, 0, :], add)
                            elif 1 <= nxt < NT:
                                v.wait_ge(sem["dve"], link.value())
                                ins = v.scalar_tensor_tensor(out=st[:, d, nxt, :], in0=st[:, d, t, :],
                                                             scalar=decb[:, NT * d + t:NT * d + t + 1], in1=add,
                                                             op0=ALU.mult, op1=ALU.add)
                            else:
                                continue
                            ins.then_inc(sem["dve"], 1)
                            link.n += 1
                        v.wait_ge(sem["dve"], link.value())
                        v.sem_inc(sem["st"], 1)
                for n in groups:
                    three = slice(3 * n, 3 * n + 3)
                    for d in range(2):
                        v.wait_ge(sem["omm"], 6 * h + 2 * n + d + 1)
                    o = [ps[:, 5 + d, 0:3 * V1].rearrange("p (j c) -> p j c", j=3) for d in range(2)]
                    for d in range(2):
                        link(v.scalar_tensor_tensor(out=den[:, d, three], in0=o[d][:, :, DK], scalar=-1.0,
                                                    in1=cols[:, three, 2 + d], op0=ALU.mult, op1=ALU.max))
                        link(v.tensor_tensor(den[:, d, three], den[:, d, three], o[d][:, :, DK], ALU.max))
                        link(v.reciprocal(den[:, d, three], den[:, d, three]))
                        r = den[:, d, three].unsqueeze(2).broadcast_to([P, 3, DK])
                        link(v.tensor_tensor((y, y2)[d][:, three, :], o[d][:, :, 0:DK], r, ALU.mult))
                    v.tensor_tensor(y[:, three, :], y[:, three, :], y2[:, three, :], ALU.add).then_inc(sem["y"], 1)
                v.wait_ge(sem["rstd"], h + 1)
                for t in range(NT):
                    ins = v.scalar_tensor_tensor(out=y2[:, t, :], in0=y[:, t, :], scalar=rstd[:, t:t + 1],
                                                 in1=mo[s][:, t, :], op0=ALU.mult, op1=ALU.mult)
                ins.then_inc(sem["yn"], 1)

            PER = 2 + 8 + 8 + 24
            with v.Fori(0, 2) as i:
                link.loop(i, 2 * PER)
                for s in range(2):
                    work(i, s)
            link.end(2)


def hgrn(nc, g):
    io, ps = g.io, g.ps
    LEVELS = 8
    with Phase(nc, "hgr") as ph:
        two = lambda name, shape: [ph.sb(f"{name}{s}", shape) for s in range(2)]
        q, hf = two("q", [P, T]), two("hf", [P, 2, T])
        va, hg = two("va", [P, NT, P]), two("hg", [P, NT, P])
        s0, gn = two("s0", [P, 2, P]), two("gn", [P, 1])
        tot = [ph.sb(f"tot{n}", [P, 2, T >> n]) for n in range(8)]
        qp, kp = ph.sb("qp", [P, 2, T]), ph.sb("kp", [P, 2, T])
        ad = ph.sb("ad", [P, 2, NT, 32])
        am = ph.sb("am", [P, 2, NT, P])
        kt = ph.sb("kt", [P, 2, T])
        st = ph.sb("st", [P, 2, NT, P])
        y2 = ph.sb("y2", [P, NT, P])
        junk = ph.sb("junk", [P, P])
        ss, ms, rstd, half = (ph.sb(n, [P, NT]) for n in ("ss", "ms", "rstd", "half"))
        yt = ph.sb("yt", [P, T])
        mask = ph.sb("mask", [P, 12, 32], I32)
        NLOAD = 8
        loaded = [ph.sem(f"loaded{s}") for s in range(2)]
        free = ph.sem("free")
        sem = {n: ph.sem(n) for n in ("const", "mask", "gates", "ini", "lmm", "pc", "upd", "far", "diag", "ktm", "kte",
                                      "smm", "dve", "omm", "ss", "ms", "rstd", "yn", "ytm", "yte", "yout", "cout", "st")}
        block = ph.block()

        def taken(l, d):
            return l + 2 * d + 1 if l < 2 else 2 * l + d + 1

        def far_order(d):
            return (0, 1) if d == 0 else (1, 0)

        @block.sync
        def _(sp):
            def load(i, s):
                h = 2 * i + s
                sp.wait_ge(free, h + 1)
                feat = lambda r: g.feat_dram[bass.ds((h + r) * P, P), :]
                tok = lambda c: g.tok_dram[:, bass.ds(h * P + c, P)].rearrange("(t p) v -> p t v", p=P)
                for dst, src in ((q[s][:], feat(R_HQ)), (hf[s][:, 0, :], feat(R_HF)), (hf[s][:, 1, :], feat(R_HF + 4)),
                                 (va[s][:], tok(C_HI)), (hg[s][:], tok(C_HG)),
                                 (s0[s][:, 0, :], io["hg_s0"][0, bass.ds(h * P, P), :]),
                                 (s0[s][:, 1, :], io["hg_s0"][1, bass.ds(h * P, P), :]),
                                 (gn[s][:], io["hg_g"][bass.ds(h * P, P), :])):
                    sp.dma_start(dst, src).then_inc(loaded[s], 16)

            sp.dma_start(mask[:], io["hg_mask"]).then_inc(sem["mask"], 16)
            with nc.allow_non_contiguous_dma(reason="one norm weight for a partition"):
                with sp.Fori(0, 2) as i:
                    for s in range(2):
                        load(i, s)

        @block.gpsimd
        def _(gp):
            gp.memset(half[:], -0.5).then_inc(sem["const"], 1)
            gp.memset(ad[:], 0.0).then_inc(sem["const"], 1)
            gp.memset(am[:], 0.0).then_inc(sem["const"], 1)
            with gp.Fori(0, 4) as i:
                gp.wait_ge(sem["st"], 6 * i + 6)
                for d in range(2):
                    gp.dma_start(g.outs["hg_s"][d, bass.ds(i * P, P), :], st[:, d, 0, :]).then_inc(sem["cout"], 16)
                gp.wait_ge(sem["ms"], i + 1)
                gp.tensor_tensor(rstd[:], ms[:], half[:], ALU.pow).then_inc(sem["rstd"], 1)

        @block.tensor
        def _(pe):
            def work(i, s):
                h = 2 * i + s
                pe.wait_ge(loaded[s], 16 * NLOAD * i + 16 * NLOAD)
                pe.wait_ge(sem["yte"], h + 1)
                pe.wait_ge(sem["gates"], 2 * h + 2)
                for l in range(6):
                    for d in range(2):
                        bank = 2 * (l % 2) + d
                        if l == 1:
                            pe.wait_ge(sem["ini"], 2 * h + d + 1)
                        if l >= 2:
                            pe.wait_ge(sem["upd"], 14 * h + 2 * (l - 2) + d + 1)
                            pe.wait_ge(sem["pc"], 12 * h + taken(l - 2, d))
                        for b in range(T // 32):
                            c = slice(32 * b, 32 * b + 32)
                            at = 32 * (b % 4)
                            mm = pe.matmul(ps[at:at + 32, bank, b // 4 * 32:b // 4 * 32 + 32], kp[:, d, c],
                                           q[s][:, c] if l == 0 else qp[:, d, c], start=True, stop=True)
                        mm.then_inc(sem["lmm"], 1)
                for d in range(2):
                    pe.wait_ge(sem["upd"], 14 * h + 8 + d + 1)
                    pe.wait_ge(sem["pc"], 12 * h + 8 + d + 1)
                    kb, qb = far_order(d)
                    for t in range(NT):
                        for half_ in range(2):
                            at = 64 * half_ + 32 * kb
                            mm = pe.matmul(ps[at:at + 32, d, 32 * t:32 * t + 32],
                                           kp[:, d, t * P + at:t * P + at + 32],
                                           qp[:, d, t * P + 64 * half_ + 32 * qb:t * P + 64 * half_ + 32 * qb + 32],
                                           start=True, stop=True)
                    mm.then_inc(sem["lmm"], 1)
                for d in range(2):
                    pe.wait_ge(sem["upd"], 14 * h + 10 + d + 1)
                    kb, qb = far_order(d)
                    for t in range(NT):
                        bank, col = 4 + 2 * d + t // 5, t % 5 * 64
                        mm = pe.matmul(ps[64 * kb:64 * kb + 64, bank, col:col + 64],
                                       kp[:, d, t * P + 64 * kb:t * P + 64 * kb + 64],
                                       qp[:, d, t * P + 64 * qb:t * P + 64 * qb + 64], start=True, stop=True)
                    mm.then_inc(sem["lmm"], 1)
                for n in range(3):
                    for d in range(2):
                        m = 2 * n + d
                        first = 3 * n if d == 0 else 6 - 3 * n
                        if m < 2:
                            pe.wait_ge(sem["upd"], 14 * h + 12 + d + 1)
                            pe.wait_ge(sem["far"], 4 * h + 2)
                        else:
                            pe.wait_ge(sem["kte"], 6 * h + m - 1)
                        for j in range(3):
                            c = slice((first + j) * P, (first + j) * P + P)
                            mm = pe.transpose(ps[:, m % 2, j * P:j * P + P], kp[:, d, c], g.ident[:])
                        mm.then_inc(sem["ktm"], 1)
                for n in range(3):
                    for d in range(2):
                        m = 2 * n + d
                        first = 3 * n if d == 0 else 6 - 3 * n
                        pe.wait_ge(sem["kte"], 6 * h + m + 1)
                        pe.wait_ge(sem["pc"], 12 * h + 12)
                        if m >= 2:
                            pe.wait_ge(sem["st"], 6 * h + m - 1)
                        for j in range(3):
                            c = slice((first + j) * P, (first + j) * P + P)
                            mm = pe.matmul(ps[:, 2 + m % 2, j * P:j * P + P], kt[:, d, c], va[s][:, first + j, :],
                                           start=True, stop=True)
                        mm.then_inc(sem["smm"], 1)
                pe.wait_ge(sem["far"], 4 * h + 4)
                pe.wait_ge(sem["diag"], h + 1)
                pe.wait_ge(sem["st"], 6 * h + 6)
                for t in range(NT):
                    out = ps[:, 4 + t // 3, t % 3 * P:t % 3 * P + P]
                    for d in range(2):
                        mm = pe.matmul(out, am[:, d, t, :], va[s][:, t, :], start=d == 0, stop=t == 0 and d == 1)
                    if t:
                        for d in range(2):
                            mm = pe.matmul(out, qp[:, d, t * P:t * P + P], st[:, d, t, :], start=False, stop=d == 1)
                    if t % 3 == 2:
                        mm.then_inc(sem["omm"], 1)
                pe.wait_ge(sem["yn"], h + 1)
                for t in range(NT):
                    mm = pe.transpose(ps[:, t // 3, t % 3 * P:t % 3 * P + P], y2[:, t, :], g.ident[:])
                mm.then_inc(sem["ytm"], 1)

            with pe.Fori(0, 2) as i:
                for s in range(2):
                    work(i, s)

        @block.scalar
        def _(act):
            act.sem_inc(sem["yout"], 16)
            act.sem_inc(sem["yte"], 1)
            act.sem_inc(free, 2)
            act.wait_ge(sem["const"], 3)

            def work(i, s):
                h = 2 * i + s
                act.wait_ge(loaded[s], 16 * NLOAD * i + 16 * NLOAD)
                act.activation(kp[:], hf[s][:], ACT.Sigmoid, scale=-1.0).then_inc(sem["gates"], 1)
                act.activation(tot[0][:], hf[s][:], ACT.Sigmoid).then_inc(sem["gates"], 1)
                for d in range(2):
                    act.wait_ge(sem["lmm"], 16 * h + 12 + d + 1)
                    kb, qb = far_order(d)
                    for half_ in range(2):
                        at, to = 64 * half_ + 32 * kb, 64 * half_ + 32 * qb
                        ins = act.activation(am[at:at + 32, d, :, to:to + 32],
                                             ps[at:at + 32, d, 0:32 * NT].rearrange("p (t c) -> p t c", c=32), ACT.Copy)
                    ins.then_inc(sem["far"], 1)
                for d in range(2):
                    act.wait_ge(sem["lmm"], 16 * h + 14 + d + 1)
                    kb, qb = far_order(d)
                    rows, to = slice(64 * kb, 64 * kb + 64), slice(64 * qb, 64 * qb + 64)
                    act.activation(am[rows, d, 0:5, to], ps[rows, 4 + 2 * d, 0:320].rearrange("p (t c) -> p t c", c=64), ACT.Copy)
                    act.activation(am[rows, d, 5:NT, to], ps[rows, 5 + 2 * d, 0:256].rearrange("p (t c) -> p t c", c=64),
                                   ACT.Copy).then_inc(sem["far"], 1)
                for n in range(3):
                    for d in range(2):
                        m = 2 * n + d
                        first = 3 * n if d == 0 else 6 - 3 * n
                        act.wait_ge(sem["ktm"], 6 * h + m + 1)
                        act.activation(kt[:, d, first * P:first * P + TH], ps[:, m % 2, 0:TH], ACT.Copy).then_inc(sem["kte"], 1)
                act.wait_ge(sem["pc"], 12 * h + 12)
                for d in range(2):
                    for b in range(4):
                        r = slice(32 * b, 32 * b + 32)
                        ins = act.activation(am[r, d, :, r], ad[r, d, :, :], ACT.Copy)
                ins.then_inc(sem["diag"], 1)
                for t in range(NT):
                    if t % 3 == 0:
                        act.wait_ge(sem["omm"], 3 * h + t // 3 + 1)
                    if t:
                        act.wait_ge(sem["ss"], 9 * h + t)
                    act.activation(junk[:], ps[:, 4 + t // 3, t % 3 * P:t % 3 * P + P], ACT.Square,
                                   accum_out=ss[:, t:t + 1]).then_inc(sem["ss"], 1)
                act.wait_ge(sem["ss"], 9 * h + NT)
                act.activation(ms[:], ss[:], ACT.Copy, bias=EPS, scale=1.0 / DK).then_inc(sem["ms"], 1)
                act.wait_ge(sem["ytm"], h + 1)
                act.wait_ge(sem["yout"], 16 * h + 16)
                act.activation(yt[:].rearrange("p (a n) -> p a n", a=3), ps[:, 0:3, 0:TH], ACT.Copy,
                               scale=gn[s][:, 0:1]).then_inc(sem["yte"], 1)
                act.wait_ge(sem["yte"], h + 2)
                act.dma_start(g.y_dram[bass.ds((HEADS + h) * P, P), :], yt[:]).then_inc(sem["yout"], 16)
                act.wait_ge(sem["cout"], 32 * h + 32)
                act.sem_inc(free, 1)

            with act.Fori(0, 2) as i:
                for s in range(2):
                    work(i, s)
            act.wait_ge(sem["yout"], 80)

        @block.vector
        def _(v):
            link = Chain(v, sem["dve"])
            v.wait_ge(sem["mask"], 16)
            v.wait_ge(sem["const"], 3)

            def work(i, s):
                h = 2 * i + s
                v.wait_ge(loaded[s], 16 * NLOAD * i + 16 * NLOAD)
                v.wait_ge(sem["gates"], 2 * h + 2)
                v.wait_ge(free, h + 2)
                for d in range(2):
                    v.tensor_tensor(qp[:, d, :], q[s][:], tot[0][:, d, :], ALU.mult).then_inc(sem["ini"], 1)

                def take(l, d):
                    m = mask[:, 2 * l + d, :].unsqueeze(1).broadcast_to([P, NT, 32])
                    v.copy_predicated(ad[:, d, :, :], m, ps[:, 2 * (l % 2) + d, 0:32 * NT].rearrange("p (t c) -> p t c", c=32)
                                      ).then_inc(sem["pc"], 1)

                def widen(l, d):
                    size = 1 << (l - 1)
                    kb, qb = far_order(d)
                    v.wait_ge(sem["lmm"], 16 * h + 2 * l + d + 1)
                    if l > 1 or d:
                        v.wait_ge(sem["pc"], 12 * h + (2 if l == 1 else min(2 * l + d, 12)))
                    pair = lambda x: x[:, d, :].rearrange("p (n a e) -> p n a e", a=2, e=size)
                    t2 = tot[l - 1][:, d, :].rearrange("p (n a) -> p n a", a=2)
                    wide = lambda b: t2[:, :, b:b + 1].broadcast_to([P, T // (2 * size), size])
                    v.tensor_tensor(pair(qp)[:, :, qb, :], pair(qp)[:, :, qb, :], wide(kb), ALU.mult)
                    if l == 1:
                        take(0, d)
                        v.wait_ge(sem["pc"], 12 * h + 2 * d + 1)
                    elif l < 6:
                        take(l, d)
                    v.tensor_tensor(pair(kp)[:, :, kb, :], pair(kp)[:, :, kb, :], wide(qb), ALU.mult).then_inc(sem["upd"], 1)
                    if l == 1:
                        take(1, d)
                    link(v.tensor_tensor(tot[l][:, d, :], t2[:, :, 0], t2[:, :, 1], ALU.mult))

                for l in range(1, LEVELS):
                    for d in range(2):
                        widen(l, d)
                for n in range(3):
                    for d in range(2):
                        m = 2 * n + d
                        first = 3 * n if d == 0 else 6 - 3 * n
                        v.wait_ge(sem["smm"], 6 * h + m + 1)
                        if n == 0:
                            v.tensor_copy(st[:, d, 1 if d == 0 else NT - 1, :], s0[s][:, d, :]).then_inc(sem["dve"], 1)
                            link.n += 1
                        for j in range(3) if d == 0 else (2, 1, 0):
                            t = first + j
                            add = ps[:, 2 + m % 2, j * P:j * P + P]
                            nxt = t + 1 if d == 0 else t - 1
                            if t == 0:
                                ins = v.tensor_copy(st[:, d, 0, :], add)
                            elif 1 <= nxt < NT:
                                v.wait_ge(sem["dve"], link.value())
                                ins = v.scalar_tensor_tensor(out=st[:, d, nxt, :], in0=st[:, d, t, :],
                                                             scalar=tot[7][:, d, t:t + 1], in1=add,
                                                             op0=ALU.mult, op1=ALU.add)
                            else:
                                continue
                            ins.then_inc(sem["dve"], 1)
                            link.n += 1
                        v.wait_ge(sem["dve"], link.value())
                        v.sem_inc(sem["st"], 1)
                v.wait_ge(sem["rstd"], h + 1)
                for t in range(NT):
                    ins = v.scalar_tensor_tensor(out=y2[:, t, :], in0=ps[:, 4 + t // 3, t % 3 * P:t % 3 * P + P],
                                                 scalar=rstd[:, t:t + 1], in1=hg[s][:, t, :], op0=ALU.mult, op1=ALU.mult)
                ins.then_inc(sem["yn"], 1)

            PER = 14 + 2 + 8 + 8
            with v.Fori(0, 2) as i:
                link.loop(i, 2 * PER)
                for s in range(2):
                    work(i, s)
            link.end(2)


def attention(nc, g):
    io, ps = g.io, g.ps
    NK = NT + 1
    H1 = HD + 1
    H2 = 2 * HD + 1
    G = AH // KV
    QS = HD ** -0.5
    with Phase(nc, "att") as ph:
        kn = ph.sb("kn", [P, NT, KV, HD])
        k2 = ph.sb("k2", [P, NT, KV, HD])
        kr = ph.sb("kr", [P, NK, KV, HD])
        kpart = [ph.sb("kparthi", [P, NK, KV, 2 * HD], F32R), ph.sb("kpartlo", [P, NK, KV, H1], F32R)]
        kt = [ph.sb(f"kt{n}", [P, KV, NK * P], F32R) for n in ("hi", "lo")]
        va = ph.sb("va", [P, NK, KV, H1])
        nil = ph.sb("nil", [1, G * H1], BF16)
        unit, zero = ph.sb("unit", [P, NK, KV]), ph.sb("zero", [P, G, 1])
        kss, kms, krs, khalf = (ph.sb(n, [P, NT * KV]) for n in ("kss", "kms", "krs", "khalf"))
        grow = ph.sb("grow", [P, 2, HD])
        tab = ph.sb("tab", [P, NT - 1, 2, HD // 2])
        qtab = ph.sb("qtab", [P, NT - 1, 4, HD // 2])
        r1, r2 = ph.sb("r1", [P, NT - 1, KV, HD // 2]), ph.sb("r2", [P, NT - 1, KV, HD // 2])
        q = ph.sb("q", [P, AH, HD])
        qtb = ph.sb("qtb", [P, 4, HD // 2])
        q2, qn, qr = (ph.sb(n, [P, AH, HD]) for n in ("q2", "qn", "qr"))
        u1, u2 = ph.sb("u1", [P, AH, HD // 2]), ph.sb("u2", [P, AH, HD // 2])
        qss, qms, qrs = (ph.sb(n, [P, AH]) for n in ("qss", "qms", "qrs"))
        qpart = [ph.sb(f"qpart{i}", [P, G, H2], F32R) for i in range(KV)]
        qt = [ph.sb(f"qt{i}", [P, G * P], F32R) for i in range(KV)]
        qm = [ph.sb(f"qm{i}", [P, G * P], F32R) for i in range(KV)]
        prc, ptc = ph.sb("prc", [P, AH * P]), ph.sb("ptc", [P, AH * P])
        pt = [ph.sb(f"pt{i}", [P, G * P]) for i in range(3)]
        mx = ph.sb("mx", [P, 2])
        rs = ph.sb("rs", [P, KV, G])
        mxc, rsc = ph.sb("mxc", [P, AH]), ph.sb("rsc", [P, AH])
        y = ph.sb("y", [P, AH, HD])
        yt = ph.sb("yt", [P, 4, P])
        names = ("load qload const knd kpow kout ktm kte qd qpow rope cpart qtm qte csmm cmx cex cptm cpte comm cdone "
                 "part s1 mx nm ptm pte s2 ex pv on yout kv dve")
        sem = {n: ph.sem(n) for n in names.split()}
        block = ph.block()
        PT, ST, OB = 3, 4, 7
        SHIFTS = range(0, 3)
        use = lambda i, k: 2 + 5 * i + k

        @block.sync
        def _(sp):
            tok = lambda c, w: g.tok_dram[:, c:c + w].rearrange("(t p) v -> p t v", p=P)
            with nc.allow_non_contiguous_dma(reason="rows of 64 values"):
                sp.dma_start(kn[:].rearrange("p t h d -> p t (h d)"), tok(C_AK, KV * HD)).then_inc(sem["load"], 16)
                sp.dma_start(kr[:, 8].rearrange("p h d -> p (h d)"), io["cache_k"]).then_inc(sem["load"], 16)
                sp.dma_start(grow[:].rearrange("p a d -> p (a d)"), io["qk_g"].partition_broadcast(P)).then_inc(sem["load"], 16)
                sp.dma_start(tab[:], io["rope"]).then_inc(sem["load"], 16)
                sp.dma_start(q[:].rearrange("p h d -> p (h d)"), g.tok_dram[0:P, C_AQ:C_AQ + AH * HD]).then_inc(sem["qload"], 16)
                for kv in range(KV):
                    src = g.tok_dram[:, C_AV + kv * HD:C_AV + kv * HD + HD]
                    sp.dma_start(va[:, 0:8, kv, 0:HD], src[CTX:T, :].rearrange("(t p) v -> p t v", p=P)).then_inc(sem["kv"], 16)
                    sp.dma_start(va[:, 9, kv, 0:HD], src[0:CTX, :]).then_inc(sem["kv"], 16)
                    sp.dma_start(va[:, 8, kv, 0:HD], io["cache_v"][:, kv * HD:kv * HD + HD]).then_inc(sem["kv"], 16)
            sp.wait_ge(sem["qd"], 4)
            sp.dma_start(q[:].rearrange("p h d -> p (h d)"), g.tok_dram[P:2 * P, C_AQ:C_AQ + AH * HD]).then_inc(sem["qload"], 16)
            sp.wait_ge(sem["kpow"], 3)
            sp.dma_start(g.outs["k"], kn[:, 0].rearrange("p h d -> p (h d)")).then_inc(sem["kout"], 16)
            sp.dma_start(g.outs["v"], g.tok_dram[0:CTX, C_AV:C_AV + KV * HD]).then_inc(sem["kout"], 16)
            with sp.Fori(0, 7) as i:
                sp.wait_ge(sem["qd"], 4 * i + 8)
                sp.dma_start(q[:].rearrange("p h d -> p (h d)"),
                             g.tok_dram[bass.ds(i * P + 2 * P, P), C_AQ:C_AQ + AH * HD]).then_inc(sem["qload"], 16)
            sp.wait_ge(sem["kout"], 32)

        @block.gpsimd
        def _(gp):
            gp.memset(khalf[:], -0.5).then_inc(sem["const"], 1)
            gp.memset(va[:, :, :, HD:H1], 1.0).then_inc(sem["const"], 1)
            gp.memset(nil[:], 0.0).then_inc(sem["const"], 1)
            gp.wait_ge(sem["const"], 1)
            gp.wait_ge(sem["knd"], 3)
            gp.tensor_tensor(krs[:], kms[:], khalf[:], ALU.pow).then_inc(sem["kpow"], 1)
            gp.wait_ge(sem["qd"], 3)
            gp.tensor_tensor(qrs[:], qms[:], khalf[:, 0:AH], ALU.pow).then_inc(sem["qpow"], 1)

            def rope(n):
                gp.wait_ge(sem["qd"], 4 * n + 4 + 3)
                gp.tensor_tensor(qrs[:], qms[:], khalf[:, 0:AH], ALU.pow).then_inc(sem["qpow"], 1)
                gp.wait_ge(sem["qd"], 4 * n + 4 + 4)
                x = qn[:].rearrange("p h (d e) -> p h d e", e=2)
                o = qr[:].rearrange("p h (d e) -> p h d e", e=2)
                w = lambda c: qtb[:, c, :].unsqueeze(1).broadcast_to([P, AH, HD // 2])
                for e in range(2):
                    a, b = (0, 1) if e == 0 else (2, 3)
                    gp.tensor_tensor(u1[:], x[:, :, :, 0], w(a), ALU.mult).then_inc(sem["rope"], 1)
                    gp.tensor_tensor(u2[:], x[:, :, :, 1], w(b), ALU.mult).then_inc(sem["rope"], 1)
                    gp.wait_ge(sem["rope"], 6 * n + 3 * e + 2)
                    gp.tensor_tensor(o[:, :, :, e], u1[:], u2[:], ALU.subtract if e == 0 else ALU.add).then_inc(sem["rope"], 1)
                    gp.wait_ge(sem["rope"], 6 * n + 3 * e + 3)

            rope(0)
            with gp.Fori(0, 7) as i:
                rope(i + 1)

        def turn_queries(pe, kv, bank):
            for a in range(G):
                mm = pe.transpose(ps[:, bank, a * P:a * P + P], qpart[kv][:, a, 1:H2].bitcast(F32), g.ident[:])
            return mm

        def turn_shifts(pe, kv, bank):
            for a in range(G):
                mm = pe.transpose(ps[0:H1, bank, a * P:a * P + P], qpart[kv][:, a, 0:H1].bitcast(F32), g.ident[:])
            return mm

        @block.tensor
        def _(pe):
            pe.wait_ge(sem["knd"], 6)
            n = 0
            for part in range(2):
                rows = (P, H1)[part]
                for kv in range(KV):
                    for t0, nt in ((0, 4), (4, 4), (8, 2)):
                        if n >= 6:
                            pe.wait_ge(sem["kte"], n - 5)
                        for t in range(nt):
                            mm = pe.transpose(ps[0:rows, n % 6, t * P:t * P + P],
                                              kpart[part][:, t0 + t, kv, :].bitcast(F32), g.ident[:])
                        mm.then_inc(sem["ktm"], 1)
                        n += 1
            pe.wait_ge(sem["kte"], 12)
            pe.wait_ge(sem["cpart"], 2)
            for kv in range(KV):
                turn_queries(pe, kv, kv)
                mm = turn_shifts(pe, kv, 2 + kv)
            mm.then_inc(sem["qtm"], 1)
            pe.wait_ge(sem["qte"], 4)
            for c in range(AH):
                kv, at = c // G, slice(c % G * P, c % G * P + P)
                pe.matmul(ps[:, 4 + kv, at], qt[kv][:, at], kt[0][:, kv, 9 * P:10 * P], start=True, stop=False)
                mm = pe.matmul(ps[:, 4 + kv, at], qm[kv][0:H1, at], kt[1][0:H1, kv, 9 * P:10 * P], start=False, stop=True)
            mm.then_inc(sem["csmm"], 1)
            pe.wait_ge(sem["cex"], 8)
            for c in range(AH):
                mm = pe.transpose(ps[:, 6 + c // G, c % G * P:c % G * P + P], prc[:, c * P:c * P + P], g.ident[:])
            mm.then_inc(sem["cptm"], 1)
            pe.wait_ge(sem["cpte"], 1)
            pe.wait_ge(sem["kv"], 96)
            pe.wait_ge(sem["const"], 3)
            for c in range(AH):
                mm = pe.matmul(ps[:, c // G, c % G * H1:c % G * H1 + H1], ptc[:, c * P:c * P + P], va[:, 9, c // G, :],
                               start=True, stop=True)
            mm.then_inc(sem["comm"], 1)

            def queries(u, kv):
                pe.wait_ge(sem["pte"], u) if not (isinstance(u, int) and u == 0) else None
                turn_queries(pe, kv, PT).then_inc(sem["ptm"], 1)

            def shift_scores(n, kv, a):
                if not (isinstance(n, int) and n + a == 0):
                    pe.wait_ge(sem["mx"], 4 * n + a)
                for c in SHIFTS:
                    mm = pe.matmul(ps[:, c, 0:TH], qt[kv][:, a * P:a * P + P], kt[0][:, kv, c * TH:c * TH + TH],
                                   start=True, stop=True)
                mm.then_inc(sem["s1"], 1)

            def shifts(n, kv, u):
                pe.wait_ge(sem["nm"], 4 * n + 4)
                pe.wait_ge(sem["pte"], u)
                turn_shifts(pe, kv, PT).then_inc(sem["ptm"], 1)

            def scores(n, kv, j):
                pe.wait_ge(sem["ex"], 9 * n + j + 1)
                out, at = ps[:, ST + j % 3, :], slice(j * P, j * P + P)
                pe.matmul(out, kt[0][:, kv, at], qt[kv][:], start=True, stop=False)
                pe.matmul(out, kt[1][0:H1, kv, at], qm[kv][0:H1, :], start=False, stop=True).then_inc(sem["s2"], 1)

            def values(n, kv, j):
                pe.wait_ge(sem["ex"], 9 * n + j + 4)
                if j == 0:
                    pe.wait_ge(sem["on"], n + 1)
                    pe.matmul(ps[:, OB, 0:G * H1], nil[:, 0:P], nil[:], start=True, stop=False)
                for a in range(G):
                    mm = pe.matmul(ps[:, OB, a * H1:a * H1 + H1], pt[j % 3][:, a * P:a * P + P], va[:, j, kv, :],
                                   start=False, stop=j == NT - 1 and a == G - 1)
                mm.then_inc(sem["pv"], 1)

            def output(u, i):
                pe.wait_ge(sem["on"], 2 * i + 1)
                pe.wait_ge(sem["pte"], u)
                for t in range(4):
                    mm = pe.transpose(ps[:, PT, t * P:t * P + P],
                                      y[:, 2 * t:2 * t + 2, :].rearrange("p h d -> p (h d)"), g.ident[:])
                mm.then_inc(sem["ptm"], 1)

            def group(i, kv, more):
                n, nkv = 2 * i + kv, 1 - kv
                u = use(i, 0 if kv == 0 else 3)
                pe.wait_ge(sem["pte"], use(i, 0 if kv == 0 else 3))
                if more:
                    if kv == 0:
                        pe.wait_ge(sem["part"], 2 * i + 2)
                    else:
                        pe.wait_ge(sem["part"], 2 * i + 3)
                    queries(u, nkv)
                for j in range(NT):
                    scores(n, kv, j)
                    if more and j in (1, 3, 5, 7):
                        a = j // 2
                        if a == 0:
                            pe.wait_ge(sem["pte"], u + 1)
                        shift_scores(n + 1, nkv, a)
                    if j >= 2:
                        values(n, kv, j - 2)
                    if j == 3 and kv == 0:
                        output(use(i, 1), i)
                if more:
                    shifts(n + 1, nkv, use(i, 2 if kv == 0 else 4))
                values(n, kv, NT - 2)
                values(n, kv, NT - 1)

            pe.sem_inc(sem["pv"], 3)
            pe.wait_ge(sem["cdone"], 1)
            pe.wait_ge(sem["part"], 1)
            queries(0, 0)
            pe.wait_ge(sem["pte"], 1)
            for a in range(G):
                shift_scores(0, 0, a)
            shifts(0, 0, 1)
            with pe.Fori(0, 7) as i:
                group(i, 0, True)
                group(i, 1, True)
            group(7, 0, True)
            group(7, 1, False)
            output(use(7, 3), 8)

        @block.scalar
        def _(act):
            for n in range(12):
                act.wait_ge(sem["ktm"], n + 1)
                part, kv, (t0, nt) = n // 6, n // 3 % 2, ((0, 4), (4, 4), (8, 2))[n % 3]
                rows = (P, H1)[part]
                act.activation(kt[part][0:rows, kv, t0 * P:(t0 + nt) * P], ps[0:rows, n % 6, 0:nt * P], ACT.Copy).then_inc(sem["kte"], 1)
            act.wait_ge(sem["qtm"], 1)
            for kv in range(KV):
                act.activation(qt[kv][:], ps[:, kv, :], ACT.Copy).then_inc(sem["qte"], 1)
                act.activation(qm[kv][0:H1, :], ps[0:H1, 2 + kv, :], ACT.Copy).then_inc(sem["qte"], 1)
            act.wait_ge(sem["cmx"], 1)
            for c in range(AH):
                act.activation(prc[:, c * P:c * P + P], ps[:, 4 + c // G, c % G * P:c % G * P + P], ACT.Exp,
                               bias=mxc[:, c:c + 1], scale=QS).then_inc(sem["cex"], 1)
            act.wait_ge(sem["cptm"], 1)
            act.activation(ptc[:].rearrange("p (a n) -> p a n", a=2), ps[:, 6:8, :], ACT.Copy).then_inc(sem["cpte"], 1)
            act.sem_inc(sem["ex"], 3)
            act.sem_inc(sem["yout"], 16)

            def queries(u, kv):
                act.wait_ge(sem["ptm"], u + 1)
                act.activation(qt[kv][:], ps[:, PT, :], ACT.Copy).then_inc(sem["pte"], 1)

            def shifts(u, kv):
                act.wait_ge(sem["ptm"], u + 1)
                act.activation(qm[kv][0:H1, :], ps[0:H1, PT, :], ACT.Copy).then_inc(sem["pte"], 1)

            def output(u, i):
                act.wait_ge(sem["ptm"], u + 1)
                act.wait_ge(sem["yout"], 16 * i + 16)
                act.activation(yt[:].rearrange("p t n -> p (t n)"), ps[:, PT, :], ACT.Copy).then_inc(sem["pte"], 1)
                act.wait_ge(sem["pte"], u + 1)
                act.dma_start(g.y_dram[2 * 4 * P:, bass.ds(i * P, P)].rearrange("(t p) n -> p t n", p=P), yt[:]).then_inc(sem["yout"], 16)

            def group(i, kv, more):
                n = 2 * i + kv
                if more:
                    queries(use(i, 0 if kv == 0 else 3), 1 - kv)
                for j in range(NT):
                    act.wait_ge(sem["s2"], 9 * n + j + 1)
                    act.wait_ge(sem["pv"], 9 * n + j + 1)
                    act.activation(pt[j % 3][:], ps[:, ST + j % 3, :], ACT.Exp, scale=QS).then_inc(sem["ex"], 1)
                    if j == 3 and kv == 0:
                        output(use(i, 1), i)
                if more:
                    shifts(use(i, 2 if kv == 0 else 4), 1 - kv)

            queries(0, 0)
            shifts(1, 0)
            with act.Fori(0, 7) as i:
                group(i, 0, True)
                group(i, 1, True)
            group(7, 0, True)
            group(7, 1, False)
            output(use(7, 3), 8)
            act.wait_ge(sem["yout"], 16 * 10)

        @block.vector
        def _(v):
            link = Chain(v, sem["dve"])
            wide = lambda x, n: x.unsqueeze(2).broadcast_to([P, n, HD])
            flat = lambda x: x.rearrange("p t h d -> p (t h) d")
            v.wait_ge(sem["load"], 64)
            v.tensor_tensor(k2[:], kn[:], kn[:], ALU.mult).then_inc(sem["knd"], 1)
            v.wait_ge(sem["knd"], 1)
            v.tensor_reduce(kss[:], flat(k2[:]), AX.X, ALU.add).then_inc(sem["knd"], 1)
            v.wait_ge(sem["knd"], 2)
            v.tensor_scalar(kms[:], kss[:], 1.0 / HD, EPS, ALU.mult, ALU.add).then_inc(sem["knd"], 1)
            gq = grow[:, 0, :].rearrange("p (d e) -> p d e", e=2)
            for c, (e, t) in enumerate(((0, 0), (1, 1), (0, 1), (1, 0))):
                link(v.tensor_tensor(qtab[:, :, c, :], tab[:, :, t, :],
                                     gq[:, :, e].unsqueeze(1).broadcast_to([P, NT - 1, HD // 2]), ALU.mult))
            v.wait_ge(sem["kpow"], 1)
            link(v.tensor_tensor(flat(kn[:]), flat(kn[:]), wide(krs[:], NT * KV), ALU.mult))
            link(v.tensor_tensor(flat(kn[:]), flat(kn[:]), grow[:, 1, :].unsqueeze(1).broadcast_to([P, NT * KV, HD]), ALU.mult))
            v.sem_inc(sem["kpow"], 2)
            x = kn[:, 1:].rearrange("p t h (d e) -> p t h d e", e=2)
            o = kr[:, 0:8].rearrange("p t h (d e) -> p t h d e", e=2)
            w = lambda c: tab[:, :, c, :].unsqueeze(2).broadcast_to([P, NT - 1, KV, HD // 2])
            for e in range(2):
                link(v.tensor_tensor(r1[:], x[:, :, :, :, 0], w(e), ALU.mult))
                link(v.tensor_tensor(r2[:], x[:, :, :, :, 1], w(1 - e), ALU.mult))
                link(v.tensor_tensor(o[:, :, :, :, e], r1[:], r2[:], ALU.subtract if e == 0 else ALU.add))
            link(v.tensor_copy(kr[:, 9], kn[:, 0]))
            for a in range(2):
                link(v.tensor_copy(flat(kpart[0][:, :, :, a * HD:a * HD + HD]), flat(kr[:])))
            link(v.memset(zero[:], 0.0))
            link(v.memset(unit[:], 1.0))
            v.tensor_copy(kpart[1][:, :, :, 0], unit[:]).then_inc(sem["knd"], 1)
            for kv in range(KV):
                v.tensor_tensor(kpart[1][:, :, kv, 1:H1], kr[:, :, kv, :], kpart[0][:, :, kv, 0:HD].bitcast(F32),
                                ALU.subtract).then_inc(sem["knd"], 1)

            def norm_a(n):
                v.wait_ge(sem["qload"], 16 * n + 16)
                v.tensor_tensor(q2[:], q[:], q[:], ALU.mult).then_inc(sem["qd"], 1)
                v.wait_ge(sem["qd"], 4 * n + 1)
                v.tensor_reduce(qss[:], q2[:], AX.X, ALU.add).then_inc(sem["qd"], 1)
                v.wait_ge(sem["qd"], 4 * n + 2)
                v.tensor_scalar(qms[:], qss[:], 1.0 / HD, EPS, ALU.mult, ALU.add).then_inc(sem["qd"], 1)

            def norm_b(n, table):
                v.wait_ge(sem["qpow"], n + 1)
                if table is not None:
                    v.tensor_copy(qtb[:], table)
                v.tensor_tensor(qn[:], q[:], wide(qrs[:], AH), ALU.mult).then_inc(sem["qd"], 1)

            def split(kv, done):
                x = qr[:].rearrange("p (a k) d -> p k a d", k=KV)[:, kv]
                link(v.tensor_copy(qpart[kv][:, :, 1:H1], x))
                v.tensor_tensor(qpart[kv][:, :, H1:H2], x, qpart[kv][:, :, 1:H1].bitcast(F32), ALU.subtract).then_inc(done, 1)

            norm_a(0)
            norm_b(0, None)
            v.wait_ge(sem["qd"], 4)
            for kv in range(KV):
                link(v.tensor_copy(qpart[kv][:, :, 0:1], zero[:]))
            link(v.tensor_tensor(qr[:], qn[:], grow[:, 0, :].unsqueeze(1).broadcast_to([P, AH, HD]), ALU.mult))
            split(0, sem["cpart"])
            split(1, sem["cpart"])
            norm_a(1)
            norm_b(1, qtab[:, 0])
            v.wait_ge(sem["csmm"], 1)
            link(v.tensor_reduce(mxc[:].rearrange("p (k a) -> p k a", k=KV), ps[:, 4:6, :].rearrange("p k (a n) -> p k a n", a=G),
                                 AX.X, ALU.max))
            v.tensor_scalar(mxc[:], mxc[:], -QS, None, ALU.mult).then_inc(sem["cmx"], 1)
            v.wait_ge(sem["rope"], 6)
            split(0, sem["part"])
            split(1, sem["part"])
            norm_a(2)
            norm_b(2, qtab[:, 1])
            v.wait_ge(sem["comm"], 1)
            r4 = rsc[:].rearrange("p (k a) -> p k a", k=KV)
            yk = y[:].rearrange("p (a k) d -> p k a d", k=KV)
            heads = lambda bank: ps[:, bank, 0:G * H1].rearrange("p (a n) -> p a n", a=G)
            for kv in range(KV):
                link(v.reciprocal(r4[:, kv], heads(kv)[:, :, HD]))
                ins = v.tensor_tensor(yk[:, kv], heads(kv)[:, :, 0:HD], r4[:, kv].unsqueeze(2).broadcast_to([P, G, HD]), ALU.mult)
                ins.then_inc(sem["cdone"], 1) if kv else link(ins)
            v.sem_inc(sem["on"], 1)

            def shift(n, kv, a):
                v.wait_ge(sem["s1"], 4 * n + a + 1)
                v.tensor_reduce(mx[:, a % 2:a % 2 + 1], ps[:, 0:3, 0:TH], AX.XY, ALU.max).then_inc(sem["mx"], 1)
                v.wait_ge(sem["mx"], 4 * n + a + 1)
                v.tensor_scalar(qpart[kv][:, a, 0:1], mx[:, a % 2:a % 2 + 1], -1.0, None, ALU.mult).then_inc(sem["nm"], 1)

            def normed(n, kv):
                v.wait_ge(sem["pv"], 9 * n + 12)
                link(v.reciprocal(rs[:, kv], heads(OB)[:, :, HD]))
                v.tensor_tensor(yk[:, kv], heads(OB)[:, :, 0:HD], rs[:, kv].unsqueeze(2).broadcast_to([P, G, HD]),
                                ALU.mult).then_inc(sem["on"], 1)

            def tile(i, more, more2):
                for kv in range(KV):
                    if more:
                        if kv == 0:
                            v.wait_ge(sem["rope"], 6 * i + 12)
                            v.wait_ge(sem["ptm"], use(i, 0))
                        else:
                            v.wait_ge(sem["ptm"], use(i, 3))
                        split(kv, sem["part"])
                    if kv == 0 or more:
                        for a in range(G):
                            shift(2 * i + kv + 1, 1 - kv, a)
                            if kv and more2 and a == 1:
                                norm_a(i + 3)
                            if kv and more2 and a == 2:
                                norm_b(i + 3, qtab[:, bass.ds(i + 2, 1)].rearrange("p a c d -> p (a c) d"))
                    normed(2 * i + kv, kv)

            for a in range(G):
                shift(0, 0, a)
            with v.Fori(0, 6) as i:
                link.loop(i, 4)
                tile(i, True, True)
            link.end(6)
            tile(6, True, False)
            tile(7, False, False)


def merge(nc, g):
    io, ps = g.io, g.ps
    KB = 4
    with Phase(nc, "mrg") as ph:
        y = ph.sb("y", [P, KB, T])
        ys = [ph.sb(f"ys{n}", [P, KB, T], F32R) for n in ("hi", "lo")]
        raw = [ph.sb(f"raw{i}", [P, KB * 512]) for i in range(2)]
        w = [[ph.sb(f"w{n}{i}", [P, KB * 512], F32R) for i in range(2)] for n in ("hi", "lo")]
        bg = [ph.sb(f"bg{i}", [P, T]) for i in range(4)]
        part = [ph.sb(f"part{i}", [P, T]) for i in range(2)]
        y_in = ph.sem("y_in")
        w_in = [ph.sem(f"w_in{i}") for i in range(2)]
        bg_in = [ph.sem(f"bg_in{i}") for i in range(4)]
        y_hi, y_lo = ph.sem("y_hi"), ph.sem("y_lo")
        w_hi, w_lo = ph.sem("w_hi"), ph.sem("w_lo")
        mm_done = ph.sem("mm_done")
        taken = ph.sem("taken")
        bg_used = ph.sem("bg_used")
        dve = ph.sem("dve")
        NB = 3
        block = ph.block()

        @block.sync
        def _(sp):
            for n in range(NB):
                if n:
                    sp.wait_ge(y_lo, KB * n)
                sp.dma_start(y[:], g.y_dram[n * 512:n * 512 + 512, :].rearrange("(k p) t -> p k t", p=P)).then_inc(y_in, 16)
                for s in range(2):
                    if n:
                        sp.wait_ge(w_lo, 2 * n + s - 1)
                    sp.dma_start(raw[s][:], io["w_branch"][2 * n + s]).then_inc(w_in[s], 16)

        @block.gpsimd
        def _(gp):
            for n in range(8 * NB):
                if n >= 4:
                    gp.wait_ge(bg_used, n - 3)
                gp.dma_start(bg[n % 4][:], g.bg_dram[n * P:n * P + P, :]).then_inc(bg_in[n % 4], 16)

        @block.scalar
        def _(act):
            def weights(n, s):
                act.wait_ge(w_in[s], 16 * n + 16)
                if n:
                    act.wait_ge(mm_done, 8 * n + 4 * s - 4)
                act.activation(w[0][s][:], raw[s][:], ACT.Copy).then_inc(w_hi, 1)

            def ys_hi(n):
                act.wait_ge(y_in, 16 * n + 16)
                if n:
                    act.wait_ge(mm_done, 8 * n)
                for k in range(KB):
                    act.activation(ys[0][:, k, :], y[:, k, :], ACT.Copy).then_inc(y_hi, 1)

            ys_hi(0)
            for n in range(NB):
                for s in range(2):
                    if n + s == 0:
                        weights(0, 0)
                        weights(0, 1)
                    elif (n, s) != (NB - 1, 1):
                        m = 2 * n + s + 1
                        weights(m // 2, m % 2) if m > 1 else None
                if n < NB - 1:
                    ys_hi(n + 1)

        @block.vector
        def _(v):
            link = Chain(v, dve)
            v.sem_inc(taken, 2)

            def weights(m):
                v.wait_ge(w_hi, m + 1)
                v.tensor_tensor(w[1][m % 2][:], raw[m % 2][:], w[0][m % 2][:].bitcast(F32), ALU.subtract).then_inc(w_lo, 1)

            def ys_lo(n):
                for k in range(KB):
                    v.wait_ge(y_hi, KB * n + k + 1)
                    v.tensor_tensor(ys[1][:, k, :], y[:, k, :], ys[0][:, k, :].bitcast(F32), ALU.subtract).then_inc(y_lo, 1)

            ys_lo(0)
            weights(0)
            weights(1)
            for n in range(NB):
                for t in range(8):
                    if t == 4 and n:
                        weights(2 * n + 1)
                    m = 8 * n + t
                    v.wait_ge(mm_done, m + 1)
                    v.wait_ge(bg_in[m % 4], 16 * (m // 4) + 16)
                    into = g.merged[:, t, :]
                    dst = part[t % 2][:] if n else into
                    v.tensor_tensor(dst.rearrange("p (a n) -> p a n", a=3), ps[:, 3 * (t % 2):3 * (t % 2) + 3, 0:TH],
                                    bg[m % 4][:].rearrange("p (a n) -> p a n", a=3), ALU.mult).then_inc(taken, 1)
                    v.wait_ge(taken, m + 3)
                    v.sem_inc(bg_used, 1)
                    if n:
                        link(v.tensor_tensor(into, into, part[t % 2][:], ALU.add))
                if n < NB - 1:
                    ys_lo(n + 1)
                    weights(2 * n + 2)

        @block.tensor
        def _(pe):
            with pe.Fori(0, NB) as n:
                for t in range(8):
                    s = t // 4
                    if t == 0:
                        pe.wait_ge(y_lo, KB * n + KB)
                    if t % 4 == 0:
                        pe.wait_ge(w_lo, 2 * n + s + 1)
                    pe.wait_ge(taken, 8 * n + t + 1)
                    ws = [x[s][:].rearrange("p (k n) -> p k n", k=KB) for x in w]
                    for c in range(3):
                        for k in range(KB):
                            mm = three_passes(pe, ps[:, 3 * (t % 2) + c, 0:TH], [x[:, k, t % 4 * P:t % 4 * P + P] for x in ws],
                                              [x[:, k, c * TH:(c + 1) * TH] for x in ys], k == 0, k == KB - 1)
                    mm.then_inc(mm_done, 1)


def out_norm(nc, g):
    io, ps = g.io, g.ps
    with Phase(nc, "out") as ph:
        raw = [ph.sb(f"raw{i}", [P, D]) for i in range(4)]
        w = [ph.sb(f"w{n}", [P, KD, D], F32R) for n in ("hi", "lo")]
        g1 = ph.sb("g1", [P, 2, D])
        free = g.merged[:].rearrange("p k t -> p (k t)")
        xin, x1, xs, hm = ([free[:, (2 * n + i) * D:(2 * n + i + 1) * D] for i in range(2)] for n in range(4))
        hm = [x.rearrange("p (k n) -> p k n", k=KD) for x in hm]
        junk = free[:, 8 * D:9 * D]
        m_hi, m_lo = ph.sem("m_hi"), ph.sem("m_lo")
        ss, ms, rstd = (ph.sb(n, [P, NT]) for n in ("ss", "ms", "rstd"))
        half = ph.sb("half", [P, 1])
        w_in = [ph.sem(f"w_in{i}") for i in range(4)]
        x_in = [ph.sem(f"x_in{i}") for i in range(2)]
        x_out = [ph.sem(f"x_out{i}") for i in range(2)]
        g_in = ph.sem("g_in")
        w_hi, w_lo = ph.sem("w_hi"), ph.sem("w_lo")
        mm_done, gated, x1_done, squared = ph.sem("mm_done"), ph.sem("gated"), ph.sem("x1_done"), ph.sem("squared")
        pool, rstd_done, xs_done = ph.sem("pool"), ph.sem("rstd_done"), ph.sem("xs_done")
        turned, scaled, h_full, h_hi, h_lo = (ph.sem(n) for n in ("turned", "scaled", "h_full", "h_hi", "h_lo"))
        block = ph.block()

        @block.sync
        def _(sp):
            for who in range(2):
                sp.dma_start(g1[:, who, :], g.gate_rows[who, 0:D].partition_broadcast(P)).then_inc(g_in, 16)
            for k in range(KD):
                if k >= 4:
                    sp.wait_ge(w_lo, k - 3)
                sp.dma_start(raw[k % 4][:], io["w_out"][k * P:k * P + P, :]).then_inc(w_in[k % 4], 16)
            sp.wait_ge(m_lo, KD)
            sp.dma_start(xin[0][:], io["x_prompt"]).then_inc(x_in[0], 16)
            for i in range(1, NT):
                if i >= 2:
                    sp.wait_ge(x1_done, i - 1)
                sp.dma_start(xin[i % 2][:], io["x_sample"][i * P - P:i * P, :]).then_inc(x_in[i % 2], 16)

        @block.gpsimd
        def _(gp):
            gp.memset(half[:], -0.5).then_inc(pool, 1)
            for i in range(NT):
                gp.wait_ge(squared, i + 1)
                gp.tensor_scalar(ms[:, i:i + 1], ss[:, i:i + 1], 1.0 / D, EPS, ALU.mult, ALU.add).then_inc(pool, 1)
                gp.wait_ge(pool, i + 2)
                gp.tensor_tensor(rstd[:, i:i + 1], ms[:, i:i + 1], half[:], ALU.pow).then_inc(rstd_done, 1)

        @block.scalar
        def _(act):
            def square(i):
                act.wait_ge(x1_done, i + 1)
                act.dma_start(g.x1_dram[i * P:i * P + P, :], x1[i % 2][:]).then_inc(x_out[i % 2], 16)
                if i:
                    act.wait_ge(squared, i)
                act.activation(junk[:], x1[i % 2][:], ACT.Square, accum_out=ss[:, i:i + 1]).then_inc(squared, 1)
                act.wait_ge(rstd_done, i + 1)
                if i >= 2:
                    act.wait_ge(turned, i - 1)
                act.activation(xs[i % 2][:], x1[i % 2][:], ACT.Copy, scale=rstd[:, i:i + 1]).then_inc(xs_done, 1)

            def split(i):
                act.wait_ge(h_full, i + 1)
                act.activation(g.h[0][:, :, i * P:i * P + P], hm[i % 2][:], ACT.Copy).then_inc(h_hi, 1)

            for k in range(KD):
                act.activation(g.h[0][:, k, :], g.merged[:, k, :], ACT.Copy).then_inc(m_hi, 1)
                act.wait_ge(w_in[k % 4], 16 * (k // 4) + 16)
                act.activation(w[0][:, k, :], raw[k % 4][:], ACT.Copy).then_inc(w_hi, 1)
            for i in range(NT):
                square(i)
                if i:
                    split(i - 1)
            split(NT - 1)
            act.wait_ge(x_out[0], 16 * 5)
            act.wait_ge(x_out[1], 16 * 4)

        @block.vector
        def _(v):
            for k in range(KD):
                v.wait_ge(m_hi, k + 1)
                v.tensor_tensor(g.h[1][:, k, :], g.merged[:, k, :], g.h[0][:, k, :].bitcast(F32), ALU.subtract).then_inc(m_lo, 1)
                v.wait_ge(w_hi, k + 1)
                v.tensor_tensor(w[1][:, k, :], raw[k % 4][:], w[0][:, k, :].bitcast(F32), ALU.subtract).then_inc(w_lo, 1)
            v.wait_ge(g_in, 32)
            v.wait_ge(m_lo, KD)

            def residual(i):
                who = min(i, 1)
                v.wait_ge(mm_done, i + 1)
                if i >= 2:
                    v.wait_ge(x_out[i % 2], 16 * (i // 2))
                    v.wait_ge(xs_done, i - 1)
                v.tensor_tensor(x1[i % 2][:].rearrange("p (a n) -> p a n", a=2), ps[:, 2 * (i % 2):2 * (i % 2) + 2, :],
                                g1[:, who, :].rearrange("p (a n) -> p a n", a=2), ALU.mult).then_inc(gated, 1)
                v.wait_ge(gated, i + 1)
                v.wait_ge(x_in[i % 2], 16 * (i // 2) + 16)
                v.tensor_tensor(x1[i % 2][:], x1[i % 2][:], xin[i % 2][:], ALU.add).then_inc(x1_done, 1)

            def modulated(i):
                who = min(i, 1)
                col = lambda c: g.mod[:, c, :, who:who + 1].broadcast_to([P, KD, P])
                if i >= 2:
                    v.wait_ge(h_lo, i - 1)
                v.wait_ge(turned, i + 1)
                v.tensor_tensor(hm[i % 2][:], ps[:, 4 + 2 * (i % 2):6 + 2 * (i % 2), :].rearrange("p a (k n) -> p (a k) n", n=P),
                                col(2), ALU.mult).then_inc(scaled, 1)
                v.wait_ge(scaled, i + 1)
                v.tensor_tensor(hm[i % 2][:], hm[i % 2][:], col(3), ALU.add).then_inc(h_full, 1)

            def split(i):
                v.wait_ge(h_hi, i + 1)
                v.tensor_tensor(g.h[1][:, :, i * P:i * P + P], hm[i % 2][:], g.h[0][:, :, i * P:i * P + P].bitcast(F32),
                                ALU.subtract).then_inc(h_lo, 1)

            for i in range(NT):
                residual(i)
                if i >= 1:
                    modulated(i - 1)
                if i >= 2:
                    split(i - 2)
            split(NT - 2)
            modulated(NT - 1)
            split(NT - 1)

        @block.tensor
        def _(pe):
            def turn(i):
                pe.wait_ge(xs_done, i + 1)
                if i >= 2:
                    pe.wait_ge(scaled, i - 1)
                for k in range(KD):
                    mm = pe.transpose(ps[:, 4 + 2 * (i % 2) + k // 4, k % 4 * P:k % 4 * P + P], xs[i % 2][:, k * P:k * P + P],
                                      g.ident[:])
                mm.then_inc(turned, 1)

            for i in range(NT):
                if i >= 2:
                    pe.wait_ge(gated, i - 1)
                for k in range(KD):
                    if i == 0:
                        pe.wait_ge(m_lo, k + 1)
                        pe.wait_ge(w_lo, k + 1)
                    for n in range(2):
                        mm = three_passes(pe, ps[:, 2 * (i % 2) + n, :], [x[:, k, i * P:i * P + P] for x in g.h],
                                          [x[:, k, 512 * n:512 * n + 512] for x in w], k == 0, k == KD - 1)
                mm.then_inc(mm_done, 1)
                if i:
                    turn(i - 1)
            turn(NT - 1)


def ffn(nc, g):
    io, ps = g.io, g.ps
    with Phase(nc, "ffn") as ph:
        raw = [ph.sb(f"raw{i}", [P, UNIT]) for i in range(2)]
        w = [[ph.sb(f"w{n}{i}", [P, KD, HALF], F32R) for i in range(2)] for n in ("hi", "lo")]
        oraw = [ph.sb(f"oraw{i}", [P, D]) for i in range(2)]
        ow = [[ph.sb(f"ow{n}{i}", [P, D], F32R) for i in range(2)] for n in ("hi", "lo")]
        gate = ph.sb("gate", [P, T])
        a = [[ph.sb(f"a{n}{i}", [P, T], F32R) for i in range(2)] for n in ("hi", "lo")]
        w_in = [ph.sem(f"w_in{i}") for i in range(2)]
        o_in = [ph.sem(f"o_in{i}") for i in range(2)]
        w_hi, w_lo, o_hi, o_lo = (ph.sem(n) for n in ("w_hi", "w_lo", "o_hi", "o_lo"))
        gu_mm = ph.sem("gu_mm")
        silu = ph.sem("silu")
        prod = ph.sem("prod")
        a_hi, a_lo = ph.sem("a_hi"), ph.sem("a_lo")
        out_mm = ph.sem("out_mm")
        added = ph.sem("added")
        cleared = ph.sem("cleared")
        GATE, UP, OUT = 0, 3, 6
        block = ph.block()

        @block.sync
        def _(sp):
            def load(j, s, wait=True):
                if wait:
                    sp.wait_ge(w_lo, j - 1)
                sp.dma_start(raw[s][:], io["w_ffn_in"][bass.ds(j, 1)].rearrange("a p n -> (a p) n")).then_inc(w_in[s], 16)
                if wait:
                    sp.wait_ge(o_lo, j - 1)
                sp.dma_start(oraw[s][:], io["w_ffn_out"][bass.ds(j * P, P), :]).then_inc(o_in[s], 16)

            load(0, 0, False)
            load(1, 1, False)
            with sp.Fori(0, NH // 2 - 1) as i:
                for s in range(2):
                    load(2 * i + s + 2, s)

        @block.gpsimd
        def _(gp):
            gp.memset(g.acc, 0.0).then_inc(cleared, 1)

        def times(j, s):
            return 8 * j + 16 - 8 * s

        @block.scalar
        def _(act):
            act.sem_inc(silu, 3)

            def w_split(j, s, wait=True):
                act.wait_ge(w_in[s], times(j, s))
                if wait:
                    act.wait_ge(gu_mm, 6 * j - 6)
                act.activation(w[0][s][:].rearrange("p k n -> p (k n)"), raw[s][:], ACT.Copy).then_inc(w_hi, 1)

            def step(j, s, first=False, last=False):
                if not last:
                    w_split(j + 1, 1 - s, not first)
                for t in range(3):
                    act.wait_ge(gu_mm, 6 * j + t + 1)
                    if not first:
                        act.wait_ge(a_lo, 3 * j + t - 2)
                    act.activation(gate[:, t * TH:t * TH + TH], ps[:, GATE + t, 0:TH], ACT.Silu).then_inc(silu, 1)
                    if t == 0:
                        act.wait_ge(o_in[s], times(j, s))
                        if not first:
                            act.wait_ge(added, 18 * j - 16)
                        act.activation(ow[0][s][:], oraw[s][:], ACT.Copy).then_inc(o_hi, 1)
                for t in range(3):
                    act.wait_ge(prod, 3 * j + t + 4)
                    act.activation(a[0][s][:, t * TH:t * TH + TH], gate[:, t * TH:t * TH + TH], ACT.Copy).then_inc(a_hi, 1)

            w_split(0, 0, False)
            step(0, 0, first=True)
            with act.Fori(0, NH // 2 - 1) as i:
                for s in range(2):
                    step(2 * i + 1 + s, 1 - s)
            step(NH - 1, 1, last=True)

        @block.vector
        def _(v):
            v.sem_inc(prod, 3)
            v.sem_inc(added, 2)

            def w_split(j, s):
                v.wait_ge(w_hi, j + 1)
                v.tensor_tensor(w[1][s][:].rearrange("p k n -> p (k n)"), raw[s][:],
                                w[0][s][:].rearrange("p k n -> p (k n)").bitcast(F32), ALU.subtract).then_inc(w_lo, 1)

            def add(j, us):
                for u in us:
                    dst = g.acc[:, u // 2, u % 2 * 512:u % 2 * 512 + 512]
                    v.wait_ge(out_mm, 18 * j + u + 1)
                    v.tensor_tensor(dst, dst, ps[:, OUT + u % 2, :], ALU.add).then_inc(added, 1)

            def times_up(j, t):
                r = slice(t * TH, t * TH + TH)
                v.wait_ge(gu_mm, 6 * j + t + 4)
                v.wait_ge(silu, 3 * j + t + 4)
                v.tensor_tensor(gate[:, r], gate[:, r], ps[:, UP + t, 0:TH], ALU.mult).then_inc(prod, 1)

            def a_split(j, s, t):
                r = slice(t * TH, t * TH + TH)
                v.wait_ge(a_hi, 3 * j + t + 1)
                v.tensor_tensor(a[1][s][:, r], gate[:, r], a[0][s][:, r].bitcast(F32), ALU.subtract).then_inc(a_lo, 1)

            def step(j, s, first=False, last=False):
                if not first:
                    add(j - 1, range(0, 3))
                if not last:
                    w_split(j + 1, 1 - s)
                if not first:
                    add(j - 1, range(3, 6))
                v.wait_ge(o_hi, j + 1)
                v.tensor_tensor(ow[1][s][:], oraw[s][:], ow[0][s][:].bitcast(F32), ALU.subtract).then_inc(o_lo, 1)
                if not first:
                    add(j - 1, range(6, 9))
                for t in range(3):
                    u = 9 + 3 * t
                    if not first:
                        add(j - 1, range(u, u + 2))
                    times_up(j, t)
                    if not first:
                        add(j - 1, range(u + 2, u + 3))
                    a_split(j, s, t)

            w_split(0, 0)
            v.wait_ge(cleared, 1)
            step(0, 0, first=True)
            with v.Fori(0, NH // 2 - 1) as i:
                for s in range(2):
                    step(2 * i + 1 + s, 1 - s)
            step(NH - 1, 1, last=True)
            add(NH - 1, range(18))

        @block.tensor
        def _(pe):
            def out(j, s, us):
                for u in us:
                    tile = u // 2
                    if u == 0:
                        pe.wait_ge(o_lo, j + 1)
                    if u % 6 == 0:
                        pe.wait_ge(a_lo, 3 * j + u // 6 + 1)
                    pe.wait_ge(added, 18 * j + u + 1)
                    three_passes(pe, ps[:, OUT + u % 2, :], [x[s][:, tile * P:tile * P + P] for x in a],
                                 [x[s][:, u % 2 * 512:u % 2 * 512 + 512] for x in ow], True, True).then_inc(out_mm, 1)

            def step(j, s, first=False):
                pe.wait_ge(w_lo, j + 1)
                for n in range(6):
                    t = n % 3
                    pe.wait_ge(silu if n < 3 else prod, 3 * j + t + 1)
                    for k in range(KD):
                        mm = three_passes(pe, ps[:, (GATE if n < 3 else UP) + t, 0:TH],
                                          [x[s][:, k, n // 3 * P:n // 3 * P + P] for x in w],
                                          [x[:, k, t * TH:t * TH + TH] for x in g.h], k == 0, k == KD - 1)
                        if k == KD - 1:
                            mm.then_inc(gu_mm, 1)
                        if k in (2, 5, 7) and not first:
                            u = 3 * n + (2, 5, 7).index(k)
                            out(j - 1, 1 - s, range(u, u + 1))

            step(0, 0, first=True)
            with pe.Fori(0, NH // 2 - 1) as i:
                for s in range(2):
                    step(2 * i + 1 + s, 1 - s)
            step(NH - 1, 1)
            out(NH - 1, 1, range(18))


def finish(nc, g):
    io = g.io
    with Phase(nc, "fin") as ph:
        g2 = ph.sb("g2", [P, 2, D])
        fg = ph.sb("fg", [P, D])
        x1 = ph.sb("x1", [P, NT, D])
        out = [ph.sb(f"out{i}", [P, D]) for i in range(3)]
        junk = ph.sb("junk", [P, D])
        ss, ms, rstd = (ph.sb(n, [P, NT]) for n in ("ss", "ms", "rstd"))
        half = ph.sb("half", [P, 1])
        g_in, x_in, y_out = ph.sem("g_in"), [ph.sem(f"x_in{i}") for i in range(3)], ph.sem("y_out")
        gated, summed, squared, pool, rstd_done, y_done = (ph.sem(n) for n in ("gated", "summed", "squared", "pool",
                                                                             "rstd_done", "y_done"))
        y_outs = [ph.sem(f"y_out{i}") for i in range(3)]
        block = ph.block()

        @block.sync
        def _(sp):
            for who in range(2):
                sp.dma_start(g2[:, who, :], g.gate_rows[who, D:2 * D].partition_broadcast(P)).then_inc(g_in, 16)
            for n in range(3):
                sp.dma_start(x1[:, 3 * n:3 * n + 3, :],
                             g.x1_dram[3 * n * P:3 * (n + 1) * P, :].rearrange("(t p) d -> p t d", p=P)).then_inc(x_in[n], 16)
            sp.dma_start(fg[:], io["final_g"].partition_broadcast(P)).then_inc(g_in, 16)
            for i in range(NT):
                sp.wait_ge(y_done, i + 1)
                dst = g.outs["y_sample"][i * P - P:i * P, :] if i else g.outs["y_prompt"]
                sp.dma_start(dst, out[i % 3][:]).then_inc(y_outs[i % 3], 16)
            for s in y_outs:
                sp.wait_ge(s, 48)

        @block.gpsimd
        def _(gp):
            gp.memset(half[:], -0.5).then_inc(pool, 1)
            for i in range(NT):
                gp.wait_ge(squared, i + 1)
                gp.tensor_scalar(ms[:, i:i + 1], ss[:, i:i + 1], 1.0 / D, EPS, ALU.mult, ALU.add).then_inc(pool, 1)
                gp.wait_ge(pool, i + 2)
                gp.tensor_tensor(rstd[:, i:i + 1], ms[:, i:i + 1], half[:], ALU.pow).then_inc(rstd_done, 1)

        @block.scalar
        def _(act):
            for i in range(NT):
                act.wait_ge(summed, i + 1)
                if i:
                    act.wait_ge(squared, i)
                act.activation(junk[:], x1[:, i, :], ACT.Square, accum_out=ss[:, i:i + 1]).then_inc(squared, 1)

        @block.vector
        def _(v):
            def total(i):
                v.tensor_tensor(g.acc[:, i, :], g.acc[:, i, :], g2[:, min(i, 1), :], ALU.mult).then_inc(gated, 1)
                v.wait_ge(x_in[i // 3], 16)
                v.wait_ge(gated, i + 1)
                v.tensor_tensor(x1[:, i, :], x1[:, i, :], g.acc[:, i, :], ALU.add).then_inc(summed, 1)

            v.wait_ge(g_in, 48)
            total(0)
            total(1)
            for i in range(NT):
                if i + 2 < NT:
                    total(i + 2)
                v.wait_ge(rstd_done, i + 1)
                if i >= 3:
                    v.wait_ge(y_outs[i % 3], 16 * (i // 3))
                v.scalar_tensor_tensor(out=out[i % 3][:], in0=x1[:, i, :], scalar=rstd[:, i:i + 1], in1=fg[:],
                                       op0=ALU.mult, op1=ALU.mult).then_inc(y_done, 1)


OUTS = [("y_prompt", [CTX, D]), ("y_sample", [LAT, D]), ("k", [CTX, KV * HD]), ("v", [CTX, KV * HD]),
        ("ml_s", [2, HEADS * P, DK + 1]), ("ml_m", [HEADS, 2]), ("hg_s", [2, HEADS * P, DK])]


def build(nc, io, outs):
    with ExitStack() as stack:
        g = Core()
        g.io, g.outs = io, outs
        dram = lambda name, shape: nc.dram_tensor(name, shape, F32).ap()
        g.gate_rows = dram("gate_rows", [2, 2 * D])
        g.tok_dram = dram("tok_dram", [T, TW])
        g.feat_dram = dram("feat_dram", [NFQ * HALF, T])
        g.bg_dram = dram("bg_dram", [NBG * HALF, T])
        g.gate_dram = dram("gate_dram", [HEADS, 10, T])
        g.decay_dram = dram("decay_dram", [HEADS, 2 * NT])
        g.y_dram = dram("y_dram", [3 * 4 * P, T])
        g.x1_dram = dram("x1_dram", [T, D])
        sb = lambda n, s, d=F32: stack.enter_context(nc.sbuf_tensor(n, s, d))
        g.ps = stack.enter_context(nc.psum_tensor("ps", [P, 8, 512], F32))
        g.ident = sb("ident", [P, P])
        g.mod = sb("mod", [P, 4, KD, 2])
        g.vcol = sb("vcol", [P, 80])
        g.sc = sb("sc", [P, KD, 2])
        g.mcol = sb("mcol", [P, 16, 2])

        def operand(hs, name):
            return [hs.enter_context(nc.sbuf_tensor(f"{name}_{n}", [P, KD, T], F32R)) for n in ("hi", "lo")]

        with ExitStack() as hs:
            g.h = operand(hs, "h")
            modulate(nc, g)
            project(nc, g)
        gate_rows(nc, g)
        mlstm(nc, g)
        hgrn(nc, g)
        attention(nc, g)
        g.merged = sb("merged", [P, KD, T])
        merge(nc, g)
        g.h = operand(stack, "h2")
        out_norm(nc, g)
        g.acc = g.merged[:].rearrange("p k t -> p (k t)").rearrange("p (t d) -> p t d", d=D)
        ffn(nc, g)
        finish(nc, g)


def units(a, width):
    k, n = a.shape
    return np.ascontiguousarray(a.reshape(k // P, P, n // width, width).transpose(2, 1, 0, 3)
                                .reshape(n // width, P, k // P * width))


def lay_out(i):
    w_in = np.asarray(i["w_in"])[0]
    o = {}
    at = {}
    pos = 0
    for name, n in (("mq", 512), ("mk", 512), ("mv", 512), ("mo", 512), ("mg", 16), ("hq", 512), ("hf", 1024),
                    ("hi", 512), ("hg", 512), ("aq", 512), ("ak", 128), ("av", 128), ("bg", 3072)):
        at[name] = w_in[:, pos:pos + n]
        pos += n
    aq = at["aq"].reshape(D, KV, AH // KV, HD).transpose(0, 2, 1, 3).reshape(D, AH * HD)
    tok = np.concatenate([at["mv"], at["mo"], at["hi"], at["hg"], aq], axis=1)
    wt = tok.reshape(2, 4, P, NTB, 512).transpose(3, 0, 2, 1, 4).reshape(2 * NTB, P, UNIT)
    last = np.concatenate([at["ak"], at["av"], at["mg"]], axis=1)
    feat = np.concatenate([at["mq"], at["mk"], at["hq"], at["hf"], at["bg"]], axis=1)
    o["w_tok"] = np.ascontiguousarray(wt)
    o["w_tok_last"] = units(last, TLAST)[0]
    o["w_feat"] = units(feat, HALF)
    wa = np.asarray(i["w_ada"])[0].reshape(D, 6, D)
    wa = np.concatenate([wa[:, 0:2], wa[:, 3:5], wa[:, 2:3], wa[:, 5:6]], axis=1).reshape(D, 6 * D)
    o["w_ada"] = units(wa, 512).reshape(12, P, KD, 512)
    o["b_ada"] = np.asarray(i["b_ada"])[0]
    o["norm1_g"] = np.asarray(i["norm1_g"])[0]
    o["norm2_g"] = np.asarray(i["norm2_g"])[0]
    o["c"] = np.asarray(i["c"])[0]
    o["c_ctx"] = np.asarray(i["c_ctx"])
    o["x_prompt"] = np.asarray(i["x_prompt"])[0]
    o["x_sample"] = np.asarray(i["x_sample"])[0]
    o["ml_gate_b"] = np.asarray(i["ml_gate_b"])[0].transpose(2, 0, 1).reshape(HEADS, 4)
    o["ml_m0"] = np.asarray(i["state_ml_m"])[0, 0].T
    o["ml_s0"] = np.concatenate([np.asarray(i["state_ml_C"])[0, 0], np.asarray(i["state_ml_n"])[0, 0][..., None]],
                                axis=-1).reshape(2, HEADS * P, DK + 1)
    o["cache_k"] = np.asarray(i["cache_k"])[0, 0].reshape(PAST, KV * HD)
    o["cache_v"] = np.asarray(i["cache_v"])[0, 0].reshape(PAST, KV * HD)
    o["qk_g"] = np.concatenate([np.asarray(i["q_norm_g"])[0], np.asarray(i["k_norm_g"])[0]])
    pos = np.arange(LAT)
    inv = (np.float32(ROPE_THETA) ** (-np.arange(HD // 4, dtype=np.float32) / np.float32(HD // 4))).astype(np.float32)
    ang = np.concatenate([(pos // GRID_W).astype(np.float32)[:, None] * inv,
                          (pos % GRID_W).astype(np.float32)[:, None] * inv], axis=-1)
    o["rope"] = np.stack([np.cos(ang), np.sin(ang)], axis=1).astype(np.float32).reshape(LAT // P, P, 2, HD // 2) \
        .transpose(1, 0, 2, 3)
    o["hg_s0"] = np.asarray(i["state_hg_S"])[0, 0].reshape(2, HEADS * P, DK)
    o["hg_g"] = np.asarray(i["hg_norm_g"])[0][:, None]
    key, query = np.arange(P)[:, None] % 32, np.arange(32)[None, :]
    masks = [key == query] * 2
    for l in range(1, 6):
        same = (key >> l) == (query >> l)
        kh, qh = (key >> (l - 1)) & 1, (query >> (l - 1)) & 1
        masks += [same & (kh == 0) & (qh == 1), same & (kh == 1) & (qh == 0)]
    o["hg_mask"] = np.stack(masks, axis=1).astype(np.int32)
    wb = np.asarray(i["w_branch"])[0]
    wb = np.stack([wb[0], wb[1], wb[2].reshape(KV, AH // KV, HD, D).transpose(1, 0, 2, 3).reshape(AH * HD, D)])
    o["w_branch"] = np.concatenate([units(x, 512) for x in wb])
    o["w_out"] = np.asarray(i["w_out"])[0]
    wf = np.asarray(i["w_ffn_in"])[0].reshape(D, 2, NH, P).transpose(0, 2, 1, 3).reshape(D, 2 * FFN)
    o["w_ffn_in"] = units(wf, HALF)
    o["w_ffn_out"] = np.asarray(i["w_ffn_out"])[0]
    o["final_g"] = np.asarray(i["final_g"])
    o["ml_g"] = np.asarray(i["ml_norm_g"])[0][:, None]
    return {k: np.ascontiguousarray(v) for k, v in o.items()}


def kernel(**inputs):
    import concourse.bacc as bacc
    from concourse.bass_utils import run_bass_kernel_spmd

    nc = bacc.Bacc("TRN2", target_bir_lowering=False, num_devices=1)
    arrays = {f"in_{name}": a for name, a in lay_out(inputs).items()}
    io = {name[3:]: nc.dram_tensor(name, a.shape, mybir.dt.from_np(a.dtype), kind="ExternalInput").ap()
          for name, a in arrays.items()}
    outs = {name: nc.dram_tensor(f"out_{name}", shape, F32, kind="ExternalOutput").ap() for name, shape in OUTS}
    build(nc, io, outs)
    r = run_bass_kernel_spmd(nc, [arrays], core_ids=[0]).results[0]
    y_prompt, y_sample, k, v, ml_s, ml_m, hg_s = (np.asarray(r[f"out_{name}"]) for name, _ in OUTS)
    kv = (1, 1, CTX, KV, HD)
    ml_s = ml_s.reshape(1, 1, 2, HEADS, DK, DK + 1)
    return (y_prompt[None], y_sample[None], k.reshape(kv), v.reshape(kv), np.ascontiguousarray(ml_s[..., :DK]),
            np.ascontiguousarray(ml_s[..., DK]), np.ascontiguousarray(ml_m.T)[None, None],
            hg_s.reshape(1, 1, 2, HEADS, DK, DK))
```
